# Optimizing a Trainium2 kernel written in Bass

```python
import jax, jax.numpy as jnp
from jax import lax
import numpy as np

D_MODEL = 1024
BATCH = 1
SEQ = 256
DEPTH = 2

CHUNK = 64
HEAD_DIM = 64
SB_HEADS = 4
SB_WIDTH = SB_HEADS * HEAD_DIM
SB_BLOCK = 128
POOL_WINDOWS = (2, 4, 8, 16)
N_POOL_GROUPS = len(POOL_WINDOWS)
POOL_GROUP = 64
POOL_WIDTH = N_POOL_GROUPS * POOL_GROUP
SW_Q_HEADS = 8
SW_KV_HEADS = 2
SW_GROUP = SW_Q_HEADS // SW_KV_HEADS
SW_WINDOW = 128
SW_WINDOW_CHUNKS = SW_WINDOW // CHUNK
SW_Q_WIDTH = SW_Q_HEADS * HEAD_DIM
SW_KV_WIDTH = SW_KV_HEADS * HEAD_DIM
ROPE_THETA = 10000.0
IN_SPLITS = (SB_WIDTH, SB_WIDTH, SB_WIDTH, POOL_WIDTH, SW_Q_WIDTH, SW_KV_WIDTH, SW_KV_WIDTH)
IN_COLS = sum(IN_SPLITS)
SPLIT_POINTS = tuple(int(v) for v in np.cumsum(IN_SPLITS)[:-1])
N_BRANCH = 3
D_FF = 2816
N_EXPERTS = 8
TOP_K = 2
D_FF_EXPERT = 3584
MOE_BLOCK = 256
N_DENSE = (DEPTH + 1) // 2
N_MOE = DEPTH // 2
LN_EPS = 1e-5
DEEPNORM_ALPHA = (2 * DEPTH) ** 0.25
DEEPNORM_BETA = (8 * DEPTH) ** -0.25

kernel_name = 'hybrid_streaming_sb_pool_swa_moe_trunk'

def normalize(x):
    xf = x.astype(jnp.float32)
    mu = jnp.mean(xf, axis=-1, keepdims=True)
    var = jnp.mean(jnp.square(xf - mu), axis=-1, keepdims=True)
    return ((xf - mu) * lax.rsqrt(var + LN_EPS)).astype(x.dtype)

def layer_norm(x, g, b):
    return normalize(x) * g + b

def ada_modulation(c, w, b):
    m = jax.nn.silu(c) @ w + b
    shift, scale, gate = jnp.split(m, 3, axis=-1)
    return shift[:, None], scale[:, None], gate[:, None]

def rotary(t, pos):
    half = HEAD_DIM // 2
    inv_freq = jnp.power(ROPE_THETA, -jnp.arange(half, dtype=jnp.float32) / half)
    ang = pos.astype(jnp.float32)[:, None] * inv_freq[None, :]
    cos = jnp.cos(ang)[None, :, None, :]
    sin = jnp.sin(ang)[None, :, None, :]
    tf = t.astype(jnp.float32)
    t1, t2 = tf[..., :half], tf[..., half:]
    return jnp.concatenate([t1 * cos - t2 * sin, t2 * cos + t1 * sin], axis=-1).astype(t.dtype)

def stick_breaking_attention(q, k, v):
    b, s, h, d = q.shape
    n_blk = s // SB_BLOCK
    kf = k.astype(jnp.float32)
    vf = v.astype(jnp.float32)
    q_blocks = q.astype(jnp.float32).reshape(b, n_blk, SB_BLOCK, h, d).transpose(1, 0, 2, 3, 4)
    key_pos = jnp.arange(s)

    def one_block(args):
        q_blk, blk = args
        query_pos = blk * SB_BLOCK + jnp.arange(SB_BLOCK)
        past = key_pos[None, :] < query_pos[:, None]
        z = jnp.einsum('bqhd,bkhd->bhqk', q_blk, kf) * (HEAD_DIM ** -0.5)
        log_keep = jnp.where(past, jax.nn.log_sigmoid(-z), 0.0)
        log_rest = lax.cumsum(log_keep, axis=3, reverse=True) - log_keep
        log_w = jnp.where(past, z + log_keep + log_rest, -jnp.inf)
        return jnp.einsum('bhqk,bkhd->bqhd', jnp.exp(log_w), vf)

    out = lax.map(one_block, (q_blocks, jnp.arange(n_blk)))
    return out.transpose(1, 0, 2, 3, 4).reshape(b, s, h * d).astype(q.dtype)

def multiscale_pool(u, w_pool, pool_scale):
    b, s, _ = u.shape
    uf = u.astype(jnp.float32)
    count_pos = jnp.arange(s, dtype=jnp.float32)[None, :, None] + 1.0
    groups = []
    for g, win in enumerate(POOL_WINDOWS):
        ug = uf[..., g * POOL_GROUP:(g + 1) * POOL_GROUP]
        csum = jnp.cumsum(ug, axis=1)
        lagged = jnp.pad(csum, ((0, 0), (win, 0), (0, 0)))[:, :s]
        groups.append((csum - lagged) / jnp.minimum(count_pos, win) - ug)
    pooled = jnp.stack(groups, axis=2)
    mixed = jnp.einsum('bsgc,gce->bsge', pooled, w_pool)
    return (mixed.reshape(b, s, POOL_WIDTH) * pool_scale).astype(u.dtype)

def sliding_window_sink_attention(q, k, v, sinks):
    b, s = q.shape[:2]
    n_chunk = s // CHUNK
    back = SW_WINDOW_CHUNKS - 1
    qc = q.astype(jnp.float32).reshape(b, n_chunk, CHUNK, SW_KV_HEADS, SW_GROUP, HEAD_DIM)

    def band(t):
        tc = t.astype(jnp.float32).reshape(b, n_chunk, CHUNK, SW_KV_HEADS, HEAD_DIM)
        tp = jnp.pad(tc, ((0, 0), (back, 0), (0, 0), (0, 0), (0, 0)))
        return jnp.concatenate([tp[:, j:j + n_chunk] for j in range(back + 1)], axis=2)

    kb, vb = band(k), band(v)
    slot_chunk = jnp.arange(n_chunk)[:, None] - back + jnp.repeat(jnp.arange(back + 1), CHUNK)[None, :]
    valid = slot_chunk >= 0
    scores = jnp.einsum('bnqhgd,bnkhd->bnhgqk', qc, kb) * (HEAD_DIM ** -0.5)
    scores = jnp.where(valid[None, :, None, None, None, :], scores, -jnp.inf)
    sink = jnp.broadcast_to(sinks.astype(jnp.float32).reshape(SW_KV_HEADS, SW_GROUP)[None, None, :, :, None, None],
                            scores.shape[:-1] + (1,))
    probs = jax.nn.softmax(jnp.concatenate([scores, sink], axis=-1), axis=-1)[..., :-1]
    out = jnp.einsum('bnhgqk,bnkhd->bnqhgd', probs, vb)
    return out.reshape(b, s, SW_Q_WIDTH).astype(q.dtype)

def token_mixer(h, pos, w_in, w_pool, pool_scale, sinks, w_gate, w_branch_a, w_branch_b, w_branch_c, w_out):
    b, s, _ = h.shape
    qa, ka, va, u, qc, kc, vc = jnp.split(h @ w_in, SPLIT_POINTS, axis=-1)

    def heads(t, n):
        return t.reshape(b, s, n, HEAD_DIM)

    y_a = stick_breaking_attention(heads(qa, SB_HEADS), heads(ka, SB_HEADS), heads(va, SB_HEADS))
    y_b = multiscale_pool(u, w_pool, pool_scale)
    y_c = sliding_window_sink_attention(rotary(heads(qc, SW_Q_HEADS), pos), rotary(heads(kc, SW_KV_HEADS), pos),
                                        heads(vc, SW_KV_HEADS), sinks)
    g_a, g_b, g_c = jnp.split(jax.nn.sigmoid(h @ w_gate), N_BRANCH, axis=-1)
    merged = g_a * (y_a @ w_branch_a) + g_b * (y_b @ w_branch_b) + g_c * (y_c @ w_branch_c)
    return merged @ w_out

def swiglu(h, w1, w3, w2):
    return (jax.nn.silu(h @ w1) * (h @ w3)) @ w2

def moe_swiglu(h, w_router, b_router, w1, w3, w2):
    b, s, d = h.shape
    n_tok = b * s
    xf = h.reshape(n_tok, d)
    logits = (xf @ w_router).astype(jnp.float32) + b_router.astype(jnp.float32)
    top_logit, top_idx = lax.top_k(logits, TOP_K)
    top_w = jax.nn.softmax(top_logit, axis=-1)
    e_flat = top_idx.reshape(-1)
    w_flat = top_w.reshape(-1)
    tok_flat = jnp.repeat(jnp.arange(n_tok, dtype=jnp.int32), TOP_K)
    order = jnp.argsort(e_flat)
    e_sorted, tok_sorted, w_sorted = e_flat[order], tok_flat[order], w_flat[order]
    counts = jnp.bincount(e_flat, length=N_EXPERTS)
    padded = (counts + MOE_BLOCK - 1) // MOE_BLOCK * MOE_BLOCK
    start = jnp.cumsum(counts) - counts
    padded_end = jnp.cumsum(padded)
    padded_start = padded_end - padded
    dest = padded_start[e_sorted] + jnp.arange(n_tok * TOP_K) - start[e_sorted]
    n_rows = n_tok * TOP_K + N_EXPERTS * MOE_BLOCK
    n_blk = n_rows // MOE_BLOCK
    row_tok = jnp.zeros((n_rows,), jnp.int32).at[dest].set(tok_sorted)
    row_w = jnp.zeros((n_rows,), jnp.float32).at[dest].set(w_sorted)
    blk_exp = jnp.clip(jnp.searchsorted(padded_end, jnp.arange(n_blk) * MOE_BLOCK, side='right'), 0, N_EXPERTS - 1)

    def expert_block(args):
        toks, e = args
        xb = xf[toks]
        return (jax.nn.silu(xb @ w1[e]) * (xb @ w3[e])) @ w2[e]

    out = lax.map(expert_block, (row_tok.reshape(n_blk, MOE_BLOCK), blk_exp))
    y = jnp.zeros((n_tok, d), jnp.float32).at[row_tok].add(out.reshape(n_rows, d).astype(jnp.float32) * row_w[:, None])
    return y.reshape(b, s, d).astype(h.dtype)

def setup_inputs(seed: int = 0) -> dict:
    key = jax.random.key(seed)
    keys = iter(jax.random.split(key, 32))

    def normal(shape, std):
        return jax.random.normal(next(keys), shape, jnp.float32) * std

    L, D = DEPTH, D_MODEL
    beta = DEEPNORM_BETA
    in_gains = (1.0, 1.0, beta, beta, 1.0, 1.0, beta)
    col_gain = jnp.concatenate([jnp.full((w,), g, jnp.float32) for w, g in zip(IN_SPLITS, in_gains)])
    return {
        'x': normal((BATCH, SEQ, D), 1.0),
        'c': normal((BATCH, D), 1.0),
        'w_mod_mix': normal((L, D, 3 * D), 0.2 * D ** -0.5),
        'b_mod_mix': normal((L, 3 * D), 0.02),
        'w_in': normal((L, D, IN_COLS), D ** -0.5) * col_gain,
        'w_pool': normal((L, N_POOL_GROUPS, POOL_GROUP, POOL_GROUP), POOL_GROUP ** -0.5),
        'pool_scale': 1.0 + normal((L, POOL_WIDTH), 0.1),
        'sinks': normal((L, SW_Q_HEADS), 0.5),
        'w_gate': normal((L, D, N_BRANCH * D), D ** -0.5),
        'w_branch_a': normal((L, SB_WIDTH, D), beta * SB_WIDTH ** -0.5),
        'w_branch_b': normal((L, POOL_WIDTH, D), beta * POOL_WIDTH ** -0.5),
        'w_branch_c': normal((L, SW_Q_WIDTH, D), beta * SW_Q_WIDTH ** -0.5),
        'w_out': normal((L, D, D), beta * D ** -0.5),
        'ln_mix_g': 1.0 + normal((L, D), 0.02),
        'ln_mix_b': normal((L, D), 0.02),
        'w_mod_ffn': normal((L, D, 3 * D), 0.2 * D ** -0.5),
        'b_mod_ffn': normal((L, 3 * D), 0.02),
        'ffn_w1': normal((N_DENSE, D, D_FF), beta * D ** -0.5),
        'ffn_w3': normal((N_DENSE, D, D_FF), beta * D ** -0.5),
        'ffn_w2': normal((N_DENSE, D_FF, D), beta * D_FF ** -0.5),
        'w_router': normal((N_MOE, D, N_EXPERTS), D ** -0.5),
        'b_router': normal((N_MOE, N_EXPERTS), 0.01),
        'exp_w1': normal((N_MOE, N_EXPERTS, D, D_FF_EXPERT), beta * D ** -0.5),
        'exp_w3': normal((N_MOE, N_EXPERTS, D, D_FF_EXPERT), beta * D ** -0.5),
        'exp_w2': normal((N_MOE, N_EXPERTS, D_FF_EXPERT, D), beta * D_FF_EXPERT ** -0.5),
        'ln_ffn_g': 1.0 + normal((L, D), 0.02),
        'ln_ffn_b': normal((L, D), 0.02),
    }

def reference(x, c, w_mod_mix, b_mod_mix, w_in, w_pool, pool_scale, sinks, w_gate, w_branch_a, w_branch_b,
              w_branch_c, w_out, ln_mix_g, ln_mix_b, w_mod_ffn, b_mod_ffn, ffn_w1, ffn_w3, ffn_w2, w_router,
              b_router, exp_w1, exp_w3, exp_w2, ln_ffn_g, ln_ffn_b):
    pos = jnp.arange(x.shape[1])
    for layer in range(DEPTH):
        shift, scale, gate = ada_modulation(c, w_mod_mix[layer], b_mod_mix[layer])
        h = normalize(x) * (1.0 + scale) + shift
        mix = token_mixer(h, pos, w_in[layer], w_pool[layer], pool_scale[layer], sinks[layer], w_gate[layer],
                          w_branch_a[layer], w_branch_b[layer], w_branch_c[layer], w_out[layer])
        x = layer_norm(DEEPNORM_ALPHA * x + (1.0 + gate) * mix, ln_mix_g[layer], ln_mix_b[layer])
        shift, scale, gate = ada_modulation(c, w_mod_ffn[layer], b_mod_ffn[layer])
        h = normalize(x) * (1.0 + scale) + shift
        i = layer // 2
        if layer % 2 == 0:
            ff = swiglu(h, ffn_w1[i], ffn_w3[i], ffn_w2[i])
        else:
            ff = moe_swiglu(h, w_router[i], b_router[i], exp_w1[i], exp_w3[i], exp_w2[i])
        x = layer_norm(DEEPNORM_ALPHA * x + (1.0 + gate) * ff, ln_ffn_g[layer], ln_ffn_b[layer])
    return x


_drawn_inputs = setup_inputs


def setup_inputs(seed=0):
    import zlib

    import numpy as np

    out = dict(_drawn_inputs(seed))
    spreads = {}
    factors = {'w_mod_mix': 2.789,
     'b_mod_mix': 8.0,
     'pool_scale': 8.0,
     'sinks': 48.845,
     'w_branch_c': 3.845,
     'w_mod_ffn': 2.898,
     'b_mod_ffn': 8.0,
     'b_router': 181.845}
    for name, (base, spread) in spreads.items():
        noise = np.random.default_rng([zlib.crc32(name.encode()), seed]).standard_normal(out[name].shape)
        drawn = base * np.exp(spread * noise) if base else spread * noise
        out[name] = __import__('jax').numpy.asarray(drawn.astype(out[name].dtype))
    for name, factor in factors.items():
        out[name] = (out[name] * factor).astype(out[name].dtype)
    return out
```

```python
from contextlib import ExitStack

import numpy as np

import concourse.bass as bass
from concourse import mybir

F32 = mybir.dt.float32
F32R = mybir.dt.float32r
I32 = mybir.dt.int32
ALU = mybir.AluOpType
ACT = mybir.ActivationFunctionType
AX_X = mybir.AxisListType.X

P = 128
D = 1024
KD = D // P
SEQ = 256
TT = SEQ // P
DEPTH = 2
HD = 64
HALF = HD // 2
SB_HEADS = 4
WINDOWS = (2, 4, 8, 16)
Q_HEADS, KV_HEADS = 8, 2
CHUNK = 64
D_FF, D_FFE, EXPERTS = 2816, 3584, 8
EPS = 1e-5
ALPHA = (2 * DEPTH) ** 0.25
SCALE = HD ** -0.5
FAR = -1e30
BANK = 512

QA, KA, VA, UB, QC, KC, VC = 0, 256, 512, 768, 1024, 1536, 1792
PROJ = 1920

SPILL = WINDOWS[-1]
BAND_W = 2 * P + SPILL
C_IDENT, C_ONES, C_PAST, C_TRI = 0, P, 2 * P, 3 * P
C_BAND = 4 * P
C_COS = C_BAND + len(WINDOWS) * BAND_W
C_SIN = C_COS + TT * HD
C_SWM = C_SIN + TT * HD
C_IOTA = C_SWM + P
CONSTS = C_IOTA + SEQ


def constants():
    c = np.zeros((P, CONSTS), np.float32)
    i = np.arange(P)
    c[:, C_IDENT:C_IDENT + P] = np.eye(P)
    c[:, C_ONES:C_ONES + P] = 1.0
    c[:, C_PAST:C_PAST + P] = i[:, None] < i[None, :]
    c[:, C_TRI:C_TRI + P] = i[:, None] >= i[None, :]
    j, s = np.arange(P)[:, None], np.arange(SEQ)[None, :]
    for g, w in enumerate(WINDOWS):
        own = ((s - j >= 0) & (s - j < w)) / np.minimum(s + 1.0, w)
        full = ((s - j >= 0) & (s - j < w)) / float(w)
        base = C_BAND + g * BAND_W
        c[:, base:base + P] = own[:, :P] - np.eye(P)
        c[:, base + P:base + 2 * P] = full[:, :P] - np.eye(P)
        c[:, base + 2 * P:base + BAND_W] = full[:, P:P + SPILL]
    inv = np.power(np.float32(10000.0), -np.arange(HALF, dtype=np.float32) / np.float32(HALF)).astype(np.float32)
    for t in range(TT):
        ang = (np.arange(P) + t * P).astype(np.float32)[:, None] * inv[None, :]
        cos, sin = np.cos(ang), np.sin(ang)
        c[:, C_COS + t * HD:C_COS + (t + 1) * HD] = np.concatenate([cos, cos], 1)
        c[:, C_SIN + t * HD:C_SIN + (t + 1) * HD] = np.concatenate([-sin, sin], 1)
    c[:HD, C_SWM + HD:C_SWM + P] = FAR
    c[:, C_IOTA:C_IOTA + SEQ] = np.arange(SEQ)
    return c


RING, SPLIT = 6, 3
PIECE = 2048
IN_PANELS = 4
GATE_PANELS = 3 * D // BANK
MODS = 12


def mod_stream():
    return [("mod", q) for q in range(MODS)]


def mix_stream():
    s = [("in", n, h) for n in range(3) for h in range(2)] + [("in", 3, 0)]
    for q in range(2 * GATE_PANELS):
        s += [("gate", q // 2, q % 2), ("mod", q)]
    s += [("branch", n, h) for n in range(2) for h in range(2)]
    s += [("out", n, h) for n in range(2) for h in range(2)]
    return s


def ffn_stream(width, mods):
    panels = [min(BANK, width - n) for n in range(0, width, BANK)]
    s = []
    for p, w in enumerate(panels):
        halves = w // (BANK // 2)
        s += [("A", p, h) for h in range(halves)] + [("B", p, h) for h in range(halves)]
        if p:
            s += [("C", p - 1, h) for h in range(2)]
    s += [("C", len(panels) - 1, h) for h in range(panels[-1] // (BANK // 2))]
    if mods:
        for q in reversed(range(MODS)):
            s.insert(2 * q + 5, ("mod", q))
    return panels, s


class Stretch:

    def __init__(self, pieces):
        self.pieces = pieces
        self.loads, self.split_no = [], []
        landed, n = [0] * RING, 0
        for i, piece in enumerate(pieces):
            landed[i % RING] += 32 if piece[0] == "branch" and piece[2] == 0 else 16
            self.loads.append(landed[i % RING])
            self.split_no.append(None if piece[0] == "mod" else n)
            n += piece[0] != "mod"
        self.landed, self.n_split, self.n = landed, n, len(pieces)
        assert n % SPLIT == 0


MOD0 = Stretch(mod_stream())
MIX = Stretch(mix_stream())
DENSE_PANELS, _dense = ffn_stream(D_FF, True)
DENSE = Stretch(_dense)
EXPERT_PANELS, _expert = ffn_stream(D_FFE, False)
EXPERT = Stretch(_expert)
assert EXPERT.n % RING == 0
LAYER_PIECES = MIX.n + DENSE.n
LAYER_SPLITS = MIX.n_split + DENSE.n_split

DVE_MIX_STEPS, DVE_DENSE_STEPS, DVE_ROUTE_STEPS = 37, 13, 34
ACT_MIX_STEPS = 2


class Chain:

    def __init__(self, eng, sem, base=0):
        self.eng, self.sem, self.base, self.n = eng, sem, base, 0

    def step(self, ins):
        ins.then_inc(self.sem, 1)
        self.n += 1
        self.eng.wait_ge(self.sem, self.base + self.n)


def trunk(nc, I, consts, out):
    with ExitStack() as ctx:
        def sb(name, shape, dt=F32, scope=ctx):
            return scope.enter_context(nc.sbuf_tensor(name, shape, dt))

        def sem(name):
            return ctx.enter_context(nc.semaphore(name))

        w_raw = sb("w_raw", [P, RING, PIECE])
        w_hi = sb("w_hi", [P, SPLIT, PIECE], F32R)
        w_lo = sb("w_lo", [P, SPLIT, PIECE], F32R)
        x = sb("x_sb", [P, TT, D])
        hbuf = sb("hbuf", [P, TT, D])
        actT_hi = sb("actT_hi", [P, KD, SEQ], F32R)
        actT_lo = sb("actT_lo", [P, KD, SEQ], F32R)
        cst = sb("cst", [P, CONSTS])
        mod_acc = sb("mod_acc", [P, 3 * D])
        gate1 = sb("gate1", [P, D])
        c_act = sb("c_act", [P, KD])
        stats = sb("stats", [P, TT, 2, 6])
        mv = sb("mv", [P, TT, 2])
        veps = sb("veps", [P, TT])
        std = sb("std", [P, TT])
        rstd = sb("rstd", [P, TT])
        small = sb("small", [P, 64])
        sinks = sb("sinks_sb", [P, Q_HEADS])
        pool_scale = sb("pool_scale_sb", [P, 2])
        counts_i = sb("counts_i", [P, EXPERTS], I32)

        mix = ExitStack()
        lnrow = sb("lnrow", [P, 2, D], scope=mix)
        mix.close()
        cT = sb("cT", [P, 6, SEQ], scope=mix)
        scores = sb("scores", [P, Q_HEADS, P], scope=mix)
        probT = sb("probT", [P, Q_HEADS, P], scope=mix)
        proj = sb("proj", [P, TT, PROJ], scope=mix)
        gates = sb("gates", [P, TT, 3 * D], scope=mix)
        w_pool = sb("w_pool_sb", [P, 2, HD], scope=mix)
        v_even = sb("v_even", [P, P], scope=mix)
        mix.close()
        aT = sb("aT", [P, 4, SEQ], scope=mix)
        z = sb("z_sb", [P, 1536], scope=mix)
        mix.close()
        soft = hbuf[:, :, :].rearrange("p t d -> p (t d)")[:, 0:1536]
        yT = hbuf[:, :, :].rearrange("p t d -> p (t d)").rearrange("p (k q) -> p k q", k=KD)
        ffn = ExitStack()
        h_hi = sb("h_hi", [P, TT, D], F32R, scope=ffn)
        h_lo = sb("h_lo", [P, TT, D], F32R, scope=ffn)
        yacc = sb("yacc", [P, TT, D], scope=ffn)
        silu = sb("silu", [P, 2, BANK], scope=ffn)
        gated = sb("gated", [P, 2, BANK], scope=ffn)
        gT_hi = sb("gT_hi", [P, 2, 4, P], F32R, scope=ffn)
        gT_lo = sb("gT_lo", [P, 2, 4, P], F32R, scope=ffn)
        pick = sb("pick", [P, TT, SEQ], F32R, scope=ffn)
        pick_w = sb("pick_w", [P, TT, SEQ], scope=ffn)
        place = sb("place", [P, 2, SEQ], scope=ffn)
        w_rt = sb("w_rt", [P, KD, EXPERTS], scope=ffn)
        w_rt_hi = sb("w_rt_hi", [P, KD, EXPERTS], F32R, scope=ffn)
        w_rt_lo = sb("w_rt_lo", [P, KD, EXPERTS], F32R, scope=ffn)
        b_rt = sb("b_rt", [P, EXPERTS], scope=ffn)
        rt = sb("rt", [P, 8, TT, EXPERTS], scope=ffn)
        rs = sb("rs", [P, 8, TT, 1], scope=ffn)
        posm = sb("posm", [P, TT, EXPERTS], scope=ffn)
        wsel = sb("wsel", [P, TT, EXPERTS], scope=ffn)
        ffn.close()

        ps = ctx.enter_context(nc.psum_tensor("ps", [P, 8, BANK], F32))

        ident = cst[:, C_IDENT:C_IDENT + P]
        ones = cst[:, C_ONES:C_ONES + P]
        past = cst[:, C_PAST:C_PAST + P]
        tri = cst[:, C_TRI:C_TRI + P]
        iota = cst[:, C_IOTA:C_IOTA + SEQ]
        sw_mask = cst[:, C_SWM:C_SWM + P]

        raw_loaded = [sem(f"raw_loaded{i}") for i in range(RING)]
        piece_used = sem("piece_used")
        split_hi = sem("split_hi")
        split_used = sem("split_used")
        mod_step = sem("mod_step")
        acc_ready = sem("acc_ready")
        x_loaded, c_loaded, cst_loaded = sem("x_loaded"), sem("c_loaded"), sem("cst_loaded")
        small_loaded, ln_loaded, rt_loaded = sem("small_loaded"), sem("ln_loaded"), sem("rt_loaded")
        acc_free, acc_zero, yacc_zero = sem("acc_free"), sem("acc_zero"), sem("yacc_zero")
        c_ready = sem("c_ready")
        out_stored = sem("out_stored")
        var_ready, std_ready = sem("var_ready"), sem("std_ready")
        mod_sent = sem("mod_sent")
        mod_read = sem("mod_read")
        h_ready, hT_sent, hT_hi_ready, hT_lo_ready = sem("h_ready"), sem("hT_sent"), sem("hT_hi_ready"), sem("hT_lo_ready")
        x_ready = sem("x_ready")
        dve_mix, dve_ffn, act_mix = sem("dve_mix"), sem("dve_ffn"), sem("act_mix")
        proj_ready, aT_sent, aT_ready = sem("proj_ready"), sem("aT_sent"), sem("aT_ready")
        z_sent, z_ready, softplus_ready, soft_ready = sem("z_sent"), sem("z_ready"), sem("softplus_ready"), sem("soft_ready")
        suffix_sent, logw_ready, expw_ready, w_ready = sem("suffix_sent"), sem("logw_ready"), sem("expw_ready"), sem("w_ready")
        ya_sent, ya_ready = sem("ya_sent"), sem("ya_ready")
        rope_ready, cT_sent, cT_ready = sem("rope_ready"), sem("cT_sent"), sem("cT_ready")
        pool_sent, pooled_ready, yb_sent, yb_ready = sem("pool_sent"), sem("pooled_ready"), sem("yb_sent"), sem("yb_ready")
        sc_sent, sc_ready, exp_ready, prob_ready = sem("sc_sent"), sem("sc_ready"), sem("exp_ready"), sem("prob_ready")
        pT_sent, pT_ready, yc_sent, yc_ready = sem("pT_sent"), sem("pT_ready"), sem("yc_sent"), sem("yc_ready")
        v_ready, gate_ready = sem("v_ready"), sem("gate_ready")
        yT_hi_ready, yT_lo_ready = sem("yT_hi_ready"), sem("yT_lo_ready")
        merged_ready, mT_sent, mT_hi_ready, mT_lo_ready = sem("merged_ready"), sem("mT_sent"), sem("mT_hi_ready"), sem("mT_lo_ready")
        silu_ready, gated_ready = sem("silu_ready"), sem("gated_ready")
        gT_sent, gT_hi_ready, gT_lo_ready = sem("gT_sent"), sem("gT_hi_ready"), sem("gT_lo_ready")
        hh_ready, hl_ready, rt_hi, rt_lo = sem("hh_ready"), sem("hl_ready"), sem("rt_hi"), sem("rt_lo")
        logits_sent, gap_ready, e2_ready, sel_ready = sem("logits_sent"), sem("gap_ready"), sem("e2_ready"), sem("sel_ready")
        pos_sent, counts_ready = sem("pos_sent"), sem("counts_ready")
        pick_ready, place_sent, place_ready = sem("pick_ready"), sem("place_sent"), sem("place_ready")
        gathered = [sem(f"gathered{b}") for b in range(2)]
        xg_hi_ready = [sem(f"xg_hi_ready{b}") for b in range(2)]
        xg_lo_ready = [sem(f"xg_lo_ready{b}") for b in range(2)]
        y_act, y_dve, scattered, added = sem("y_act"), sem("y_dve"), sem("scattered"), sem("added")

        block = ctx.enter_context(nc.Block())

        def weight_rows(w):
            return w.rearrange("(k p) n -> p k n", p=P)

        def bank(b, n=BANK):
            return ps[:, b, 0:n]

        @block.sync
        def _(sp):
            sp.sem_inc(piece_used, RING)
            sp.sem_inc(split_used, SPLIT)

            def load(slot, piece, layer, expert=None):
                kind, a, h = piece[0], piece[1], piece[-1]
                dst = w_raw[:, slot, :]
                d4, d8 = dst.rearrange("p (k n) -> p k n", k=4), dst.rearrange("p (k n) -> p k n", k=8)
                d2 = dst.rearrange("p (k n) -> p k n", k=2)
                if kind == "mod":
                    w = I["w_mod_ffn"] if layer[0] == "ffn" else I["w_mod_mix"]
                    src = weight_rows(w[layer[1]])
                    pairs = [(d2, src[:, 2 * (a % 4):2 * (a % 4) + 2, D * (a // 4):D * (a // 4 + 1)])]
                elif kind == "branch":
                    cols = slice(a * BANK, (a + 1) * BANK)
                    if h == 0:
                        pairs = [(d4[:, 0:2, :], weight_rows(I["w_branch_a"][layer])[:, :, cols]),
                                 (d4[:, 2:4, :], weight_rows(I["w_branch_b"][layer])[:, :, cols])]
                    else:
                        pairs = [(d4, weight_rows(I["w_branch_c"][layer])[:, :, cols])]
                elif kind == "C":
                    w = I["ffn_w2"][0] if expert is None else I["exp_w2"][0, expert]
                    pairs = [(d2, weight_rows(w)[:, 4 * a + 2 * h:4 * a + 2 * h + 2, :])]
                else:
                    w = {"in": lambda: I["w_in"][layer], "gate": lambda: I["w_gate"][layer],
                         "out": lambda: I["w_out"][layer],
                         "A": lambda: I["ffn_w1"][0] if expert is None else I["exp_w1"][0, expert],
                         "B": lambda: I["ffn_w3"][0] if expert is None else I["exp_w3"][0, expert]}[kind]()
                    width = w.shape[-1]
                    c0, c1 = a * BANK, min((a + 1) * BANK, width)
                    if c1 - c0 == BANK:
                        pairs = [(d4, weight_rows(w)[:, 4 * h:4 * h + 4, c0:c1])]
                    else:
                        pairs = [(d8, weight_rows(w)[:, :, c0:c1])]
                for d, s in pairs:
                    sp.dma_start(d, s).then_inc(raw_loaded[slot], 16)

            def stream(stretch, base, layer, expert=None, mod_layer=None, gap=True):
                for i, piece in enumerate(stretch.pieces):
                    if i < RING:
                        before = base - RING + i + 1 if not gap or i >= RING // 2 else base - RING // 2 + i + 1
                    else:
                        before = base + i - RING + 1
                    sp.wait_ge(piece_used, before + RING)
                    load(i % RING, piece, mod_layer if piece[0] == "mod" else layer, expert)

            sp.dma_start(c_act[:, :], I["c"].rearrange("b (k p) -> p (b k)", p=P),
                         allow_slow_non_contiguous=True).then_inc(c_loaded, 16)
            xv = I["x"].rearrange("b (t p) d -> p (b t) d", p=P)
            sp.dma_start(x[:, :, :], xv).then_inc(x_loaded, 16)
            sp.dma_start(cst[:, :], consts).then_inc(cst_loaded, 16)
            stream(MOD0, 0, None, mod_layer=("mix", 0), gap=False)
            with sp.Fori(0, DEPTH) as layer:
                stream(MIX, layer * LAYER_PIECES + MOD0.n, layer, mod_layer=("ffn", layer))
                with sp.If(layer < 1):
                    stream(DENSE, MOD0.n + MIX.n, 0, mod_layer=("mix", 1))
                with sp.Else():
                    moe0 = MOD0.n + LAYER_PIECES + MIX.n
                    sp.wait_ge(piece_used, moe0 + RING)
                    with sp.Fori(0, EXPERTS) as e:
                        stream(EXPERT, e * EXPERT.n + moe0, 1, expert=e, gap=False)
            sp.wait_ge(x_ready, 2 * DEPTH + 1)
            sp.dma_start(out.rearrange("b (t p) d -> p (b t) d", p=P), x[:, :, :]).then_inc(out_stored, 16)
            sp.wait_ge(out_stored, 16)

        @block.gpsimd
        def _(gp):
            def fresh_acc(bias_row, n):
                nc.gpsimd.memset(mod_acc[:, :], 0.0).then_inc(acc_zero, 1)
                gp.wait_ge(acc_zero, n + 1)
                gp.dma_start(mod_acc[0:1, :], bias_row).then_inc(acc_ready, 16)

            def ln_rows(g, b):
                gp.dma_start(lnrow[:, 0, :], g.partition_broadcast(P)).then_inc(ln_loaded, 16)
                gp.dma_start(lnrow[:, 1, :], b.partition_broadcast(P)).then_inc(ln_loaded, 16)

            fresh_acc(I["b_mod_mix"][0:1, :], 0)
            with gp.Fori(0, DEPTH) as layer:
                gp.wait_ge(mod_read, layer * 2 + 1)
                gp.dma_start(sinks[:, :], I["sinks"][bass.ds(layer, 1), :].rearrange("a h -> (a h)").partition_broadcast(P)).then_inc(small_loaded, 16)
                gp.dma_start(pool_scale[:, :], I["pool_scale"][bass.ds(layer, 1), :].rearrange("a (k p) -> p (a k)", p=P),
                             allow_slow_non_contiguous=True).then_inc(small_loaded, 16)
                for par in range(2):
                    gp.dma_start(w_pool[par * HD:(par + 1) * HD, :, :],
                                 I["w_pool"][bass.ds(layer, 1)].rearrange("a (k r) c e -> c r (a k) e", r=2)[:, par],
                                 ).then_inc(small_loaded, 16)
                gp.wait_ge(mod_sent, layer * 2 + 1)
                gp.sem_inc(acc_free, 1)
                fresh_acc(I["b_mod_ffn"][bass.ds(layer, 1), :], layer * 2 + 1)
                gp.wait_ge(merged_ready, layer * 4 + 4)
                ln_rows(I["ln_mix_g"][bass.ds(layer, 1), :].rearrange("a d -> (a d)"),
                        I["ln_mix_b"][bass.ds(layer, 1), :].rearrange("a d -> (a d)"))
                with gp.If(layer < 1):
                    gp.wait_ge(mod_sent, 2)
                    fresh_acc(I["b_mod_mix"][1:2, :], 2)
                    ln_rows(I["ln_ffn_g"][0], I["ln_ffn_b"][0])
                with gp.Else():
                    gp.wait_ge(x_ready, 4)
                    gp.dma_start(w_rt[:, :, :], I["w_router"][0].rearrange("(k p) e -> p k e", p=P),
                                 ).then_inc(rt_loaded, 16)
                    gp.dma_start(b_rt[:, :], I["b_router"][0].partition_broadcast(P)).then_inc(rt_loaded, 16)
                    nc.gpsimd.memset(yacc[:, :, :], 0.0).then_inc(yacc_zero, 1)
                    for b in range(2):
                        gp.wait_ge(gathered[b], EXPERTS)
                    ln_rows(I["ln_ffn_g"][1], I["ln_ffn_b"][1])

        @block.scalar
        def _(act):
            A = nc.scalar.activation

            def round_piece(stretch, i, load_base, split_base):
                j = stretch.split_no[i]
                act.wait_ge(raw_loaded[i % RING], load_base[i % RING] + stretch.loads[i])
                act.wait_ge(split_used, split_base + j + 1)
                nc.scalar.copy(w_hi[:, j % SPLIT, :], w_raw[:, i % RING, :]).then_inc(split_hi, 1)

            def stream(stretch, load_base, split_base, after):
                for i, piece in enumerate(stretch.pieces):
                    if piece[0] == "mod":
                        continue
                    j = stretch.split_no[i]
                    if j >= SPLIT:
                        after(j - SPLIT)
                    round_piece(stretch, i, load_base, split_base)
                for j in range(stretch.n_split - SPLIT, stretch.n_split):
                    after(j)

            def root(n):
                act.wait_ge(var_ready, n)
                A(std[:, :], veps[:, :], ACT.Sqrt).then_inc(std_ready, 1)

            def pre_norm(sub):
                root(sub * 2 + 1)
                for t in range(TT):
                    act.wait_ge(hT_sent, sub * TT + t + 1)
                    for c in range(2):
                        A(actT_hi[:, 4 * c:4 * c + 4, t * P:(t + 1) * P],
                          bank((6, 0)[t] + c).rearrange("p (k q) -> p k q", k=4), ACT.Copy).then_inc(hT_hi_ready, 1)

            act.wait_ge(c_loaded, 16)
            A(c_act[:, :], c_act[:, :], ACT.Silu).then_inc(c_ready, 1)

            with act.Fori(0, DEPTH) as layer:
                sbase = layer * LAYER_SPLITS
                chain = Chain(act, act_mix, layer * ACT_MIX_STEPS)
                pre_norm(layer * 2)

                def used(j):
                    act.wait_ge(split_used, sbase + j + 1 + SPLIT)

                def exp_scores(t):
                    act.wait_ge(sc_ready, layer * 2 + t + 1)
                    A(scores[:, :, :], scores[:, :, :], ACT.Exp)
                    A(small[:, 16:24], small[:, 16:24], ACT.Exp).then_inc(exp_ready, 1)

                def probs_T(t):
                    act.wait_ge(pT_sent, layer * 2 + t + 1)
                    A(probT[:, :, :], ps[:, 4:6, :].rearrange("p b (i q) -> p (b i) q", q=P), ACT.Copy).then_inc(pT_ready, 1)

                def after(j):
                    if j in (1, 3, 5):
                        used(j)
                        n = j // 2
                        for t in range(TT):
                            A(proj[:, t, n * BANK:(n + 1) * BANK], bank(2 * (n % 2) + t), ACT.Copy).then_inc(proj_ready, 1)
                    if j == 4:
                        act.wait_ge(aT_sent, layer + 1)
                        for b in range(2):
                            A(aT[:, 2 * b:2 * b + 2, :], bank(4 + b).rearrange("p (c q) -> p c q", c=2), ACT.Copy).then_inc(aT_ready, 1)
                    if j == 6:
                        used(j)
                        for t in range(TT):
                            twice = proj[:, t, KC:VC].rearrange("p (g r d) -> p r g d", g=2, r=2)
                            for r in range(2):
                                A(twice[:, r], bank(2 + t)[:, 0:P].rearrange("p (g d) -> p g d", g=2), ACT.Copy)
                            A(proj[:, t, VC:PROJ], bank(2 + t)[:, P:2 * P], ACT.Copy).then_inc(proj_ready, 1)
                        act.wait_ge(z_ready, layer * 2 + 2)
                        chain.step(A(soft, z[:, :], ACT.Abs))
                        chain.step(A(soft, soft, ACT.Exp, scale=-1.0))
                        A(soft, soft, ACT.Ln, bias=1.0).then_inc(softplus_ready, 1)
                    if j == 9:
                        act.wait_ge(logw_ready, layer + 1)
                        A(z[:, :], z[:, :], ACT.Exp).then_inc(expw_ready, 1)
                    if j == 11:
                        act.wait_ge(cT_sent, layer + 1)
                        act.wait_ge(ya_sent, layer + 1)
                        for b in range(3):
                            A(cT[:, 2 * b:2 * b + 2, :], bank(4 + b).rearrange("p (c q) -> p c q", c=2), ACT.Copy).then_inc(cT_ready, 1)
                    if j == 12:
                        act.wait_ge(pool_sent, layer + 1)
                        A(proj[:, :, QA:KA], bank(7).rearrange("p (k q) -> p k q", k=2), ACT.Copy).then_inc(pooled_ready, 1)
                        A(v_even[0:HD, :], proj[0:HD, 1, VC:PROJ], ACT.Copy)
                        A(v_even[HD:P, :], proj[HD:P, 0, VC:PROJ], ACT.Copy).then_inc(v_ready, 1)
                    if j == 13:
                        exp_scores(0)
                    if j == 14:
                        probs_T(0)
                    if j == 16:
                        exp_scores(1)
                    if j == 17:
                        probs_T(1)
                    if j >= 8 and j % 2 == 0 and j <= 18:
                        used(j)
                        g = (j - 8) // 2
                        for t in range(TT):
                            A(gates[:, t, g * BANK:(g + 1) * BANK], bank(2 * (g % 2) + t), ACT.Sigmoid).then_inc(gate_ready, 1)
                    if j == 18:
                        act.wait_ge(ya_ready, layer + 1)
                        act.wait_ge(yb_ready, layer + 1)
                        A(actT_hi[:, 0:4, :], yT[:, 0:4, :], ACT.Copy).then_inc(yT_hi_ready, 1)
                        act.wait_ge(yc_ready, layer * 2 + 2)
                        A(actT_hi[:, 4:8, :], yT[:, 4:8, :], ACT.Copy).then_inc(yT_hi_ready, 1)
                    if j == 22:
                        for t in range(TT):
                            act.wait_ge(mT_sent, layer * 2 + t + 1)
                            for c in range(2):
                                A(actT_hi[:, 4 * c:4 * c + 4, t * P:(t + 1) * P],
                                  bank(4 + 2 * t + c).rearrange("p (k q) -> p k q", k=4), ACT.Copy).then_inc(mT_hi_ready, 1)

                layer_loads = [MIX.landed[s] + DENSE.landed[s] for s in range(RING)]
                stream(MIX, [layer * layer_loads[s] + MOD0.landed[s] for s in range(RING)], sbase, after)
                assert chain.n == ACT_MIX_STEPS, chain.n
                root(layer * 4 + 2)

                def swiglu(stretch, panels, load_base, split_base, panel0, blocks, tail):
                    first_b = {stretch.split_no[i]: p[1] for i, p in enumerate(stretch.pieces) if p[0] == "B" and p[2] == 0}
                    last = {(p[0], p[1]): stretch.split_no[i] for i, p in enumerate(stretch.pieces) if p[0] != "mod"}
                    last = {v: k for k, v in last.items()}

                    def gT_part(p):
                        act.wait_ge(gT_sent, panel0 + p + 1)
                        w = panels[p]
                        for b in range(blocks):
                            ins = A(gT_hi[:, b, 0:w // P, :], ps[:, b, 0:w].rearrange("p (c q) -> p c q", q=P), ACT.Copy)
                        ins.then_inc(gT_hi_ready, 1)

                    def after(j):
                        kind, p = last.get(j, ("", 0))
                        if kind == "A":
                            act.wait_ge(split_used, split_base + j + 1 + SPLIT)
                            if p:
                                act.wait_ge(gated_ready, panel0 + p)
                            w = panels[p]
                            for b in range(blocks):
                                ins = A(silu[:, b, 0:w], ps[:, b, 0:w], ACT.Silu)
                            ins.then_inc(silu_ready, 1)
                        if j in first_b and first_b[j]:
                            gT_part(first_b[j] - 1)
                        if kind == "C" and p == len(panels) - 2:
                            gT_part(len(panels) - 1)

                    stream(stretch, load_base, split_base, after)
                    tail()

                with act.If(layer < 1):
                    pre_norm(1)
                    swiglu(DENSE, DENSE_PANELS, [MOD0.landed[s] + MIX.landed[s] for s in range(RING)],
                           MIX.n_split, 0, 2, lambda: root(4))
                with act.Else():
                    pre_norm(3)
                    for t in range(TT):
                        ins = A(h_hi[:, t, :], hbuf[:, t, :], ACT.Copy)
                    ins.then_inc(hh_ready, 1)
                    act.wait_ge(rt_loaded, 32)
                    A(w_rt_hi[:, :, :], w_rt[:, :, :], ACT.Copy).then_inc(rt_hi, 1)
                    act.wait_ge(gap_ready, 1)
                    A(rs[:, 4], rs[:, 3], ACT.Exp).then_inc(e2_ready, 1)
                    act.wait_ge(counts_ready, 1)
                    moe_loads = [MOD0.landed[s] + 2 * MIX.landed[s] + DENSE.landed[s] for s in range(RING)]
                    with act.Fori(0, EXPERTS) as e:
                        count = act.value_load(counts_i[0:1, bass.ds(e, 1)], min_val=0, max_val=SEQ)

                        def expert(blocks):
                            for b in range(blocks):
                                act.wait_ge(gathered[b], e + 1)
                                A(actT_hi[:, :, b * P:(b + 1) * P],
                                  ps[:, 0:2, :].rearrange("p c (k q) -> p (c k) q", q=P), ACT.Copy).then_inc(xg_hi_ready[b], 1)
                            act.wait_ge(place_sent, e + 1)
                            A(place[:, 0:blocks, :], ps[:, 4, 0:blocks * SEQ].rearrange("p (b q) -> p b q", q=SEQ),
                              ACT.Copy).then_inc(place_ready, 1)

                            def rows_out():
                                act.wait_ge(split_used, e * EXPERT.n_split + (LAYER_SPLITS + MIX.n_split + EXPERT.n_split + SPLIT))
                                for b in range(blocks):
                                    ins = A(hbuf[:, b, 0:BANK], bank(4 + 2 * b), ACT.Copy)
                                ins.then_inc(y_act, 1)

                            swiglu(EXPERT, EXPERT_PANELS, [e * EXPERT.landed[s] + moe_loads[s] for s in range(RING)],
                                   e * EXPERT.n_split + (LAYER_SPLITS + MIX.n_split),
                                   e * len(EXPERT_PANELS) + len(DENSE_PANELS), blocks, rows_out)

                        with act.If(count > P):
                            expert(2)
                        with act.Else():
                            act.sem_inc(xg_hi_ready[1], 1)
                            expert(1)
                    root(8)

        @block.vector
        def _(dve):
            TS, TTn, STT, RED = nc.vector.tensor_scalar, nc.vector.tensor_tensor, nc.vector.scalar_tensor_tensor, nc.vector.tensor_reduce

            def rest_of_piece(stretch, i, split_base):
                j = stretch.split_no[i]
                dve.wait_ge(split_hi, split_base + j + 1)
                TTn(w_lo[:, j % SPLIT, :], w_raw[:, i % RING, :], w_hi[:, j % SPLIT, :].bitcast(F32),
                    ALU.subtract).then_inc(piece_used, 1)

            def mod_piece(stretch, i, load_base, piece_base, step_base, acc_no):
                q = stretch.pieces[i][1]
                if q == 0:
                    dve.wait_ge(acc_ready, acc_no * 16)
                    dve.wait_ge(c_ready, 1)
                dve.wait_ge(raw_loaded[i % RING], load_base[i % RING] + stretch.loads[i])
                w = w_raw[:, i % RING, :].rearrange("p (k n) -> p k n", k=2)
                previous = max((m for m in range(i) if stretch.pieces[m][0] == "mod"), default=None)
                for m in range(4):
                    k, n = m // 2, m % 2
                    acc = mod_acc[:, (q // 4) * D + n * BANK:(q // 4) * D + (n + 1) * BANK]
                    if m == 0 and q:
                        dve.wait_ge(mod_step, step_base + 3 * q)
                    if m == 1 and q:
                        dve.wait_ge(piece_used, piece_base + previous + 1 + RING)
                    if m >= 2:
                        dve.wait_ge(mod_step, step_base + 3 * q + m - 1)
                    ins = STT(acc, w[:, k, n * BANK:(n + 1) * BANK], c_act[:, 2 * (q % 4) + k:2 * (q % 4) + k + 1], acc,
                              ALU.mult, ALU.add)
                    ins.then_inc(piece_used if m == 3 else mod_step, 1)

            def stream(stretch, load_base, split_base, piece_base, step_base, acc_no, after):
                for i, piece in enumerate(stretch.pieces):
                    if piece[0] == "mod":
                        mod_piece(stretch, i, load_base, piece_base, step_base, acc_no)
                        continue
                    j = stretch.split_no[i]
                    if j >= SPLIT:
                        after(j - SPLIT)
                    rest_of_piece(stretch, i, split_base)
                for j in range(stretch.n_split - SPLIT, stretch.n_split):
                    after(j)

            def statistics(chain, src, n):
                for t in range(TT):
                    for c in range(2):
                        ins = nc.vector.bn_stats(stats[:, t, c, :], src[:, t, c * BANK:(c + 1) * BANK])
                chain.step(ins)
                nc.vector.memset(veps[:, :], 0.0)
                for t in range(TT):
                    ins = nc.vector.bn_aggr(mv[:, t, :], stats[:, t, :, :].rearrange("p c s -> p (c s)"))
                chain.step(ins)
                TS(veps[:, :], mv[:, :, 1], EPS, None, ALU.add).then_inc(var_ready, 1)
                dve.wait_ge(std_ready, n)
                chain.step(nc.vector.reciprocal(rstd[:, :], std[:, :]))

            def pre_norm(chain, sub):
                dve.wait_ge(x_ready, sub + 1)
                statistics(chain, x, sub * 2 + 1)
                for t in range(TT):
                    ins = TS(hbuf[:, t, :], x[:, t, :], mv[:, t, 0:1], rstd[:, t:t + 1], ALU.subtract, ALU.mult)
                chain.step(ins)
                dve.wait_ge(mod_sent, sub + 1)
                for t in range(TT):
                    for c in range(2):
                        part = hbuf[:, t, c * BANK:(c + 1) * BANK]
                        ins = STT(part, bank(2 + c), 1.0, part, ALU.add, ALU.mult)
                    chain.step(ins)
                    for c in range(2):
                        part = hbuf[:, t, c * BANK:(c + 1) * BANK]
                        ins = TTn(part, part, bank(c), ALU.add)
                    ins.then_inc(h_ready, 1)
                for c in range(2):
                    ins = TS(gate1[:, c * BANK:(c + 1) * BANK], bank(4 + c), 1.0, None, ALU.add)
                ins.then_inc(mod_read, 1)
                for t in range(TT):
                    for c in range(2):
                        dve.wait_ge(hT_hi_ready, sub * 4 + 2 * t + c + 1)
                        at = (slice(None), slice(4 * c, 4 * c + 4), slice(t * P, (t + 1) * P))
                        TTn(actT_lo[at], bank((6, 0)[t] + c).rearrange("p (k q) -> p k q", k=4), actT_hi[at].bitcast(F32),
                            ALU.subtract).then_inc(hT_lo_ready, 1)

            def post_norm(chain, sub, f, n_ln):
                dve.wait_ge(mod_read, sub + 1)
                for t in range(TT):
                    for c in range(2):
                        ins = TTn(hbuf[:, t, c * BANK:(c + 1) * BANK], f(t, c), gate1[:, c * BANK:(c + 1) * BANK], ALU.mult)
                chain.step(ins)
                for t in range(TT):
                    ins = STT(hbuf[:, t, :], x[:, t, :], ALPHA, hbuf[:, t, :], ALU.mult, ALU.add)
                chain.step(ins)
                statistics(chain, hbuf, sub * 2 + 2)
                for t in range(TT):
                    ins = TS(hbuf[:, t, :], hbuf[:, t, :], mv[:, t, 0:1], rstd[:, t:t + 1], ALU.subtract, ALU.mult)
                chain.step(ins)
                dve.wait_ge(ln_loaded, n_ln)
                for t in range(TT):
                    ins = TTn(hbuf[:, t, :], hbuf[:, t, :], lnrow[:, 0, :], ALU.mult)
                chain.step(ins)
                for t in range(TT):
                    ins = TTn(x[:, t, :], hbuf[:, t, :], lnrow[:, 1, :], ALU.add)
                ins.then_inc(x_ready, 1)

            dve.wait_ge(x_loaded, 16)
            dve.sem_inc(x_ready, 1)
            dve.sem_inc(added, 4)
            for i in range(MOD0.n):
                mod_piece(MOD0, i, [0] * RING, 0, 0, 1)
            dve.wait_ge(cst_loaded, 16)

            with dve.Fori(0, DEPTH) as layer:
                sbase = layer * LAYER_SPLITS
                chain = Chain(dve, dve_mix, layer * DVE_MIX_STEPS)
                step = chain.step
                pre_norm(chain, layer * 2)
                z0 = z[:, 0:1024].rearrange("p (h q) -> p h q", h=4)
                z1 = z[:, 1024:1536].rearrange("p (h q) -> p h q", h=4)
                s0 = soft[:, 0:1024].rearrange("p (h q) -> p h q", h=4)
                s1 = soft[:, 1024:1536].rearrange("p (h q) -> p h q", h=4)
                past4 = past.unsqueeze(1).broadcast_to([P, 4, P])
                sink_v = sinks[:, :].rearrange("p (i r) -> p r i", r=2)
                mx = small[:, 0:8]
                mx_v = mx.rearrange("p (r i) -> p r i", r=2)
                es = small[:, 16:24]
                den, rden = small[:, 24:32], small[:, 32:40]

                def rotate(t):
                    v = proj[:, t, QC:VC].rearrange("p (h d) -> p h d", d=HD)
                    n = v.shape[1]
                    ta = gates[:, 0, 3 * D - n * HD:3 * D].rearrange("p (h d) -> p h d", d=HD)
                    tb = gates[:, 1, 3 * D - n * HD:3 * D].rearrange("p (h d) -> p h d", d=HD)
                    cos = cst[:, C_COS + t * HD:C_COS + (t + 1) * HD].unsqueeze(1).broadcast_to([P, n, HD])
                    sin = cst[:, C_SIN + t * HD:C_SIN + (t + 1) * HD].unsqueeze(1)
                    TTn(ta, v, cos, ALU.mult)
                    TTn(tb[:, :, 0:HALF], v[:, :, HALF:HD], sin[:, :, 0:HALF].broadcast_to([P, n, HALF]), ALU.mult)
                    step(TTn(tb[:, :, HALF:HD], v[:, :, 0:HALF], sin[:, :, HALF:HD].broadcast_to([P, n, HALF]), ALU.mult))
                    TTn(v, ta, tb, ALU.add).then_inc(rope_ready, 1)
                    dve.wait_ge(rope_ready, layer * 2 + t + 1)

                def shift_scores(t):
                    dve.wait_ge(sc_sent, layer * 2 + t + 1)
                    raw = ps[:, 4:6, :].rearrange("p b (i q) -> p (b i) q", q=P)
                    if t == 0:
                        step(STT(scores[:, :, :], raw, SCALE, sw_mask.unsqueeze(1).broadcast_to([P, 8, P]), ALU.mult, ALU.add))
                        dve.wait_ge(small_loaded, layer * 64 + 64)
                    else:
                        step(TS(scores[:, :, :], raw, SCALE, None, ALU.mult))
                    step(RED(mx, scores[:, :, :], AX_X, ALU.max))
                    step(TTn(mx_v, mx_v, sink_v, ALU.max))
                    TTn(es.rearrange("p (r i) -> p r i", r=2), sink_v, mx_v, ALU.subtract)
                    TTn(scores[:, :, :], scores[:, :, :], mx.unsqueeze(2).broadcast_to([P, 8, P]), ALU.subtract).then_inc(sc_ready, 1)

                def divide_scores(t):
                    dve.wait_ge(exp_ready, layer * 2 + t + 1)
                    step(RED(den, scores[:, :, :], AX_X, ALU.add))
                    step(TTn(den, den, es, ALU.add))
                    step(nc.vector.reciprocal(rden, den))
                    TTn(scores[:, :, :], scores[:, :, :], rden.unsqueeze(2).broadcast_to([P, 8, P]), ALU.mult).then_inc(prob_ready, 1)

                def yc_out(t):
                    dve.wait_ge(yc_sent, layer * 2 + t + 1)
                    nc.vector.tensor_copy(yT[:, 4:8, t * P:(t + 1) * P], bank(6).rearrange("p (i q) -> p i q", q=P)).then_inc(yc_ready, 1)

                def merge(n):
                    where = {0: (0, 2, 4), 1: (6, 0, 2)}[n]
                    dve.wait_ge(gate_ready, layer * 12 + 12)
                    for br in range(3):
                        for t in range(TT):
                            gate = gates[:, t, br * D + n * BANK:br * D + (n + 1) * BANK]
                            ins = TTn(gate, gate, bank(where[br] + t), ALU.mult)
                        step(ins)
                    for t in range(TT):
                        g = [gates[:, t, br * D + n * BANK:br * D + (n + 1) * BANK] for br in range(3)]
                        ins = TTn(g[0], g[0], g[1], ALU.add)
                    step(ins)
                    for t in range(TT):
                        g = [gates[:, t, br * D + n * BANK:br * D + (n + 1) * BANK] for br in range(3)]
                        TTn(hbuf[:, t, n * BANK:(n + 1) * BANK], g[0], g[2], ALU.add).then_inc(merged_ready, 1)

                def after(j):
                    if j == 5:
                        dve.wait_ge(z_sent, layer + 1)
                        TS(z[:, 0:1024], ps[:, 4:6, :].rearrange("p b q -> p (b q)"), SCALE, None, ALU.mult).then_inc(z_ready, 1)
                        TS(z[:, 1024:1536].rearrange("p (b q) -> p b q", b=2), ps[:, 6:8, 0:256], SCALE, None, ALU.mult).then_inc(z_ready, 1)
                    if j == 6:
                        dve.wait_ge(softplus_ready, layer + 1)
                        step(STT(soft, z[:, :], 0.0, soft, ALU.max, ALU.add))
                        TTn(s0[:, :, 0:P], s0[:, :, 0:P], past4, ALU.mult)
                        TTn(s1, s1, past4, ALU.mult).then_inc(soft_ready, 1)
                    if j == 7:
                        dve.wait_ge(proj_ready, layer * 8 + 8)
                        for t in range(TT):
                            rotate(t)
                    if j == 8:
                        dve.wait_ge(suffix_sent, layer + 1)
                        TTn(z[:, 0:1024], z[:, 0:1024], ps[:, 4:6, :].rearrange("p b q -> p (b q)"), ALU.subtract)
                        step(TTn(z[:, 1024:1536], z[:, 1024:1536], bank(6), ALU.subtract))
                        TS(z[:, :], z[:, :], 0.0, None, ALU.min).then_inc(logw_ready, 1)
                    if j == 9:
                        dve.wait_ge(expw_ready, layer + 1)
                        TTn(z0[:, :, 0:P], z0[:, :, 0:P], past4, ALU.mult)
                        TTn(z1, z1, past4, ALU.mult).then_inc(w_ready, 1)
                    if j == 11:
                        dve.wait_ge(ya_sent, layer + 1)
                        nc.vector.tensor_copy(yT[:, 0:2, :], bank(7).rearrange("p (k q) -> p k q", k=2)).then_inc(ya_ready, 1)
                    if j == 12:
                        shift_scores(0)
                    if j == 13:
                        divide_scores(0)
                    if j == 14:
                        dve.wait_ge(yb_sent, layer + 1)
                        for k in range(2):
                            ins = TS(yT[:, 2 + k, :], bank(7)[:, k * 256:(k + 1) * 256], pool_scale[:, k:k + 1], None, ALU.mult)
                        ins.then_inc(yb_ready, 1)
                    if j == 15:
                        yc_out(0)
                        shift_scores(1)
                    if j == 16:
                        divide_scores(1)
                    if j == 18:
                        yc_out(1)
                        for c in range(2):
                            dve.wait_ge(yT_hi_ready, layer * 2 + c + 1)
                            if c:
                                dve.wait_ge(yc_ready, layer * 2 + 2)
                            part = (slice(None), slice(4 * c, 4 * c + 4), slice(None))
                            TTn(actT_lo[part], yT[part], actT_hi[part].bitcast(F32), ALU.subtract).then_inc(yT_lo_ready, 1)
                    if j == 20:
                        dve.wait_ge(split_used, sbase + 21 + SPLIT)
                        merge(0)
                    if j == 22:
                        dve.wait_ge(split_used, sbase + 23 + SPLIT)
                        merge(1)
                        for t in range(TT):
                            for c in range(2):
                                dve.wait_ge(mT_hi_ready, layer * 4 + 2 * t + c + 1)
                                at = (slice(None), slice(4 * c, 4 * c + 4), slice(t * P, (t + 1) * P))
                                TTn(actT_lo[at], bank(4 + 2 * t + c).rearrange("p (k q) -> p k q", k=4), actT_hi[at].bitcast(F32),
                                    ALU.subtract).then_inc(mT_lo_ready, 1)

                layer_loads = [MIX.landed[s] + DENSE.landed[s] for s in range(RING)]
                stream(MIX, [layer * layer_loads[s] + MOD0.landed[s] for s in range(RING)], sbase,
                       layer * LAYER_PIECES + MOD0.n, layer * (6 * MODS) + 3 * MODS, layer * 2 + 2, after)
                dve.wait_ge(split_used, sbase + MIX.n_split + SPLIT)
                post_norm(chain, layer * 2, lambda t, c: bank(2 * t + c), layer * 64 + 32)
                assert chain.n == DVE_MIX_STEPS, chain.n

                def swiglu(stretch, panels, load_base, split_base, piece_base, step_base, panel0, blocks):
                    first_b = {stretch.split_no[i]: p[1] for i, p in enumerate(stretch.pieces) if p[0] == "B" and p[2] == 0}
                    last = {(p[0], p[1]): stretch.split_no[i] for i, p in enumerate(stretch.pieces) if p[0] != "mod"}
                    last = {v: k for k, v in last.items()}

                    def gT_part(p):
                        dve.wait_ge(gT_hi_ready, panel0 + p + 1)
                        w = panels[p]
                        for b in range(blocks):
                            ins = TTn(gT_lo[:, b, 0:w // P, :], ps[:, b, 0:w].rearrange("p (c q) -> p c q", q=P),
                                      gT_hi[:, b, 0:w // P, :].bitcast(F32), ALU.subtract)
                        ins.then_inc(gT_lo_ready, 1)

                    def after(j):
                        kind, p = last.get(j, ("", 0))
                        if j in first_b and first_b[j]:
                            gT_part(first_b[j] - 1)
                        if kind == "B":
                            dve.wait_ge(split_used, split_base + j + 1 + SPLIT)
                            dve.wait_ge(silu_ready, panel0 + p + 1)
                            w = panels[p]
                            for b in range(blocks):
                                ins = TTn(gated[:, b, 0:w], silu[:, b, 0:w], ps[:, 2 + b, 0:w], ALU.mult)
                            ins.then_inc(gated_ready, 1)
                        if kind == "C" and p == len(panels) - 2:
                            gT_part(len(panels) - 1)

                    stream(stretch, load_base, split_base, piece_base, step_base, 3, after)

                with dve.If(layer < 1):
                    chain = Chain(dve, dve_ffn, 0)
                    pre_norm(chain, 1)
                    swiglu(DENSE, DENSE_PANELS, [MOD0.landed[s] + MIX.landed[s] for s in range(RING)],
                           MIX.n_split, MOD0.n + MIX.n, 6 * MODS, 0, 2)
                    dve.wait_ge(split_used, LAYER_SPLITS + SPLIT)
                    post_norm(chain, 1, lambda t, c: bank(4 + 2 * t + c), 64)
                    assert chain.n == DVE_DENSE_STEPS, chain.n
                with dve.Else():
                    chain = Chain(dve, dve_ffn, DVE_DENSE_STEPS)
                    step = chain.step
                    pre_norm(chain, 3)
                    dve.wait_ge(hh_ready, 1)
                    for t in range(TT):
                        ins = TTn(h_lo[:, t, :], hbuf[:, t, :], h_hi[:, t, :].bitcast(F32), ALU.subtract)
                    ins.then_inc(hl_ready, 1)
                    dve.wait_ge(rt_hi, 1)
                    TTn(w_rt_lo[:, :, :], w_rt[:, :, :], w_rt_hi[:, :, :].bitcast(F32), ALU.subtract).then_inc(rt_lo, 1)

                    wide = [P, TT, EXPERTS]
                    number = iota[:, 0:EXPERTS].unsqueeze(1).broadcast_to(wide)
                    logit, tmp, is1, rest, is2, sel, pos = (rt[:, n] for n in range(7))
                    m1, i1, m2, gap, e2, w1, w2 = (rs[:, n] for n in range(7))
                    dve.wait_ge(logits_sent, 1)
                    step(TTn(logit, ps[:, 2, 0:16].rearrange("p (t e) -> p t e", t=TT), b_rt[:, :].unsqueeze(1).broadcast_to(wide), ALU.add))

                    def largest(values, m, is_it):
                        step(RED(m, values, AX_X, ALU.max))
                        step(TTn(tmp, values, m.broadcast_to(wide), ALU.not_equal))
                        step(STT(tmp, tmp, 64.0, number, ALU.mult, ALU.add))
                        step(RED(i1, tmp, AX_X, ALU.min))
                        step(TTn(is_it, number, i1.broadcast_to(wide), ALU.is_equal))

                    largest(logit, m1, is1)
                    step(STT(rest, is1, -1e38, logit, ALU.mult, ALU.add))
                    largest(rest, m2, is2)
                    TTn(sel, is1, is2, ALU.add).then_inc(sel_ready, 1)
                    TTn(gap, m2, m1, ALU.subtract).then_inc(gap_ready, 1)
                    dve.wait_ge(e2_ready, 1)
                    step(TS(w2, e2, 1.0, None, ALU.add))
                    step(nc.vector.reciprocal(w1, w2))
                    step(TTn(w2, e2, w1, ALU.mult))
                    step(TTn(tmp, is1, w1.broadcast_to(wide), ALU.mult))
                    step(TTn(is2, is2, w2.broadcast_to(wide), ALU.mult))
                    step(TTn(wsel[:, :, :], tmp, is2, ALU.add))
                    dve.wait_ge(pos_sent, 1)
                    step(TS(pos, ps[:, 3, 0:16].rearrange("p (t e) -> p t e", t=TT), 1.0, None, ALU.add))
                    step(TTn(pos, pos, sel, ALU.mult))
                    step(TS(posm[:, :, :], pos, -1.0, None, ALU.add))
                    nc.vector.tensor_copy(counts_i[:, :], ps[:, 3, 16:24]).then_inc(counts_ready, 1)
                    dve.wait_ge(counts_ready, 1)
                    moe_loads = [0] * RING
                    dve.wait_ge(yacc_zero, 1)
                    with dve.Fori(0, EXPERTS) as e:
                        count = dve.value_load(counts_i[0:1, bass.ds(e, 1)], min_val=0, max_val=SEQ)

                        def expert(blocks):
                            for t in range(TT):
                                at = posm[:, t, bass.ds(e, 1)]
                                TS(pick[:, t, :], iota, at, None, ALU.is_equal)
                                ins = TS(pick_w[:, t, :], iota, at, wsel[:, t, bass.ds(e, 1)], ALU.is_equal, ALU.mult)
                            ins.then_inc(pick_ready, 1)
                            for b in range(blocks):
                                dve.wait_ge(gathered[b], e + 1)
                                nc.vector.tensor_copy(actT_lo[:, :, b * P:(b + 1) * P],
                                                      ps[:, 2:4, :].rearrange("p c (k q) -> p (c k) q", q=P)).then_inc(xg_lo_ready[b], 1)
                            swiglu(EXPERT, EXPERT_PANELS, moe_loads, e * EXPERT.n_split + (LAYER_SPLITS + MIX.n_split),
                                   0, 0, e * len(EXPERT_PANELS) + len(DENSE_PANELS), blocks)
                            dve.wait_ge(split_used, e * EXPERT.n_split + (LAYER_SPLITS + MIX.n_split + EXPERT.n_split + SPLIT))
                            for b in range(blocks):
                                ins = nc.vector.tensor_copy(hbuf[:, b, BANK:D], bank(5 + 2 * b))
                            ins.then_inc(y_dve, 1)
                            for t in range(TT):
                                for c in range(2):
                                    dve.wait_ge(scattered, e * 4 + 2 * t + c + 1)
                                    part = yacc[:, t, c * BANK:(c + 1) * BANK]
                                    TTn(part, part, bank(4 + 2 * t + c), ALU.add).then_inc(added, 1)

                        with dve.If(count > P):
                            expert(2)
                        with dve.Else():
                            dve.sem_inc(xg_lo_ready[1], 1)
                            expert(1)
                    dve.wait_ge(added, 4 * EXPERTS + 4)
                    post_norm(chain, 3, lambda t, c: yacc[:, t, c * BANK:(c + 1) * BANK], 128)
                    assert chain.n == DVE_ROUTE_STEPS, chain.n

        @block.tensor
        def _(pe):
            MM, TR = nc.tensor.matmul, nc.tensor.transpose

            def product(to, hi, lo, w_h, w_l, first, last):
                MM(to, hi, w_h, start=first, stop=False)
                MM(to, hi, w_l, start=False, stop=False)
                return MM(to, lo, w_h, start=False, stop=last)

            def split_piece(j, k, n, width):
                at = slice(k * width + n, k * width + n + min(width, BANK))
                return w_hi[:, j % SPLIT, at], w_lo[:, j % SPLIT, at]

            def pre_norm(sub):
                pe.wait_ge(x_ready, sub + 1)
                for q in range(6):
                    ins = MM(bank(q), ones, mod_acc[:, q * BANK:(q + 1) * BANK], start=True, stop=True)
                ins.then_inc(mod_sent, 1)
                for t in range(TT):
                    pe.wait_ge(h_ready, sub * TT + t + 1)
                    for k in range(KD):
                        ins = TR(ps[:, (6, 0)[t] + k // 4, (k % 4) * P:(k % 4 + 1) * P], hbuf[:, t, k * P:(k + 1) * P], ident)
                    ins.then_inc(hT_sent, 1)
                pe.wait_ge(hT_hi_ready, sub * 4 + 4)
                pe.wait_ge(hT_lo_ready, sub * 4 + 4)
                pe.wait_ge(mod_read, sub + 1)

            def transposed(t, first_bank, signal):
                for k in range(KD):
                    ins = TR(ps[:, first_bank + k // 4, (k % 4) * P:(k % 4 + 1) * P], hbuf[:, t, k * P:(k + 1) * P], ident)
                ins.then_inc(signal, 1)

            def chunk(k, t):
                return actT_hi[:, k, t * P:(t + 1) * P], actT_lo[:, k, t * P:(t + 1) * P]

            pe.wait_ge(cst_loaded, 16)
            with pe.Fori(0, DEPTH) as layer:
                pbase = layer * LAYER_PIECES + MOD0.n
                pe.wait_ge(piece_used, pbase + RING)
                pre_norm(layer * 2)

                def project(j, n, h, width=BANK):
                    ks = range(4 * h, 4 * h + 4) if width == BANK else range(KD)
                    for t in range(TT):
                        for k in ks:
                            w = split_piece(j, k - ks[0], 0, width)
                            ins = product(bank(2 * (n % 2) + t, width), *chunk(k, t), *w, k == 0, k == KD - 1)
                    ins.then_inc(split_used, 1)

                def stick_scores():
                    pe.wait_ge(aT_ready, layer * 2 + 2)
                    for h in range(SB_HEADS):
                        par, pair = h % 2, h // 2
                        rows = slice(par * HD, (par + 1) * HD)
                        MM(ps[:, 4 + par, pair * SEQ:(pair + 1) * SEQ], aT[rows, 2 + pair, 0:P], aT[rows, pair, :], start=True, stop=True)
                        ins = MM(ps[:, 6 + par, pair * P:(pair + 1) * P], aT[rows, 2 + pair, P:SEQ], aT[rows, pair, P:SEQ], start=True, stop=True)
                    ins.then_inc(z_sent, 1)

                def suffix_sums():
                    pe.wait_ge(soft_ready, layer + 1)
                    for par in range(2):
                        MM(bank(4 + par), tri, soft[:, par * BANK:(par + 1) * BANK], start=True, stop=False)
                        MM(bank(4 + par).rearrange("p (a q) -> p a q", q=SEQ)[:, :, P:SEQ], ones,
                           soft[:, 1024 + par * SEQ:1024 + (par + 1) * SEQ].rearrange("p (a q) -> p a q", q=P), start=False, stop=True)
                    MM(bank(6), tri, soft[:, 1024:1536], start=True, stop=True).then_inc(suffix_sent, 1)

                def stick_values():
                    pe.wait_ge(w_ready, layer + 1)
                    for h in range(SB_HEADS):
                        par, pair = h % 2, h // 2
                        rows = slice(par * HD, (par + 1) * HD)
                        v = slice(VA + h * HD, VA + (h + 1) * HD)
                        w0 = z[:, (2 * par + pair) * SEQ:(2 * par + pair + 1) * SEQ]
                        w1 = z[:, 1024 + (2 * par + pair) * P:1024 + (2 * par + pair + 1) * P]
                        MM(ps[rows, 7, pair * SEQ:(pair + 1) * SEQ], proj[:, 0, v], w0, start=True, stop=False)
                        ins = MM(ps[rows, 7, pair * SEQ + P:(pair + 1) * SEQ], proj[:, 1, v], w1, start=False, stop=True)
                    ins.then_inc(ya_sent, 1)

                def pool_windows():
                    pe.wait_ge(ya_ready, layer + 1)
                    for g in range(len(WINDOWS)):
                        rows = slice((g % 2) * HD, (g % 2 + 1) * HD)
                        u = slice(UB + g * HD, UB + (g + 1) * HD)
                        at, band = (g // 2) * SEQ, C_BAND + g * BAND_W
                        MM(ps[rows, 7, at:at + P], proj[:, 0, u], cst[:, band:band + P], start=True, stop=True)
                        MM(ps[rows, 7, at + P:at + 2 * P], proj[:, 1, u], cst[:, band + P:band + 2 * P], start=True, stop=False)
                        ins = MM(ps[rows, 7, at + P:at + P + SPILL], proj[:, 0, u], cst[:, band + 2 * P:band + BAND_W], start=False, stop=True)
                    ins.then_inc(pool_sent, 1)

                def pool_mix():
                    for g in range(len(WINDOWS)):
                        rows = slice((g % 2) * HD, (g % 2 + 1) * HD)
                        at = (g // 2) * SEQ
                        ins = MM(ps[rows, 7, at:at + SEQ], w_pool[rows, g // 2, :], proj[rows, g // 2, QA:KA], start=True, stop=True)
                    ins.then_inc(yb_sent, 1)

                def band_scores(t):
                    for h in range(Q_HEADS):
                        par, i, g = h % 2, h // 2, h // (Q_HEADS // KV_HEADS)
                        rows = slice(par * HD, (par + 1) * HD)
                        q0 = t * P
                        key = lambda c: cT[rows, 4 + g, c * CHUNK:(c + 1) * CHUNK]
                        before = 2 * t - 1 if t else 1
                        MM(ps[:, 4 + par, i * P:i * P + CHUNK], cT[rows, i, q0:q0 + P], key(2 * t), start=True, stop=True)
                        MM(ps[0:CHUNK, 4 + par, i * P + CHUNK:(i + 1) * P], cT[rows, i, q0:q0 + CHUNK], key(before), start=True, stop=True)
                        ins = MM(ps[CHUNK:P, 4 + par, i * P + CHUNK:(i + 1) * P], cT[rows, i, q0 + CHUNK:q0 + P], key(2 * t + 1), start=True, stop=True)
                    ins.then_inc(sc_sent, 1)

                def turn_probs(t):
                    pe.wait_ge(prob_ready, layer * 2 + t + 1)
                    for n in range(Q_HEADS):
                        ins = TR(ps[:, 4 + n // 4, (n % 4) * P:(n % 4 + 1) * P], scores[:, n, :], ident)
                    ins.then_inc(pT_sent, 1)

                def band_values(t):
                    pe.wait_ge(pT_ready, layer * 2 + t + 1)
                    pe.wait_ge(v_ready, layer + 1)
                    if t:
                        pe.wait_ge(yc_ready, layer * 2 + 1)
                    for par in range(2):
                        for g in range(KV_HEADS):
                            for odd in range(2):
                                v = v_even[:, :] if t and not odd else proj[:, t, VC:PROJ]
                                qs = slice(odd * CHUNK, (odd + 1) * CHUNK)
                                to = ps[par * HD:(par + 1) * HD, 6, 2 * g * P:(2 * g + 2) * P].rearrange("p (i q) -> p i q", q=P)
                                ins = MM(to[:, :, qs], v[:, g * HD:(g + 1) * HD], probT[:, 4 * par + 2 * g:4 * par + 2 * g + 2, qs],
                                         start=True, stop=True)
                    ins.then_inc(yc_sent, 1)

                def after(j):
                    if j == 3:
                        pe.wait_ge(proj_ready, layer * 8 + 2)
                        for c in range(4):
                            for t in range(TT):
                                ins = TR(ps[:, 4 + c // 2, (c % 2) * SEQ + t * P:(c % 2) * SEQ + (t + 1) * P], proj[:, t, c * P:(c + 1) * P], ident)
                        ins.then_inc(aT_sent, 1)
                    if j == 5:
                        stick_scores()
                    if j == 8:
                        suffix_sums()
                    if j == 10:
                        pe.wait_ge(rope_ready, layer * 2 + 2)
                        pe.wait_ge(logw_ready, layer + 1)
                        for c in range(6):
                            for t in range(TT):
                                ins = TR(ps[:, 4 + c // 2, (c % 2) * SEQ + t * P:(c % 2) * SEQ + (t + 1) * P], proj[:, t, QC + c * P:QC + (c + 1) * P], ident)
                        ins.then_inc(cT_sent, 1)
                    if j == 11:
                        stick_values()
                    if j == 12:
                        pe.wait_ge(cT_ready, layer * 3 + 3)
                        band_scores(0)
                        pool_windows()
                    if j == 13:
                        pool_mix()
                    if j == 14:
                        turn_probs(0)
                    if j == 15:
                        band_values(0)
                        band_scores(1)
                    if j == 17:
                        turn_probs(1)
                    if j == 18:
                        band_values(1)

                for i, piece in enumerate(MIX.pieces):
                    if piece[0] == "mod":
                        continue
                    j = MIX.split_no[i]
                    kind, n, h = piece
                    pe.wait_ge(piece_used, pbase + i + 1 + RING)
                    if kind == "in":
                        if n >= 2 and h == 0:
                            pe.wait_ge(proj_ready, layer * 8 + 2 * (n - 1))
                        project(j, n, h, BANK if n < 3 else BANK // 2)
                    elif kind == "gate":
                        if j == 13:
                            pe.wait_ge(small_loaded, layer * 64 + 64)
                            pe.wait_ge(pooled_ready, layer + 1)
                        if h == 0:
                            if n < 2:
                                pe.wait_ge(proj_ready, layer * 8 + 6 + 2 * n)
                            else:
                                pe.wait_ge(gate_ready, layer * 12 + 2 * (n - 1))
                        project(j, n, h)
                    elif kind == "branch":
                        where = {0: (0, 2, 4), 1: (6, 0, 2)}[n]
                        if j == 19:
                            pe.wait_ge(yT_hi_ready, layer * 2 + 2)
                            pe.wait_ge(yT_lo_ready, layer * 2 + 2)
                            pe.wait_ge(gate_ready, layer * 12 + 12)
                        groups = [(0, (0, 1)), (1, (2, 3))] if h == 0 else [(2, (4, 5, 6, 7))]
                        for br, ks in groups:
                            if n == 1 and br == 1:
                                pe.wait_ge(merged_ready, layer * 4 + 2)
                            for t in range(TT):
                                for k in ks:
                                    ins = product(bank(where[br] + t), *chunk(k, t), *split_piece(j, k % 4, 0, BANK), k == ks[0], k == ks[-1])
                        ins.then_inc(split_used, 1)
                    else:
                        if j == 23:
                            for t in range(TT):
                                pe.wait_ge(merged_ready, layer * 4 + 4)
                                transposed(t, 4 + 2 * t, mT_sent)
                            pe.wait_ge(mT_hi_ready, layer * 4 + 4)
                            pe.wait_ge(mT_lo_ready, layer * 4 + 4)
                        for t in range(TT):
                            for k in range(4 * h, 4 * h + 4):
                                ins = product(bank(2 * t + n), *chunk(k, t), *split_piece(j, k % 4, 0, BANK), k == 0, k == KD - 1)
                        ins.then_inc(split_used, 1)
                    after(j)

                def swiglu(stretch, panels, piece_base, panel0, blocks):
                    def turn(p):
                        pe.wait_ge(gated_ready, panel0 + p + 1)
                        for b in range(blocks):
                            for c in range(panels[p] // P):
                                ins = TR(ps[:, b, c * P:(c + 1) * P], gated[:, b, c * P:(c + 1) * P], ident)
                        ins.then_inc(gT_sent, 1)

                    for i, (kind, p, *rest) in enumerate(stretch.pieces):
                        if kind == "mod":
                            continue
                        j, h = stretch.split_no[i], rest[0]
                        width = panels[p]
                        pe.wait_ge(piece_used, piece_base + i + 1 + RING)
                        if kind in "AB":
                            if kind == "A" and p == 1 and h == 0:
                                pe.wait_ge(silu_ready, panel0 + 1)
                            if kind == "B" and p and h == 0:
                                pe.wait_ge(gated_ready, panel0 + p)
                            ks = range(4 * h, 4 * h + 4) if width == BANK else range(KD)
                            for b in range(blocks):
                                for k in ks:
                                    ins = product(bank((0, 2)[kind == "B"] + b, width), *chunk(k, b), *split_piece(j, k - ks[0], 0, width),
                                                  k == 0, k == KD - 1)
                            ins.then_inc(split_used, 1)
                            if kind == "B" and h == 0 and p:
                                pe.wait_ge(silu_ready, panel0 + p + 1)
                                turn(p - 1)
                        else:
                            if h == 0:
                                pe.wait_ge(gT_hi_ready, panel0 + p + 1)
                                pe.wait_ge(gT_lo_ready, panel0 + p + 1)
                            chunks = width // P
                            for b in range(blocks):
                                for c in range(2):
                                    k = 2 * h + c
                                    for n in range(2):
                                        ins = product(bank(4 + 2 * b + n), gT_hi[:, b, k, :], gT_lo[:, b, k, :],
                                                      *split_piece(j, c, n * BANK, D), p == 0 and k == 0,
                                                      p == len(panels) - 1 and k == chunks - 1)
                            ins.then_inc(split_used, 1)
                            if p == len(panels) - 2 and h == chunks // 2 - 1:
                                turn(p + 1)

                with pe.If(layer < 1):
                    pre_norm(1)
                    swiglu(DENSE, DENSE_PANELS, MOD0.n + MIX.n, 0, 2)
                with pe.Else():
                    pre_norm(3)
                    pe.wait_ge(rt_lo, 1)
                    for t in range(TT):
                        for k in range(KD):
                            ins = product(ps[:, 2, t * EXPERTS:(t + 1) * EXPERTS], *chunk(k, t), w_rt_hi[:, k, :], w_rt_lo[:, k, :], k == 0, k == KD - 1)
                    ins.then_inc(logits_sent, 1)
                    pe.wait_ge(sel_ready, 1)
                    sel = rt[:, 5]
                    to = ps[:, 3, :]
                    MM(to[:, 0:8], past, sel[:, 0, :], start=True, stop=True)
                    MM(to[:, 8:16], past, sel[:, 1, :], start=True, stop=False)
                    MM(to[:, 8:16], ones, sel[:, 0, :], start=False, stop=True)
                    MM(to[:, 16:24], ones, sel[:, 0, :], start=True, stop=False)
                    MM(to[:, 16:24], ones, sel[:, 1, :], start=False, stop=True).then_inc(pos_sent, 1)
                    pe.wait_ge(hh_ready, 1)
                    pe.wait_ge(hl_ready, 1)
                    pe.wait_ge(counts_ready, 1)
                    with pe.Fori(0, EXPERTS) as e:
                        count = pe.value_load(counts_i[0:1, bass.ds(e, 1)], min_val=0, max_val=SEQ)

                        def expert(blocks):
                            pe.wait_ge(pick_ready, e + 1)
                            for b in range(blocks):
                                if b:
                                    pe.wait_ge(xg_hi_ready[0], e + 1)
                                    pe.wait_ge(xg_lo_ready[0], e + 1)
                                for part, first_bank in ((h_hi, 0), (h_lo, 2)):
                                    for k in range(KD):
                                        to = ps[:, first_bank + k // 4, (k % 4) * P:(k % 4 + 1) * P]
                                        for t in range(TT):
                                            ins = MM(to, part[:, t, k * P:(k + 1) * P], pick[:, t, b * P:(b + 1) * P], start=t == 0, stop=t == 1)
                                ins.then_inc(gathered[b], 1)
                            pe.wait_ge(added, e * 4 + 4)
                            for b in range(blocks):
                                for t in range(TT):
                                    ins = TR(ps[:, 4, b * SEQ + t * P:b * SEQ + (t + 1) * P], pick_w[:, t, b * P:(b + 1) * P], ident)
                            ins.then_inc(place_sent, 1)
                            pe.wait_ge(place_ready, e + 1)
                            for b in range(blocks):
                                pe.wait_ge(xg_hi_ready[b], e + 1)
                                pe.wait_ge(xg_lo_ready[b], e + 1)
                            swiglu(EXPERT, EXPERT_PANELS, e * EXPERT.n + (MOD0.n + LAYER_PIECES + MIX.n),
                                   e * len(EXPERT_PANELS) + len(DENSE_PANELS), blocks)
                            pe.wait_ge(y_act, e + 1)
                            pe.wait_ge(y_dve, e + 1)
                            for t in range(TT):
                                for c in range(2):
                                    for b in range(blocks):
                                        ins = MM(bank(4 + 2 * t + c), place[:, b, t * P:(t + 1) * P], hbuf[:, b, c * BANK:(c + 1) * BANK],
                                                 start=b == 0, stop=b == blocks - 1)
                                    ins.then_inc(scattered, 1)

                        with pe.If(count > P):
                            expert(2)
                        with pe.Else():
                            pe.sem_inc(gathered[1], 1)
                            expert(1)


_INS = ['x', 'c', 'w_mod_mix', 'b_mod_mix', 'w_in', 'w_pool', 'pool_scale', 'sinks', 'w_gate', 'w_branch_a',
        'w_branch_b', 'w_branch_c', 'w_out', 'ln_mix_g', 'ln_mix_b', 'w_mod_ffn', 'b_mod_ffn', 'ffn_w1', 'ffn_w3',
        'ffn_w2', 'w_router', 'b_router', 'exp_w1', 'exp_w3', 'exp_w2', 'ln_ffn_g', 'ln_ffn_b']


def kernel(**inputs):
    import numpy as _np
    import concourse.bacc as _bacc
    from concourse import mybir as _mybir
    from concourse.bass_utils import run_bass_kernel_spmd as _run

    nc = _bacc.Bacc("TRN2", target_bir_lowering=False, num_devices=1)
    arrays, args = {}, {}
    for name in _INS:
        a = _np.ascontiguousarray(inputs[name])
        arrays[f"in_{name}_dram"] = a
        args[name] = nc.dram_tensor(f"in_{name}_dram", a.shape, _mybir.dt.from_np(a.dtype), kind="ExternalInput").ap()
    table = constants()
    arrays["constants_dram"] = table
    consts = nc.dram_tensor("constants_dram", table.shape, _mybir.dt.float32, kind="ExternalInput").ap()
    out = nc.dram_tensor("out_dram", (1, SEQ, D), _mybir.dt.float32, kind="ExternalOutput").ap()
    trunk(nc, args, consts, out)
    r = _run(nc, [arrays], core_ids=[0])
    return r.results[0]["out_dram"]
```

```python
from contextlib import ExitStack

import numpy as np

import concourse.bass as bass
from concourse import mybir

F32 = mybir.dt.float32
F32R = mybir.dt.float32r
I32 = mybir.dt.int32
ALU = mybir.AluOpType
ACT = mybir.ActivationFunctionType
AX_X = mybir.AxisListType.X

P = 128
D = 1024
KD = D // P
SEQ = 256
TT = SEQ // P
DEPTH = 2
HD = 64
HALF = HD // 2
SB_HEADS = 4
WINDOWS = (2, 4, 8, 16)
Q_HEADS, KV_HEADS = 8, 2
CHUNK = 64
D_FF, D_FFE, EXPERTS = 2816, 3584, 8
EPS = 1e-5
ALPHA = (2 * DEPTH) ** 0.25
SCALE = HD ** -0.5
FAR = -1e30
BANK = 512

QA, KA, VA, UB, QC, KC, VC = 0, 256, 512, 768, 1024, 1536, 1792
PROJ = 1920

SPILL = WINDOWS[-1]
BAND_W = 2 * P + SPILL
C_IDENT, C_ONES, C_PAST, C_TRI = 0, P, 2 * P, 3 * P
C_BAND = 4 * P
C_COS = C_BAND + len(WINDOWS) * BAND_W
C_SIN = C_COS + TT * HD
C_SWM = C_SIN + TT * HD
C_IOTA = C_SWM + P
CONSTS = C_IOTA + SEQ


def constants():
    c = np.zeros((P, CONSTS), np.float32)
    i = np.arange(P)
    c[:, C_IDENT:C_IDENT + P] = np.eye(P)
    c[:, C_ONES:C_ONES + P] = 1.0
    c[:, C_PAST:C_PAST + P] = i[:, None] < i[None, :]
    c[:, C_TRI:C_TRI + P] = i[:, None] >= i[None, :]
    j, s = np.arange(P)[:, None], np.arange(SEQ)[None, :]
    for g, w in enumerate(WINDOWS):
        own = ((s - j >= 0) & (s - j < w)) / np.minimum(s + 1.0, w)
        full = ((s - j >= 0) & (s - j < w)) / float(w)
        base = C_BAND + g * BAND_W
        c[:, base:base + P] = own[:, :P] - np.eye(P)
        c[:, base + P:base + 2 * P] = full[:, :P] - np.eye(P)
        c[:, base + 2 * P:base + BAND_W] = full[:, P:P + SPILL]
    inv = np.power(np.float32(10000.0), -np.arange(HALF, dtype=np.float32) / np.float32(HALF)).astype(np.float32)
    for t in range(TT):
        ang = (np.arange(P) + t * P).astype(np.float32)[:, None] * inv[None, :]
        cos, sin = np.cos(ang), np.sin(ang)
        c[:, C_COS + t * HD:C_COS + (t + 1) * HD] = np.concatenate([cos, cos], 1)
        c[:, C_SIN + t * HD:C_SIN + (t + 1) * HD] = np.concatenate([-sin, sin], 1)
    c[:HD, C_SWM + HD:C_SWM + P] = FAR
    c[:, C_IOTA:C_IOTA + SEQ] = np.arange(SEQ)
    return c


RING, SPLIT = 6, 3
PIECE = 2048
IN_PANELS = 4
GATE_PANELS = 3 * D // BANK
MODS = 12


def mod_stream():
    return [("mod", q) for q in range(MODS)]


def mix_stream():
    s = [("in", n, h) for n in range(3) for h in range(2)] + [("in", 3, 0)]
    for q in range(2 * GATE_PANELS):
        s += [("gate", q // 2, q % 2), ("mod", q)]
    s += [("branch", n, h) for h in range(2) for n in range(2)]
    s += [("out", n, h) for h in range(2) for n in range(2)]
    return s


def ffn_stream(width, mods):
    panels = [min(BANK, width - n) for n in range(0, width, BANK)]
    s = []
    for p, w in enumerate(panels):
        halves = w // (BANK // 2)
        s += [("A", p, h) for h in range(halves)] + [("B", p, h) for h in range(halves)]
        if p:
            s += [("C", p - 1, h) for h in range(2)]
    s += [("C", len(panels) - 1, h) for h in range(panels[-1] // (BANK // 2))]
    if mods:
        for q in reversed(range(MODS)):
            s.insert(2 * q + 5, ("mod", q))
    return panels, s


class Stretch:

    def __init__(self, pieces):
        self.pieces = pieces
        self.loads, self.split_no = [], []
        landed, n = [0] * RING, 0
        for i, piece in enumerate(pieces):
            landed[i % RING] += 32 if piece[0] == "branch" and piece[2] == 0 else 16
            self.loads.append(landed[i % RING])
            self.split_no.append(None if piece[0] == "mod" else n)
            n += piece[0] != "mod"
        self.landed, self.n_split, self.n = landed, n, len(pieces)
        assert n % SPLIT == 0


MOD0 = Stretch(mod_stream())
MIX = Stretch(mix_stream())
DENSE_PANELS, _dense = ffn_stream(D_FF, True)
DENSE = Stretch(_dense)
EXPERT_PANELS, _expert = ffn_stream(D_FFE, False)
EXPERT = Stretch(_expert)
assert EXPERT.n % RING == 0
LAYER_PIECES = MIX.n + DENSE.n
LAYER_SPLITS = MIX.n_split + DENSE.n_split

BRANCH_ORDER = [(0, 0), (1, 0), (1, 1), (0, 1), (2, 0), (2, 1)]
HW1, HW3 = 4, 5
ROUTE = 0

DVE_MIX_STEPS, DVE_DENSE_STEPS, DVE_ROUTE_STEPS = 40, 22, 33
ACT_MIX_STEPS = 2


class Chain:

    def __init__(self, eng, sem, base=0):
        self.eng, self.sem, self.base, self.n = eng, sem, base, 0

    def step(self, ins):
        ins.then_inc(self.sem, 1)
        self.n += 1
        self.eng.wait_ge(self.sem, self.base + self.n)


def trunk(nc, I, consts, out):
    with ExitStack() as ctx:
        def sb(name, shape, dt=F32, scope=ctx):
            return scope.enter_context(nc.sbuf_tensor(name, shape, dt))

        def sem(name):
            return ctx.enter_context(nc.semaphore(name))

        w_raw = sb("w_raw", [P, RING, PIECE])
        w_hi = sb("w_hi", [P, SPLIT, PIECE], F32R)
        w_lo = sb("w_lo", [P, SPLIT, PIECE], F32R)
        x = sb("x_sb", [P, TT, D])
        hbuf = sb("hbuf", [P, TT, D])
        actT_hi = sb("actT_hi", [P, KD, SEQ], F32R)
        actT_lo = sb("actT_lo", [P, KD, SEQ], F32R)
        cst = sb("cst", [P, CONSTS])
        mod_acc = sb("mod_acc", [P, 3 * D])
        gate1 = sb("gate1", [P, D])
        c_act = sb("c_act", [P, KD])
        stats = sb("stats", [P, TT, 2, 6])
        mv = sb("mv", [P, TT, 2])
        veps = sb("veps", [P, TT])
        std = sb("std", [P, TT])
        rstd = sb("rstd", [P, TT])
        small = sb("small", [P, 64])
        sinks = sb("sinks_sb", [P, Q_HEADS])
        pool_scale = sb("pool_scale_sb", [P, 2])
        counts_i = sb("counts_i", [P, EXPERTS + 1], I32)

        mix = ExitStack()
        lnrow = sb("lnrow", [P, 2, D], scope=mix)
        mix.close()
        cT = sb("cT", [P, 6, SEQ], scope=mix)
        scores = sb("scores", [P, Q_HEADS, P], scope=mix)
        probT = sb("probT", [P, Q_HEADS, P], scope=mix)
        proj = sb("proj", [P, TT, PROJ], scope=mix)
        gates = sb("gates", [P, TT, 3 * D], scope=mix)
        w_pool = sb("w_pool_sb", [P, 2, HD], scope=mix)
        v_even = sb("v_even", [P, P], scope=mix)
        mix.close()
        aT = sb("aT", [P, 4, SEQ], scope=mix)
        z = sb("z_sb", [P, 1536], scope=mix)
        mix.close()
        soft = hbuf[:, :, :].rearrange("p t d -> p (t d)")[:, 0:1536]
        yT = hbuf[:, :, :].rearrange("p t d -> p (t d)").rearrange("p (k q) -> p k q", k=KD)
        ffn = ExitStack()
        h_hi = sb("h_hi", [P, TT, D], F32R, scope=ffn)
        h_lo = sb("h_lo", [P, TT, D], F32R, scope=ffn)
        yacc = sb("yacc", [P, TT, D], scope=ffn)
        silu = sb("silu", [P, 2, BANK], scope=ffn)
        gated = sb("gated", [P, 2, BANK], scope=ffn)
        gT_hi = sb("gT_hi", [P, 2, 4, P], F32R, scope=ffn)
        gT_lo = sb("gT_lo", [P, 2, 4, P], F32R, scope=ffn)
        pick = sb("pick", [P, TT, SEQ], F32R, scope=ffn)
        pick_w = sb("pick_w", [P, TT, SEQ], scope=ffn)
        place = sb("place", [P, 2, SEQ], scope=ffn)
        w_rt = sb("w_rt", [P, KD, EXPERTS], scope=ffn)
        w_rt_hi = sb("w_rt_hi", [P, KD, EXPERTS], F32R, scope=ffn)
        w_rt_lo = sb("w_rt_lo", [P, KD, EXPERTS], F32R, scope=ffn)
        b_rt = sb("b_rt", [P, EXPERTS], scope=ffn)
        rt = sb("rt", [P, 8, TT, EXPERTS], scope=ffn)
        rs = sb("rs", [P, 8, TT, 1], scope=ffn)
        posm = sb("posm", [P, TT, EXPERTS + 1], scope=ffn)
        wsel = sb("wsel", [P, TT, EXPERTS + 1], scope=ffn)
        ffn.close()

        ps = ctx.enter_context(nc.psum_tensor("ps", [P, 8, BANK], F32))

        ident = cst[:, C_IDENT:C_IDENT + P]
        ones = cst[:, C_ONES:C_ONES + P]
        past = cst[:, C_PAST:C_PAST + P]
        tri = cst[:, C_TRI:C_TRI + P]
        iota = cst[:, C_IOTA:C_IOTA + SEQ]
        sw_mask = cst[:, C_SWM:C_SWM + P]

        raw_loaded = [sem(f"raw_loaded{i}") for i in range(RING)]
        piece_used = sem("piece_used")
        split_hi = sem("split_hi")
        split_used = sem("split_used")
        mod_step = sem("mod_step")
        acc_ready = sem("acc_ready")
        x_loaded, c_loaded, cst_loaded = sem("x_loaded"), sem("c_loaded"), sem("cst_loaded")
        small_loaded, ln_loaded, rt_loaded = sem("small_loaded"), sem("ln_loaded"), sem("rt_loaded")
        acc_free, acc_zero, yacc_zero = sem("acc_free"), sem("acc_zero"), sem("yacc_zero")
        c_ready = sem("c_ready")
        out_stored = sem("out_stored")
        var_ready, std_ready = sem("var_ready"), sem("std_ready")
        mod_sent = sem("mod_sent")
        gate_sent, scale_ready, gate1_ready = sem("gate_sent"), sem("scale_ready"), sem("gate1_ready")
        h_ready, hT_sent, hT_hi_ready, hT_lo_ready = sem("h_ready"), sem("hT_sent"), sem("hT_hi_ready"), sem("hT_lo_ready")
        x_ready = sem("x_ready")
        dve_start, dve_mix, dve_ffn, act_mix = sem("dve_start"), sem("dve_mix"), sem("dve_ffn"), sem("act_mix")
        proj_ready, aT_sent, aT_ready = sem("proj_ready"), sem("aT_sent"), sem("aT_ready")
        z_sent, z_ready, softplus_ready, soft_ready = sem("z_sent"), sem("z_ready"), sem("softplus_ready"), sem("soft_ready")
        suffix_sent, logw_ready, expw_ready, w_ready = sem("suffix_sent"), sem("logw_ready"), sem("expw_ready"), sem("w_ready")
        ya_sent, ya_ready = sem("ya_sent"), sem("ya_ready")
        rope_ready, cT_sent, cT_ready = sem("rope_ready"), sem("cT_sent"), sem("cT_ready")
        pool_sent, pooled_ready, yb_sent, yb_ready = sem("pool_sent"), sem("pooled_ready"), sem("yb_sent"), sem("yb_ready")
        sc_sent, sc_ready, exp_ready, prob_ready = sem("sc_sent"), sem("sc_ready"), sem("exp_ready"), sem("prob_ready")
        pT_sent, pT_ready, yc_sent, yc_ready = sem("pT_sent"), sem("pT_ready"), sem("yc_sent"), sem("yc_ready")
        v_ready, gate_ready = sem("v_ready"), sem("gate_ready")
        branch_read, out_sent = sem("branch_read"), sem("out_sent")
        yT_hi_ready, yT_lo_ready = sem("yT_hi_ready"), sem("yT_lo_ready")
        merged_ready, mT_sent, mT_hi_ready, mT_lo_ready = sem("merged_ready"), sem("mT_sent"), sem("mT_hi_ready"), sem("mT_lo_ready")
        silu_ready, gated_ready = sem("silu_ready"), sem("gated_ready")
        gT_sent, gT_hi_ready, gT_lo_ready = sem("gT_sent"), sem("gT_hi_ready"), sem("gT_lo_ready")
        hh_ready, hl_ready, rt_hi, rt_lo = sem("hh_ready"), sem("hl_ready"), sem("rt_hi"), sem("rt_lo")
        logits_sent, gap_ready, e2_ready, sel_ready = sem("logits_sent"), sem("gap_ready"), sem("e2_ready"), sem("sel_ready")
        pos_sent, counts_ready = sem("pos_sent"), sem("counts_ready")
        pick_ready, place_sent, place_ready = sem("pick_ready"), sem("place_sent"), sem("place_ready")
        gathered = [sem(f"gathered{b}") for b in range(2)]
        xg_hi_ready = [sem(f"xg_hi_ready{b}") for b in range(2)]
        xg_lo_ready = [sem(f"xg_lo_ready{b}") for b in range(2)]
        y_act, y_dve, scattered, added = sem("y_act"), sem("y_dve"), sem("scattered"), sem("added")

        block = ctx.enter_context(nc.Block())

        def weight_rows(w):
            return w.rearrange("(k p) n -> p k n", p=P)

        def bank(b, n=BANK):
            return ps[:, b, 0:n]

        @block.sync
        def _(sp):
            sp.sem_inc(piece_used, RING)
            sp.sem_inc(split_used, SPLIT)

            def load(slot, piece, layer, expert=None):
                kind, a, h = piece[0], piece[1], piece[-1]
                dst = w_raw[:, slot, :]
                d4, d8 = dst.rearrange("p (k n) -> p k n", k=4), dst.rearrange("p (k n) -> p k n", k=8)
                d2 = dst.rearrange("p (k n) -> p k n", k=2)
                if kind == "mod":
                    w = I["w_mod_ffn"] if layer[0] == "ffn" else I["w_mod_mix"]
                    src = weight_rows(w[layer[1]])
                    pairs = [(d2, src[:, 2 * (a % 4):2 * (a % 4) + 2, D * (a // 4):D * (a // 4 + 1)])]
                elif kind == "branch":
                    cols = slice(a * BANK, (a + 1) * BANK)
                    if h == 0:
                        pairs = [(d4[:, 0:2, :], weight_rows(I["w_branch_a"][layer])[:, :, cols]),
                                 (d4[:, 2:4, :], weight_rows(I["w_branch_b"][layer])[:, :, cols])]
                    else:
                        pairs = [(d4, weight_rows(I["w_branch_c"][layer])[:, :, cols])]
                elif kind == "C":
                    w = I["ffn_w2"][0] if expert is None else I["exp_w2"][0, expert]
                    pairs = [(d2, weight_rows(w)[:, 4 * a + 2 * h:4 * a + 2 * h + 2, :])]
                else:
                    w = {"in": lambda: I["w_in"][layer], "gate": lambda: I["w_gate"][layer],
                         "out": lambda: I["w_out"][layer],
                         "A": lambda: I["ffn_w1"][0] if expert is None else I["exp_w1"][0, expert],
                         "B": lambda: I["ffn_w3"][0] if expert is None else I["exp_w3"][0, expert]}[kind]()
                    width = w.shape[-1]
                    c0, c1 = a * BANK, min((a + 1) * BANK, width)
                    if c1 - c0 == BANK:
                        pairs = [(d4, weight_rows(w)[:, 4 * h:4 * h + 4, c0:c1])]
                    else:
                        pairs = [(d8, weight_rows(w)[:, :, c0:c1])]
                for d, s in pairs:
                    sp.dma_start(d, s).then_inc(raw_loaded[slot], 16)

            def stream(stretch, base, layer, expert=None, mod_layer=None, gap=True):
                for i, piece in enumerate(stretch.pieces):
                    if i < RING:
                        before = base - RING + i + 1 if not gap or i >= RING // 2 else base - RING // 2 + i + 1
                    else:
                        before = base + i - RING + 1
                    sp.wait_ge(piece_used, before + RING)
                    load(i % RING, piece, mod_layer if piece[0] == "mod" else layer, expert)

            sp.dma_start(c_act[:, :], I["c"].rearrange("b (k p) -> p (b k)", p=P),
                         allow_slow_non_contiguous=True).then_inc(c_loaded, 16)
            xv = I["x"].rearrange("b (t p) d -> p (b t) d", p=P)
            sp.dma_start(x[:, :, :], xv).then_inc(x_loaded, 16)
            sp.dma_start(cst[:, :], consts).then_inc(cst_loaded, 16)
            stream(MOD0, 0, None, mod_layer=("mix", 0), gap=False)
            with sp.Fori(0, DEPTH) as layer:
                stream(MIX, layer * LAYER_PIECES + MOD0.n, layer, mod_layer=("ffn", layer))
                with sp.If(layer < 1):
                    stream(DENSE, MOD0.n + MIX.n, 0, mod_layer=("mix", 1))
                with sp.Else():
                    moe0 = MOD0.n + LAYER_PIECES + MIX.n
                    sp.wait_ge(piece_used, moe0 + RING)
                    with sp.Fori(0, EXPERTS) as e:
                        stream(EXPERT, e * EXPERT.n + moe0, 1, expert=e, gap=False)
            sp.wait_ge(x_ready, 2 * DEPTH + 2)
            sp.dma_start(out.rearrange("b (t p) d -> p (b t) d", p=P), x[:, :, :]).then_inc(out_stored, 16)
            sp.wait_ge(out_stored, 16)

        @block.gpsimd
        def _(gp):
            def fresh_acc(bias_row, n):
                nc.gpsimd.memset(mod_acc[:, :], 0.0).then_inc(acc_zero, 1)
                gp.wait_ge(acc_zero, n + 1)
                gp.dma_start(mod_acc[0:1, :], bias_row).then_inc(acc_ready, 16)

            def ln_rows(g, b):
                gp.dma_start(lnrow[:, 0, :], g.partition_broadcast(P)).then_inc(ln_loaded, 16)
                gp.dma_start(lnrow[:, 1, :], b.partition_broadcast(P)).then_inc(ln_loaded, 16)

            fresh_acc(I["b_mod_mix"][0:1, :], 0)
            with gp.Fori(0, DEPTH) as layer:
                gp.wait_ge(gate1_ready, layer * 2 + 1)
                gp.dma_start(sinks[:, :], I["sinks"][bass.ds(layer, 1), :].rearrange("a h -> (a h)").partition_broadcast(P)).then_inc(small_loaded, 16)
                gp.dma_start(pool_scale[:, :], I["pool_scale"][bass.ds(layer, 1), :].rearrange("a (k p) -> p (a k)", p=P),
                             allow_slow_non_contiguous=True).then_inc(small_loaded, 16)
                for par in range(2):
                    gp.dma_start(w_pool[par * HD:(par + 1) * HD, :, :],
                                 I["w_pool"][bass.ds(layer, 1)].rearrange("a (k r) c e -> c r (a k) e", r=2)[:, par],
                                 ).then_inc(small_loaded, 16)
                gp.wait_ge(gate_sent, layer * 2 + 1)
                gp.sem_inc(acc_free, 1)
                fresh_acc(I["b_mod_ffn"][bass.ds(layer, 1), :], layer * 2 + 1)
                gp.wait_ge(merged_ready, layer * 4 + 4)
                ln_rows(I["ln_mix_g"][bass.ds(layer, 1), :].rearrange("a d -> (a d)"),
                        I["ln_mix_b"][bass.ds(layer, 1), :].rearrange("a d -> (a d)"))
                with gp.If(layer < 1):
                    gp.wait_ge(gate_sent, 2)
                    fresh_acc(I["b_mod_mix"][1:2, :], 2)
                    gp.wait_ge(x_ready, 2)
                    ln_rows(I["ln_ffn_g"][0], I["ln_ffn_b"][0])
                with gp.Else():
                    gp.wait_ge(x_ready, 4)
                    gp.dma_start(w_rt[:, :, :], I["w_router"][0].rearrange("(k p) e -> p k e", p=P),
                                 ).then_inc(rt_loaded, 16)
                    gp.dma_start(b_rt[:, :], I["b_router"][0].partition_broadcast(P)).then_inc(rt_loaded, 16)
                    nc.gpsimd.memset(yacc[:, :, :], 0.0).then_inc(yacc_zero, 1)
                    for b in range(2):
                        gp.wait_ge(gathered[b], EXPERTS)
                    ln_rows(I["ln_ffn_g"][1], I["ln_ffn_b"][1])

        @block.scalar
        def _(act):
            A = nc.scalar.activation

            def round_piece(stretch, i, load_base, split_base):
                j = stretch.split_no[i]
                act.wait_ge(raw_loaded[i % RING], load_base[i % RING] + stretch.loads[i])
                act.wait_ge(split_used, split_base + j + 1)
                nc.scalar.copy(w_hi[:, j % SPLIT, :], w_raw[:, i % RING, :]).then_inc(split_hi, 1)

            def stream(stretch, load_base, split_base, after):
                for i, piece in enumerate(stretch.pieces):
                    if piece[0] == "mod" or i < SPLIT:
                        continue
                    j = stretch.split_no[i]
                    after(j - SPLIT)
                    round_piece(stretch, i, load_base, split_base)
                for j in range(stretch.n_split - SPLIT, stretch.n_split):
                    after(j)

            def root(n, t):
                act.wait_ge(var_ready, n)
                A(std[:, t:t + 1], veps[:, t:t + 1], ACT.Sqrt).then_inc(std_ready, 1)

            def one_plus_scale(sub, free):
                act.wait_ge(mod_sent, sub + 1)
                for c in range(2):
                    ins = A(bank(free + 2 + c), bank(free + 2 + c), ACT.Identity, bias=1.0)
                ins.then_inc(scale_ready, 1)

            def one_plus_gate(sub, held):
                act.wait_ge(gate_sent, sub + 1)
                for c in range(2):
                    ins = A(gate1[:, c * BANK:(c + 1) * BANK], bank(held + 2 + c), ACT.Identity, bias=1.0)
                ins.then_inc(gate1_ready, 1)

            def round_h(sub, t, held):
                act.wait_ge(hT_sent, sub * TT + t + 1)
                for c in range(2):
                    A(actT_hi[:, 4 * c:4 * c + 4, t * P:(t + 1) * P],
                      bank(held + 2 * t + c).rearrange("p (k q) -> p k q", k=4), ACT.Copy).then_inc(hT_hi_ready, 1)

            def norms(sub, n, free, held, ahead):
                ahead(0)
                root(n + 1, 0)
                ahead(1)
                root(n + 2, 0)
                one_plus_scale(sub, free)
                root(n + 3, 1)
                ahead(2)
                round_h(sub, 0, held)
                root(n + 4, 1)
                one_plus_gate(sub, held)
                round_h(sub, 1, held)

            act.wait_ge(c_loaded, 16)
            A(c_act[:, :], c_act[:, :], ACT.Silu).then_inc(c_ready, 1)
            for t in range(TT):
                root(t + 1, t)
            one_plus_scale(0, 4)
            for i in range(SPLIT):
                round_piece(MIX, i, MOD0.landed, 0)
                if i == 0:
                    round_h(0, 0, 0)
                if i == 1:
                    one_plus_gate(0, 0)
                    round_h(0, 1, 0)

            with act.Fori(0, DEPTH) as layer:
                sbase = layer * LAYER_SPLITS
                chain = Chain(act, act_mix, layer * ACT_MIX_STEPS)

                def used(j):
                    act.wait_ge(split_used, sbase + j + 1 + SPLIT)

                def exp_scores(t):
                    act.wait_ge(sc_ready, layer * 2 + t + 1)
                    A(scores[:, :, :], scores[:, :, :], ACT.Exp)
                    A(small[:, 16:24], small[:, 16:24], ACT.Exp).then_inc(exp_ready, 1)

                def probs_T(t):
                    act.wait_ge(pT_sent, layer * 2 + t + 1)
                    A(probT[:, :, :], ps[:, 4:6, :].rearrange("p b (i q) -> p (b i) q", q=P), ACT.Copy).then_inc(pT_ready, 1)

                def after(j):
                    if j in (1, 3, 5):
                        used(j)
                        n = j // 2
                        for t in range(TT):
                            A(proj[:, t, n * BANK:(n + 1) * BANK], bank(2 * t + n % 2), ACT.Copy).then_inc(proj_ready, 1)
                    if j == 4:
                        act.wait_ge(aT_sent, layer + 1)
                        for b in range(2):
                            A(aT[:, 2 * b:2 * b + 2, :], bank(4 + b).rearrange("p (c q) -> p c q", c=2), ACT.Copy).then_inc(aT_ready, 1)
                    if j == 6:
                        used(j)
                        for t in range(TT):
                            twice = proj[:, t, KC:VC].rearrange("p (g r d) -> p r g d", g=2, r=2)
                            for r in range(2):
                                A(twice[:, r], bank(2 * t + 1)[:, 0:P].rearrange("p (g d) -> p g d", g=2), ACT.Copy)
                            A(proj[:, t, VC:PROJ], bank(2 * t + 1)[:, P:2 * P], ACT.Copy).then_inc(proj_ready, 1)
                        act.wait_ge(z_ready, layer * 2 + 2)
                        chain.step(A(soft, z[:, :], ACT.Abs))
                        chain.step(A(soft, soft, ACT.Exp, scale=-1.0))
                        A(soft, soft, ACT.Ln, bias=1.0).then_inc(softplus_ready, 1)
                    if j == 9:
                        act.wait_ge(logw_ready, layer + 1)
                        A(z[:, :], z[:, :], ACT.Exp).then_inc(expw_ready, 1)
                    if j == 11:
                        act.wait_ge(cT_sent, layer + 1)
                        act.wait_ge(ya_sent, layer + 1)
                        for b in range(3):
                            A(cT[:, 2 * b:2 * b + 2, :], bank(4 + b).rearrange("p (c q) -> p c q", c=2), ACT.Copy).then_inc(cT_ready, 1)
                    if j == 12:
                        act.wait_ge(pool_sent, layer + 1)
                        A(proj[:, :, QA:KA], bank(7).rearrange("p (k q) -> p k q", k=2), ACT.Copy).then_inc(pooled_ready, 1)
                        A(v_even[0:HD, :], proj[0:HD, 1, VC:PROJ], ACT.Copy)
                        A(v_even[HD:P, :], proj[HD:P, 0, VC:PROJ], ACT.Copy).then_inc(v_ready, 1)
                    if j == 13:
                        exp_scores(0)
                    if j == 14:
                        probs_T(0)
                    if j == 16:
                        exp_scores(1)
                    if j == 17:
                        probs_T(1)
                    if j >= 8 and j % 2 == 0 and j <= 18:
                        used(j)
                        g = (j - 8) // 2
                        for t in range(TT):
                            A(gates[:, t, g * BANK:(g + 1) * BANK], bank(2 * t + g % 2), ACT.Sigmoid).then_inc(gate_ready, 1)
                    if j == 17:
                        used(17)
                        act.wait_ge(ya_ready, layer + 1)
                        act.wait_ge(yb_ready, layer + 1)
                        A(actT_hi[:, 0:4, :], yT[:, 0:4, :], ACT.Copy).then_inc(yT_hi_ready, 1)
                    if j == 19:
                        act.wait_ge(yc_ready, layer * 2 + 2)
                        A(actT_hi[:, 4:8, :], yT[:, 4:8, :], ACT.Copy).then_inc(yT_hi_ready, 1)
                    if j == 22:
                        merged_T(0)
                    if j == 23:
                        merged_T(1)

                def merged_T(n):
                    act.wait_ge(mT_sent, layer * 2 + n + 1)
                    A(actT_hi[:, 4 * n:4 * n + 4, :].rearrange("p k (t q) -> p t k q", t=TT),
                      ps[:, 2 - 2 * n:4 - 2 * n, :].rearrange("p t (k q) -> p t k q", k=4), ACT.Copy).then_inc(mT_hi_ready, 1)

                layer_loads = [MIX.landed[s] + DENSE.landed[s] for s in range(RING)]
                stream(MIX, [layer * layer_loads[s] + MOD0.landed[s] for s in range(RING)], sbase, after)
                assert chain.n == ACT_MIX_STEPS, chain.n
                norms(layer * 2 + 1, layer * 8 + 2, 0, 4,
                      lambda i: round_piece(DENSE, i, [layer * layer_loads[s] + MOD0.landed[s] + MIX.landed[s] for s in range(RING)],
                                            sbase + MIX.n_split))

                def panel_events(stretch, panels, split_base, panel0, blocks):
                    first_b = {stretch.split_no[i]: p[1] for i, p in enumerate(stretch.pieces) if p[0] == "B" and p[2] == 0}
                    last = {(p[0], p[1]): stretch.split_no[i] for i, p in enumerate(stretch.pieces) if p[0] != "mod"}
                    last = {v: k for k, v in last.items()}

                    def gT_part(p):
                        act.wait_ge(gT_sent, panel0 + p + 1)
                        w = panels[p]
                        for b in range(blocks):
                            ins = A(gT_hi[:, b, 0:w // P, :], ps[:, HW1 + 2 * b, 0:w].rearrange("p (c q) -> p c q", q=P), ACT.Copy)
                        ins.then_inc(gT_hi_ready, 1)

                    def after(j):
                        kind, p = last.get(j, ("", 0))
                        if kind == "A":
                            act.wait_ge(split_used, split_base + j + 1 + SPLIT)
                            if p:
                                act.wait_ge(gated_ready, panel0 + p)
                            w = panels[p]
                            for b in range(blocks):
                                ins = A(silu[:, b, 0:w], ps[:, HW1 + 2 * b, 0:w], ACT.Silu)
                            ins.then_inc(silu_ready, 1)
                        if j in first_b and first_b[j]:
                            gT_part(first_b[j] - 1)
                        if kind == "C" and p == len(panels) - 2:
                            gT_part(len(panels) - 1)

                    return after

                with act.If(layer < 1):
                    stream(DENSE, [MOD0.landed[s] + MIX.landed[s] for s in range(RING)], MIX.n_split,
                           panel_events(DENSE, DENSE_PANELS, MIX.n_split, 0, 2))
                    norms(2, 6, 4, 0, lambda i: round_piece(MIX, i, [layer_loads[s] + MOD0.landed[s] for s in range(RING)], LAYER_SPLITS))
                with act.Else():
                    for t in range(TT):
                        ins = A(h_hi[:, t, :], hbuf[:, t, :], ACT.Copy)
                    ins.then_inc(hh_ready, 1)
                    act.wait_ge(rt_loaded, 32)
                    A(w_rt_hi[:, :, :], w_rt[:, :, :], ACT.Copy).then_inc(rt_hi, 1)
                    act.wait_ge(gap_ready, 1)
                    A(rs[:, 4], rs[:, 3], ACT.Exp).then_inc(e2_ready, 1)
                    act.wait_ge(counts_ready, 1)
                    moe_loads = [MOD0.landed[s] + 2 * MIX.landed[s] + DENSE.landed[s] for s in range(RING)]
                    moe_splits = LAYER_SPLITS + MIX.n_split

                    def round_expert_piece(i, e):
                        ahead, i = divmod(i, EXPERT.n)
                        round_piece(EXPERT, i, [e * EXPERT.landed[s] + moe_loads[s] + ahead * EXPERT.landed[s] for s in range(RING)],
                                    e * EXPERT.n_split + (moe_splits + ahead * EXPERT.n_split))

                    def gathered_rows(b, n):
                        act.wait_ge(gathered[b], n)
                        A(actT_hi[:, :, b * P:(b + 1) * P],
                          ps[:, 4:6, :].rearrange("p c (k q) -> p (c k) q", q=P), ACT.Copy).then_inc(xg_hi_ready[b], 1)

                    def second_block(e, n):
                        with act.If(act.value_load(counts_i[0:1, bass.ds(e, 1)], min_val=0, max_val=SEQ) > P):
                            gathered_rows(1, n)
                        with act.Else():
                            act.sem_inc(xg_hi_ready[1], 1)

                    gathered_rows(0, 1)
                    second_block(0, 1)
                    with act.Fori(0, EXPERTS) as e:
                        count = act.value_load(counts_i[0:1, bass.ds(e, 1)], min_val=0, max_val=SEQ)

                        def expert(blocks):
                            after = panel_events(EXPERT, EXPERT_PANELS, e * EXPERT.n_split + moe_splits,
                                                 e * len(EXPERT_PANELS) + len(DENSE_PANELS), blocks)
                            for i in range(SPLIT, EXPERT.n):
                                after(i - SPLIT)
                                if i - SPLIT == 3:
                                    act.wait_ge(place_sent, e + 1)
                                    A(place[:, 0:blocks, :], ps[:, 0, 0:blocks * SEQ].rearrange("p (b q) -> p b q", q=SEQ),
                                      ACT.Copy).then_inc(place_ready, 1)
                                round_expert_piece(i, e)

                            def tail(last):
                                for n in range(SPLIT):
                                    after(EXPERT.n - SPLIT + n)
                                    if n == SPLIT - 1:
                                        act.wait_ge(split_used, e * EXPERT.n_split + (moe_splits + EXPERT.n_split + SPLIT))
                                        for b in range(blocks):
                                            ins = A(hbuf[:, b, 0:BANK], bank(2 * b), ACT.Copy)
                                        ins.then_inc(y_act, 1)
                                    if not last:
                                        round_expert_piece(EXPERT.n + n, e)
                                if not last:
                                    gathered_rows(0, e + 2)
                                    second_block(e + 1, e + 2)

                            with act.If(e < EXPERTS - 1):
                                tail(False)
                            with act.Else():
                                tail(True)

                        with act.If(count > P):
                            expert(2)
                        with act.Else():
                            expert(1)
                    for t in range(TT):
                        root(15 + t, t)

        @block.vector
        def _(dve):
            TS, TTn, STT, RED = nc.vector.tensor_scalar, nc.vector.tensor_tensor, nc.vector.scalar_tensor_tensor, nc.vector.tensor_reduce

            def rest_of_piece(stretch, i, split_base):
                j = stretch.split_no[i]
                dve.wait_ge(split_hi, split_base + j + 1)
                TTn(w_lo[:, j % SPLIT, :], w_raw[:, i % RING, :], w_hi[:, j % SPLIT, :].bitcast(F32),
                    ALU.subtract).then_inc(piece_used, 1)

            def mod_piece(stretch, i, load_base, piece_base, step_base, acc_no):
                q = stretch.pieces[i][1]
                if q == 0:
                    dve.wait_ge(acc_ready, acc_no * 16)
                    dve.wait_ge(c_ready, 1)
                dve.wait_ge(raw_loaded[i % RING], load_base[i % RING] + stretch.loads[i])
                w = w_raw[:, i % RING, :].rearrange("p (k n) -> p k n", k=2)
                previous = max((m for m in range(i) if stretch.pieces[m][0] == "mod"), default=None)
                for m in range(4):
                    k, n = m // 2, m % 2
                    acc = mod_acc[:, (q // 4) * D + n * BANK:(q // 4) * D + (n + 1) * BANK]
                    if m == 0 and q:
                        dve.wait_ge(mod_step, step_base + 3 * q)
                    if m == 1 and q:
                        dve.wait_ge(piece_used, piece_base + previous + 1 + RING)
                    if m >= 2:
                        dve.wait_ge(mod_step, step_base + 3 * q + m - 1)
                    ins = STT(acc, w[:, k, n * BANK:(n + 1) * BANK], c_act[:, 2 * (q % 4) + k:2 * (q % 4) + k + 1], acc,
                              ALU.mult, ALU.add)
                    ins.then_inc(piece_used if m == 3 else mod_step, 1)

            def stream(stretch, load_base, split_base, piece_base, step_base, acc_no, after):
                for i, piece in enumerate(stretch.pieces):
                    if piece[0] == "mod":
                        mod_piece(stretch, i, load_base, piece_base, step_base, acc_no)
                        continue
                    if i < SPLIT:
                        continue
                    j = stretch.split_no[i]
                    after(j - SPLIT)
                    rest_of_piece(stretch, i, split_base)
                for j in range(stretch.n_split - SPLIT, stretch.n_split):
                    after(j)

            def statistics(chain, src, t):
                for c in range(2):
                    ins = nc.vector.bn_stats(stats[:, t, c, :], src[:, t, c * BANK:(c + 1) * BANK])
                chain.step(ins)
                nc.vector.memset(veps[:, t:t + 1], 0.0)
                chain.step(nc.vector.bn_aggr(mv[:, t, :], stats[:, t, :, :].rearrange("p c s -> p (c s)")))
                TS(veps[:, t:t + 1], mv[:, t, 1:2], EPS, None, ALU.add).then_inc(var_ready, 1)

            def inverse_std(chain, n, t):
                dve.wait_ge(std_ready, n)
                chain.step(nc.vector.reciprocal(rstd[:, t:t + 1], std[:, t:t + 1]))

            def halves(t):
                return [hbuf[:, t, c * BANK:(c + 1) * BANK] for c in range(2)]

            def residual(chain, f, t):
                for c, part in enumerate(halves(t)):
                    ins = TTn(part, f(t, c), gate1[:, c * BANK:(c + 1) * BANK], ALU.mult)
                chain.step(ins)
                for c, part in enumerate(halves(t)):
                    ins = STT(part, x[:, t, c * BANK:(c + 1) * BANK], ALPHA, part, ALU.mult, ALU.add)
                chain.step(ins)

            def layer_norm(chain, t):
                chain.step(STT(hbuf[:, t, :], hbuf[:, t, :], mv[:, t, 0:1], lnrow[:, 0, :], ALU.subtract, ALU.mult))
                return STT(x[:, t, :], hbuf[:, t, :], rstd[:, t:t + 1], lnrow[:, 1, :], ALU.mult, ALU.add)

            def modulate(chain, t, free):
                for c, part in enumerate(halves(t)):
                    ins = STT(part, x[:, t, c * BANK:(c + 1) * BANK], mv[:, t, 0:1], bank(free + 2 + c), ALU.subtract, ALU.mult)
                chain.step(ins)
                for c, part in enumerate(halves(t)):
                    ins = STT(part, part, rstd[:, t:t + 1], bank(free + c), ALU.mult, ALU.add)
                ins.then_inc(h_ready, 1)

            def rest_of_h(sub, t, held):
                for c in range(2):
                    dve.wait_ge(hT_hi_ready, sub * 4 + 2 * t + c + 1)
                    at = (slice(None), slice(4 * c, 4 * c + 4), slice(t * P, (t + 1) * P))
                    TTn(actT_lo[at], bank(held + 2 * t + c).rearrange("p (k q) -> p k q", k=4), actT_hi[at].bitcast(F32),
                        ALU.subtract).then_inc(hT_lo_ready, 1)

            def norms(chain, sub, n, free, held, f, f_done, n_ln, ahead):
                ahead(0)
                dve.wait_ge(gate1_ready, sub)
                f_done(0)
                residual(chain, f, 0)
                statistics(chain, hbuf, 0)
                dve.wait_ge(ln_loaded, n_ln)
                inverse_std(chain, n + 1, 0)
                chain.step(layer_norm(chain, 0))
                statistics(chain, x, 0)
                ahead(1)
                f_done(1)
                residual(chain, f, 1)
                statistics(chain, hbuf, 1)
                inverse_std(chain, n + 2, 0)
                dve.wait_ge(scale_ready, sub + 1)
                modulate(chain, 0, free)
                inverse_std(chain, n + 3, 1)
                chain.step(layer_norm(chain, 1))
                statistics(chain, x, 1)
                rest_of_h(sub, 0, held)
                inverse_std(chain, n + 4, 1)
                modulate(chain, 1, free)
                ahead(2)
                rest_of_h(sub, 1, held)
                dve.sem_inc(x_ready, 1)

            dve.wait_ge(x_loaded, 16)
            dve.sem_inc(x_ready, 1)
            chain = Chain(dve, dve_start)
            for t in range(TT):
                statistics(chain, x, t)
            dve.sem_inc(added, 4)
            for i in range(MOD0.n):
                mod_piece(MOD0, i, [0] * RING, 0, 0, 1)
            for t in range(TT):
                inverse_std(chain, t + 1, t)
            rest_of_piece(MIX, 0, 0)
            dve.wait_ge(scale_ready, 1)
            for t in range(TT):
                modulate(chain, t, 4)
            rest_of_h(0, 0, 0)
            rest_of_piece(MIX, 1, 0)
            rest_of_h(0, 1, 0)
            rest_of_piece(MIX, 2, 0)
            dve.wait_ge(cst_loaded, 16)

            with dve.Fori(0, DEPTH) as layer:
                sbase = layer * LAYER_SPLITS
                chain = Chain(dve, dve_mix, layer * DVE_MIX_STEPS)
                step = chain.step
                z0 = z[:, 0:1024].rearrange("p (h q) -> p h q", h=4)
                z1 = z[:, 1024:1536].rearrange("p (h q) -> p h q", h=4)
                s0 = soft[:, 0:1024].rearrange("p (h q) -> p h q", h=4)
                s1 = soft[:, 1024:1536].rearrange("p (h q) -> p h q", h=4)
                past4 = past.unsqueeze(1).broadcast_to([P, 4, P])
                sink_v = sinks[:, :].rearrange("p (i r) -> p r i", r=2)
                mx = small[:, 0:8]
                mx_v = mx.rearrange("p (r i) -> p r i", r=2)
                es = small[:, 16:24]
                den, rden = small[:, 24:32], small[:, 32:40]

                def rotate(t):
                    v = proj[:, t, QC:VC].rearrange("p (h d) -> p h d", d=HD)
                    n = v.shape[1]
                    ta = gates[:, 0, 3 * D - n * HD:3 * D].rearrange("p (h d) -> p h d", d=HD)
                    tb = gates[:, 1, 3 * D - n * HD:3 * D].rearrange("p (h d) -> p h d", d=HD)
                    cos = cst[:, C_COS + t * HD:C_COS + (t + 1) * HD].unsqueeze(1).broadcast_to([P, n, HD])
                    sin = cst[:, C_SIN + t * HD:C_SIN + (t + 1) * HD].unsqueeze(1)
                    TTn(ta, v, cos, ALU.mult)
                    TTn(tb[:, :, 0:HALF], v[:, :, HALF:HD], sin[:, :, 0:HALF].broadcast_to([P, n, HALF]), ALU.mult)
                    step(TTn(tb[:, :, HALF:HD], v[:, :, 0:HALF], sin[:, :, HALF:HD].broadcast_to([P, n, HALF]), ALU.mult))
                    TTn(v, ta, tb, ALU.add).then_inc(rope_ready, 1)
                    dve.wait_ge(rope_ready, layer * 2 + t + 1)

                def shift_scores(t):
                    dve.wait_ge(sc_sent, layer * 2 + t + 1)
                    raw = ps[:, 4:6, :].rearrange("p b (i q) -> p (b i) q", q=P)
                    if t == 0:
                        step(STT(scores[:, :, :], raw, SCALE, sw_mask.unsqueeze(1).broadcast_to([P, 8, P]), ALU.mult, ALU.add))
                        dve.wait_ge(small_loaded, layer * 64 + 64)
                    else:
                        step(TS(scores[:, :, :], raw, SCALE, None, ALU.mult))
                    step(RED(mx, scores[:, :, :], AX_X, ALU.max))
                    step(TTn(mx_v, mx_v, sink_v, ALU.max))
                    TTn(es.rearrange("p (r i) -> p r i", r=2), sink_v, mx_v, ALU.subtract)
                    TTn(scores[:, :, :], scores[:, :, :], mx.unsqueeze(2).broadcast_to([P, 8, P]), ALU.subtract).then_inc(sc_ready, 1)

                def divide_scores(t):
                    dve.wait_ge(exp_ready, layer * 2 + t + 1)
                    step(RED(den, scores[:, :, :], AX_X, ALU.add))
                    step(TTn(den, den, es, ALU.add))
                    step(nc.vector.reciprocal(rden, den))
                    TTn(scores[:, :, :], scores[:, :, :], rden.unsqueeze(2).broadcast_to([P, 8, P]), ALU.mult).then_inc(prob_ready, 1)

                def yc_out(t):
                    dve.wait_ge(yc_sent, layer * 2 + t + 1)
                    nc.vector.tensor_copy(yT[:, 4:8, t * P:(t + 1) * P], bank(6).rearrange("p (i q) -> p i q", q=P)).then_inc(yc_ready, 1)

                def gated_branch(n, br, first_bank):
                    for t in range(TT):
                        gate = gates[:, t, br * D + n * BANK:br * D + (n + 1) * BANK]
                        ins = TTn(gate, gate, bank(first_bank + t), ALU.mult)
                    ins.then_inc(branch_read, 1)
                    dve.wait_ge(branch_read, layer * 6 + BRANCH_ORDER.index((br, n)) + 1)

                def gate_columns(n, br, t):
                    return gates[:, t, br * D + n * BANK:br * D + (n + 1) * BANK]

                def after(j):
                    if j == 5:
                        dve.wait_ge(z_sent, layer + 1)
                        TS(z[:, 0:1024], ps[:, 4:6, :].rearrange("p b q -> p (b q)"), SCALE, None, ALU.mult).then_inc(z_ready, 1)
                        TS(z[:, 1024:1536].rearrange("p (b q) -> p b q", b=2), ps[:, 6:8, 0:256], SCALE, None, ALU.mult).then_inc(z_ready, 1)
                    if j == 6:
                        dve.wait_ge(softplus_ready, layer + 1)
                        step(STT(soft, z[:, :], 0.0, soft, ALU.max, ALU.add))
                        TTn(s0[:, :, 0:P], s0[:, :, 0:P], past4, ALU.mult)
                        TTn(s1, s1, past4, ALU.mult).then_inc(soft_ready, 1)
                    if j == 7:
                        dve.wait_ge(proj_ready, layer * 8 + 8)
                        for t in range(TT):
                            rotate(t)
                    if j == 8:
                        dve.wait_ge(suffix_sent, layer + 1)
                        TTn(z[:, 0:1024], z[:, 0:1024], ps[:, 4:6, :].rearrange("p b q -> p (b q)"), ALU.subtract)
                        step(TTn(z[:, 1024:1536], z[:, 1024:1536], bank(6), ALU.subtract))
                        TS(z[:, :], z[:, :], 0.0, None, ALU.min).then_inc(logw_ready, 1)
                    if j == 9:
                        dve.wait_ge(expw_ready, layer + 1)
                        TTn(z0[:, :, 0:P], z0[:, :, 0:P], past4, ALU.mult)
                        TTn(z1, z1, past4, ALU.mult).then_inc(w_ready, 1)
                    if j == 11:
                        dve.wait_ge(ya_sent, layer + 1)
                        nc.vector.tensor_copy(yT[:, 0:2, :], bank(7).rearrange("p (k q) -> p k q", k=2)).then_inc(ya_ready, 1)
                    if j == 12:
                        shift_scores(0)
                    if j == 13:
                        divide_scores(0)
                    if j == 14:
                        dve.wait_ge(yb_sent, layer + 1)
                        for k in range(2):
                            ins = TS(yT[:, 2 + k, :], bank(7)[:, k * 256:(k + 1) * 256], pool_scale[:, k:k + 1], None, ALU.mult)
                        ins.then_inc(yb_ready, 1)
                    if j == 15:
                        yc_out(0)
                        shift_scores(1)
                    if j == 16:
                        divide_scores(1)
                    if j == 17:
                        yT_rest(0)
                    if j == 18:
                        yc_out(1)
                    if j == 19:
                        dve.wait_ge(gate_ready, layer * 12 + 12)
                        yT_rest(1)
                        dve.wait_ge(split_used, sbase + 20 + SPLIT)
                        gated_branch(0, 0, 0)
                        gated_branch(0, 1, 2)
                        for t in range(TT):
                            ins = TTn(gate_columns(0, 0, t), gate_columns(0, 0, t), gate_columns(0, 1, t), ALU.add)
                        step(ins)
                    if j == 20:
                        dve.wait_ge(split_used, sbase + 21 + SPLIT)
                        gated_branch(1, 1, 0)
                        gated_branch(1, 0, 4)
                        for t in range(TT):
                            ins = TTn(gate_columns(1, 0, t), gate_columns(1, 0, t), gate_columns(1, 1, t), ALU.add)
                        step(ins)
                    if j in (22, 23):
                        n = j - 22
                        dve.wait_ge(mT_hi_ready, layer * 2 + n + 1)
                        part = (slice(None), slice(4 * n, 4 * n + 4), slice(None))
                        TTn(actT_lo[part].rearrange("p k (t q) -> p t k q", t=TT),
                            ps[:, 2 - 2 * n:4 - 2 * n, :].rearrange("p t (k q) -> p t k q", k=4),
                            actT_hi[part].bitcast(F32).rearrange("p k (t q) -> p t k q", t=TT), ALU.subtract).then_inc(mT_lo_ready, 1)
                    if j in (21, 22):
                        n = j - 21
                        dve.wait_ge(split_used, sbase + j + 1 + SPLIT)
                        gated_branch(n, 2, 2 - 2 * n)
                        for t in range(TT):
                            TTn(hbuf[:, t, n * BANK:(n + 1) * BANK], gate_columns(n, 0, t), gate_columns(n, 2, t), ALU.add).then_inc(merged_ready, 1)

                def yT_rest(c):
                    dve.wait_ge(yT_hi_ready, layer * 2 + c + 1)
                    part = (slice(None), slice(4 * c, 4 * c + 4), slice(None))
                    TTn(actT_lo[part], yT[part], actT_hi[part].bitcast(F32), ALU.subtract).then_inc(yT_lo_ready, 1)

                layer_loads = [MIX.landed[s] + DENSE.landed[s] for s in range(RING)]
                stream(MIX, [layer * layer_loads[s] + MOD0.landed[s] for s in range(RING)], sbase,
                       layer * LAYER_PIECES + MOD0.n, layer * (6 * MODS) + 3 * MODS, layer * 2 + 2, after)
                norms(chain, layer * 2 + 1, layer * 8 + 2, 0, 4, lambda t, c: bank(4 + 2 * t + c),
                      lambda t: dve.wait_ge(split_used, sbase + (MIX.n_split + SPLIT)) if t else dve.wait_ge(out_sent, layer + 1),
                      layer * 64 + 32,
                      lambda i: rest_of_piece(DENSE, i, sbase + MIX.n_split))
                assert chain.n == DVE_MIX_STEPS, chain.n

                def panel_events(stretch, panels, split_base, panel0, blocks):
                    first_b = {stretch.split_no[i]: p[1] for i, p in enumerate(stretch.pieces) if p[0] == "B" and p[2] == 0}
                    last = {(p[0], p[1]): stretch.split_no[i] for i, p in enumerate(stretch.pieces) if p[0] != "mod"}
                    last = {v: k for k, v in last.items()}

                    def gT_part(p):
                        dve.wait_ge(gT_hi_ready, panel0 + p + 1)
                        w = panels[p]
                        for b in range(blocks):
                            ins = TTn(gT_lo[:, b, 0:w // P, :], ps[:, HW1 + 2 * b, 0:w].rearrange("p (c q) -> p c q", q=P),
                                      gT_hi[:, b, 0:w // P, :].bitcast(F32), ALU.subtract)
                        ins.then_inc(gT_lo_ready, 1)

                    def after(j):
                        kind, p = last.get(j, ("", 0))
                        if j in first_b and first_b[j]:
                            gT_part(first_b[j] - 1)
                        if kind == "B":
                            dve.wait_ge(split_used, split_base + j + 1 + SPLIT)
                            dve.wait_ge(silu_ready, panel0 + p + 1)
                            w = panels[p]
                            for b in range(blocks):
                                ins = TTn(gated[:, b, 0:w], silu[:, b, 0:w], ps[:, HW3 + 2 * b, 0:w], ALU.mult)
                            ins.then_inc(gated_ready, 1)
                        if kind == "C" and p == len(panels) - 2:
                            gT_part(len(panels) - 1)

                    return after

                with dve.If(layer < 1):
                    chain = Chain(dve, dve_ffn, 0)
                    stream(DENSE, [MOD0.landed[s] + MIX.landed[s] for s in range(RING)], MIX.n_split,
                           MOD0.n + MIX.n, 6 * MODS, 3, panel_events(DENSE, DENSE_PANELS, MIX.n_split, 0, 2))
                    norms(chain, 2, 6, 4, 0, lambda t, c: bank(2 * t + c),
                          lambda t: dve.wait_ge(split_used, LAYER_SPLITS + SPLIT), 64,
                          lambda i: rest_of_piece(MIX, i, LAYER_SPLITS))
                    assert chain.n == DVE_DENSE_STEPS, chain.n
                with dve.Else():
                    chain = Chain(dve, dve_ffn, DVE_DENSE_STEPS)
                    step = chain.step
                    dve.wait_ge(hh_ready, 1)
                    for t in range(TT):
                        ins = TTn(h_lo[:, t, :], hbuf[:, t, :], h_hi[:, t, :].bitcast(F32), ALU.subtract)
                    ins.then_inc(hl_ready, 1)
                    dve.wait_ge(rt_hi, 1)
                    TTn(w_rt_lo[:, :, :], w_rt[:, :, :], w_rt_hi[:, :, :].bitcast(F32), ALU.subtract).then_inc(rt_lo, 1)

                    wide = [P, TT, EXPERTS]
                    number = iota[:, 0:EXPERTS].unsqueeze(1).broadcast_to(wide)
                    logit, tmp, is1, rest, is2, sel, pos = (rt[:, n] for n in range(7))
                    m1, i1, m2, gap, e2, w1, w2 = (rs[:, n] for n in range(7))
                    dve.wait_ge(logits_sent, 1)
                    step(TTn(logit, ps[:, ROUTE, 0:16].rearrange("p (t e) -> p t e", t=TT), b_rt[:, :].unsqueeze(1).broadcast_to(wide), ALU.add))

                    def largest(values, m, is_it):
                        step(RED(m, values, AX_X, ALU.max))
                        step(TTn(tmp, values, m.broadcast_to(wide), ALU.not_equal))
                        step(STT(tmp, tmp, 64.0, number, ALU.mult, ALU.add))
                        step(RED(i1, tmp, AX_X, ALU.min))
                        step(TTn(is_it, number, i1.broadcast_to(wide), ALU.is_equal))

                    largest(logit, m1, is1)
                    step(STT(rest, is1, -1e38, logit, ALU.mult, ALU.add))
                    largest(rest, m2, is2)
                    TTn(sel, is1, is2, ALU.add).then_inc(sel_ready, 1)
                    TTn(gap, m2, m1, ALU.subtract).then_inc(gap_ready, 1)
                    dve.wait_ge(e2_ready, 1)
                    step(TS(w2, e2, 1.0, None, ALU.add))
                    step(nc.vector.reciprocal(w1, w2))
                    step(TTn(w2, e2, w1, ALU.mult))
                    step(TTn(tmp, is1, w1.broadcast_to(wide), ALU.mult))
                    step(TTn(is2, is2, w2.broadcast_to(wide), ALU.mult))
                    nc.vector.memset(wsel[:, :, EXPERTS:], 0.0)
                    nc.vector.memset(posm[:, :, EXPERTS:], -1.0)
                    step(TTn(wsel[:, :, 0:EXPERTS], tmp, is2, ALU.add))
                    dve.wait_ge(pos_sent, 1)
                    step(TS(pos, ps[:, ROUTE + 1, 0:16].rearrange("p (t e) -> p t e", t=TT), 1.0, None, ALU.add))
                    step(TTn(pos, pos, sel, ALU.mult))
                    step(TS(posm[:, :, 0:EXPERTS], pos, -1.0, None, ALU.add))
                    nc.vector.tensor_copy(counts_i[:, 0:EXPERTS], ps[:, ROUTE + 1, 16:24]).then_inc(counts_ready, 1)
                    dve.wait_ge(counts_ready, 1)
                    moe_splits = LAYER_SPLITS + MIX.n_split

                    def pick_tokens(e):
                        for t in range(TT):
                            at = posm[:, t, bass.ds(e, 1)]
                            TS(pick[:, t, :], iota, at, None, ALU.is_equal)
                            ins = TS(pick_w[:, t, :], iota, at, wsel[:, t, bass.ds(e, 1)], ALU.is_equal, ALU.mult)
                        ins.then_inc(pick_ready, 1)

                    def rest_of_expert_piece(i, e):
                        ahead, i = divmod(i, EXPERT.n)
                        rest_of_piece(EXPERT, i, e * EXPERT.n_split + (moe_splits + ahead * EXPERT.n_split))

                    def gathered_rows(b, n):
                        dve.wait_ge(gathered[b], n)
                        nc.vector.tensor_copy(actT_lo[:, :, b * P:(b + 1) * P],
                                              ps[:, 6:8, :].rearrange("p c (k q) -> p (c k) q", q=P)).then_inc(xg_lo_ready[b], 1)

                    def second_block(e, n):
                        with dve.If(dve.value_load(counts_i[0:1, bass.ds(e, 1)], min_val=0, max_val=SEQ) > P):
                            gathered_rows(1, n)
                        with dve.Else():
                            dve.sem_inc(xg_lo_ready[1], 1)

                    pick_tokens(0)
                    gathered_rows(0, 1)
                    second_block(0, 1)
                    dve.wait_ge(yacc_zero, 1)
                    with dve.Fori(0, EXPERTS) as e:
                        count = dve.value_load(counts_i[0:1, bass.ds(e, 1)], min_val=0, max_val=SEQ)

                        def expert(blocks):
                            after = panel_events(EXPERT, EXPERT_PANELS, e * EXPERT.n_split + moe_splits,
                                                 e * len(EXPERT_PANELS) + len(DENSE_PANELS), blocks)
                            for i in range(SPLIT, EXPERT.n):
                                after(i - SPLIT)
                                rest_of_expert_piece(i, e)
                                if i == EXPERT.n // 2:
                                    pick_tokens(e + 1)

                            def tail(last):
                                for n in range(SPLIT):
                                    after(EXPERT.n - SPLIT + n)
                                    if n == SPLIT - 1:
                                        dve.wait_ge(split_used, e * EXPERT.n_split + (moe_splits + EXPERT.n_split + SPLIT))
                                        for b in range(blocks):
                                            ins = nc.vector.tensor_copy(hbuf[:, b, BANK:D], bank(2 * b + 1))
                                        ins.then_inc(y_dve, 1)
                                    if not last:
                                        rest_of_expert_piece(EXPERT.n + n, e)
                                if not last:
                                    gathered_rows(0, e + 2)
                                for t in range(TT):
                                    for c in range(2):
                                        dve.wait_ge(scattered, e * 4 + 2 * t + c + 1)
                                        part = yacc[:, t, c * BANK:(c + 1) * BANK]
                                        TTn(part, part, bank(2 * t + c), ALU.add).then_inc(added, 1)
                                if not last:
                                    second_block(e + 1, e + 2)

                            with dve.If(e < EXPERTS - 1):
                                tail(False)
                            with dve.Else():
                                tail(True)

                        with dve.If(count > P):
                            expert(2)
                        with dve.Else():
                            expert(1)
                    dve.wait_ge(added, 4 * EXPERTS + 4)
                    dve.wait_ge(ln_loaded, 128)
                    dve.wait_ge(gate1_ready, 4)
                    for t in range(TT):
                        residual(chain, lambda t, c: yacc[:, t, c * BANK:(c + 1) * BANK], t)
                        statistics(chain, hbuf, t)
                    for t in range(TT):
                        inverse_std(chain, 15 + t, t)
                        layer_norm(chain, t).then_inc(x_ready, 1)
                    assert chain.n == DVE_ROUTE_STEPS, chain.n

        @block.tensor
        def _(pe):
            MM, TR = nc.tensor.matmul, nc.tensor.transpose

            def product(to, hi, lo, w_h, w_l, first, last):
                MM(to, hi, w_h, start=first, stop=False)
                MM(to, hi, w_l, start=False, stop=False)
                return MM(to, lo, w_h, start=False, stop=last)

            def split_piece(j, k, n, width):
                at = slice(k * width + n, k * width + n + min(width, BANK))
                return w_hi[:, j % SPLIT, at], w_lo[:, j % SPLIT, at]

            def transposed(t, first_bank, signal):
                for k in range(KD):
                    ins = TR(ps[:, first_bank + k // 4, (k % 4) * P:(k % 4 + 1) * P], hbuf[:, t, k * P:(k + 1) * P], ident)
                ins.then_inc(signal, 1)

            def send_modulation(free):
                for q in range(4):
                    ins = MM(bank(free + q), ones, mod_acc[:, q * BANK:(q + 1) * BANK], start=True, stop=True)
                ins.then_inc(mod_sent, 1)

            def open_sublayer(sub, free, held):
                send_modulation(free)
                pe.wait_ge(h_ready, sub * TT + 1)
                transposed(0, held, hT_sent)
                for q in range(2):
                    ins = MM(bank(held + 2 + q), ones, mod_acc[:, (4 + q) * BANK:(5 + q) * BANK], start=True, stop=True)
                ins.then_inc(gate_sent, 1)

            def second_tile(sub, held):
                pe.wait_ge(h_ready, sub * TT + 2)
                pe.wait_ge(gate1_ready, sub + 1)
                transposed(1, held + 2, hT_sent)

            def open_tile(sub, t):
                pe.wait_ge(hT_hi_ready, sub * 4 + 2 * t + 2)
                pe.wait_ge(hT_lo_ready, sub * 4 + 2 * t + 2)

            def chunk(k, t):
                return actT_hi[:, k, t * P:(t + 1) * P], actT_lo[:, k, t * P:(t + 1) * P]

            pe.wait_ge(cst_loaded, 16)
            pe.wait_ge(piece_used, MOD0.n + RING)
            open_sublayer(0, 4, 0)
            with pe.Fori(0, DEPTH) as layer:
                pbase = layer * LAYER_PIECES + MOD0.n

                def project(j, n, h, width=BANK, tiles=range(TT)):
                    ks = range(4 * h, 4 * h + 4) if width == BANK else range(KD)
                    for t in tiles:
                        for k in ks:
                            w = split_piece(j, k - ks[0], 0, width)
                            ins = product(bank(2 * t + n % 2, width), *chunk(k, t), *w, k == 0, k == KD - 1)
                    if TT - 1 in tiles:
                        ins.then_inc(split_used, 1)

                def stick_scores():
                    pe.wait_ge(aT_ready, layer * 2 + 2)
                    for h in range(SB_HEADS):
                        par, pair = h % 2, h // 2
                        rows = slice(par * HD, (par + 1) * HD)
                        MM(ps[:, 4 + par, pair * SEQ:(pair + 1) * SEQ], aT[rows, 2 + pair, 0:P], aT[rows, pair, :], start=True, stop=True)
                        ins = MM(ps[:, 6 + par, pair * P:(pair + 1) * P], aT[rows, 2 + pair, P:SEQ], aT[rows, pair, P:SEQ], start=True, stop=True)
                    ins.then_inc(z_sent, 1)

                def suffix_sums():
                    pe.wait_ge(soft_ready, layer + 1)
                    for par in range(2):
                        MM(bank(4 + par), tri, soft[:, par * BANK:(par + 1) * BANK], start=True, stop=False)
                        MM(bank(4 + par).rearrange("p (a q) -> p a q", q=SEQ)[:, :, P:SEQ], ones,
                           soft[:, 1024 + par * SEQ:1024 + (par + 1) * SEQ].rearrange("p (a q) -> p a q", q=P), start=False, stop=True)
                    MM(bank(6), tri, soft[:, 1024:1536], start=True, stop=True).then_inc(suffix_sent, 1)

                def stick_values():
                    pe.wait_ge(w_ready, layer + 1)
                    for h in range(SB_HEADS):
                        par, pair = h % 2, h // 2
                        rows = slice(par * HD, (par + 1) * HD)
                        v = slice(VA + h * HD, VA + (h + 1) * HD)
                        w0 = z[:, (2 * par + pair) * SEQ:(2 * par + pair + 1) * SEQ]
                        w1 = z[:, 1024 + (2 * par + pair) * P:1024 + (2 * par + pair + 1) * P]
                        MM(ps[rows, 7, pair * SEQ:(pair + 1) * SEQ], proj[:, 0, v], w0, start=True, stop=False)
                        ins = MM(ps[rows, 7, pair * SEQ + P:(pair + 1) * SEQ], proj[:, 1, v], w1, start=False, stop=True)
                    ins.then_inc(ya_sent, 1)

                def pool_windows():
                    pe.wait_ge(ya_ready, layer + 1)
                    for g in range(len(WINDOWS)):
                        rows = slice((g % 2) * HD, (g % 2 + 1) * HD)
                        u = slice(UB + g * HD, UB + (g + 1) * HD)
                        at, band = (g // 2) * SEQ, C_BAND + g * BAND_W
                        MM(ps[rows, 7, at:at + P], proj[:, 0, u], cst[:, band:band + P], start=True, stop=True)
                        MM(ps[rows, 7, at + P:at + 2 * P], proj[:, 1, u], cst[:, band + P:band + 2 * P], start=True, stop=False)
                        ins = MM(ps[rows, 7, at + P:at + P + SPILL], proj[:, 0, u], cst[:, band + 2 * P:band + BAND_W], start=False, stop=True)
                    ins.then_inc(pool_sent, 1)

                def pool_mix():
                    for g in range(len(WINDOWS)):
                        rows = slice((g % 2) * HD, (g % 2 + 1) * HD)
                        at = (g // 2) * SEQ
                        ins = MM(ps[rows, 7, at:at + SEQ], w_pool[rows, g // 2, :], proj[rows, g // 2, QA:KA], start=True, stop=True)
                    ins.then_inc(yb_sent, 1)

                def band_scores(t):
                    for h in range(Q_HEADS):
                        par, i, g = h % 2, h // 2, h // (Q_HEADS // KV_HEADS)
                        rows = slice(par * HD, (par + 1) * HD)
                        q0 = t * P
                        key = lambda c: cT[rows, 4 + g, c * CHUNK:(c + 1) * CHUNK]
                        before = 2 * t - 1 if t else 1
                        MM(ps[:, 4 + par, i * P:i * P + CHUNK], cT[rows, i, q0:q0 + P], key(2 * t), start=True, stop=True)
                        MM(ps[0:CHUNK, 4 + par, i * P + CHUNK:(i + 1) * P], cT[rows, i, q0:q0 + CHUNK], key(before), start=True, stop=True)
                        ins = MM(ps[CHUNK:P, 4 + par, i * P + CHUNK:(i + 1) * P], cT[rows, i, q0 + CHUNK:q0 + P], key(2 * t + 1), start=True, stop=True)
                    ins.then_inc(sc_sent, 1)

                def turn_probs(t):
                    pe.wait_ge(prob_ready, layer * 2 + t + 1)
                    for n in range(Q_HEADS):
                        ins = TR(ps[:, 4 + n // 4, (n % 4) * P:(n % 4 + 1) * P], scores[:, n, :], ident)
                    ins.then_inc(pT_sent, 1)

                def band_values(t):
                    pe.wait_ge(pT_ready, layer * 2 + t + 1)
                    pe.wait_ge(v_ready, layer + 1)
                    if t:
                        pe.wait_ge(yc_ready, layer * 2 + 1)
                    for par in range(2):
                        for g in range(KV_HEADS):
                            for odd in range(2):
                                v = v_even[:, :] if t and not odd else proj[:, t, VC:PROJ]
                                qs = slice(odd * CHUNK, (odd + 1) * CHUNK)
                                to = ps[par * HD:(par + 1) * HD, 6, 2 * g * P:(2 * g + 2) * P].rearrange("p (i q) -> p i q", q=P)
                                ins = MM(to[:, :, qs], v[:, g * HD:(g + 1) * HD], probT[:, 4 * par + 2 * g:4 * par + 2 * g + 2, qs],
                                         start=True, stop=True)
                    ins.then_inc(yc_sent, 1)

                def project_out(j, n, h, t):
                    for k in range(4 * h, 4 * h + 4):
                        ins = product(bank(4 + 2 * t + n), *chunk(k, t), *split_piece(j, k % 4, 0, BANK), k == 0, k == KD - 1)
                    return ins

                def merged_T(n):
                    pe.wait_ge(merged_ready, layer * 4 + 2 * n + 2)
                    for t in range(TT):
                        for k in range(4):
                            ins = TR(ps[:, 2 - 2 * n + t, k * P:(k + 1) * P], hbuf[:, t, (4 * n + k) * P:(4 * n + k + 1) * P], ident)
                    ins.then_inc(mT_sent, 1)

                def after(j):
                    if j == 3:
                        pe.wait_ge(proj_ready, layer * 8 + 2)
                        for c in range(4):
                            for t in range(TT):
                                ins = TR(ps[:, 4 + c // 2, (c % 2) * SEQ + t * P:(c % 2) * SEQ + (t + 1) * P], proj[:, t, c * P:(c + 1) * P], ident)
                        ins.then_inc(aT_sent, 1)
                    if j == 5:
                        stick_scores()
                    if j == 8:
                        suffix_sums()
                    if j == 10:
                        pe.wait_ge(rope_ready, layer * 2 + 2)
                        pe.wait_ge(logw_ready, layer + 1)
                        for c in range(6):
                            for t in range(TT):
                                ins = TR(ps[:, 4 + c // 2, (c % 2) * SEQ + t * P:(c % 2) * SEQ + (t + 1) * P], proj[:, t, QC + c * P:QC + (c + 1) * P], ident)
                        ins.then_inc(cT_sent, 1)
                    if j == 11:
                        stick_values()
                    if j == 12:
                        pe.wait_ge(cT_ready, layer * 3 + 3)
                        band_scores(0)
                        pool_windows()
                    if j == 13:
                        pool_mix()
                    if j == 14:
                        turn_probs(0)
                    if j == 15:
                        band_values(0)
                        band_scores(1)
                    if j == 17:
                        turn_probs(1)
                    if j == 18:
                        band_values(1)

                open_tile(layer * 2, 0)
                for i in range(SPLIT):
                    pe.wait_ge(piece_used, pbase + i + 1 + RING)
                    project(i, *MIX.pieces[i][1:], tiles=[0])
                    if i == 1:
                        second_tile(layer * 2, 0)
                open_tile(layer * 2, 1)
                for i in range(SPLIT):
                    project(i, *MIX.pieces[i][1:], tiles=[1])

                for i, piece in enumerate(MIX.pieces):
                    if piece[0] == "mod" or i < SPLIT:
                        continue
                    j = MIX.split_no[i]
                    kind, n, h = piece
                    pe.wait_ge(piece_used, pbase + i + 1 + RING)
                    if kind == "in":
                        if n >= 2 and h == 0:
                            pe.wait_ge(proj_ready, layer * 8 + 2 * (n - 1))
                        project(j, n, h, BANK if n < 3 else BANK // 2)
                    elif kind == "gate":
                        if j == 13:
                            pe.wait_ge(small_loaded, layer * 64 + 64)
                            pe.wait_ge(pooled_ready, layer + 1)
                        if h == 0:
                            if n < 2:
                                pe.wait_ge(proj_ready, layer * 8 + 6 + 2 * n)
                            else:
                                pe.wait_ge(gate_ready, layer * 12 + 2 * (n - 1))
                        project(j, n, h)
                    elif kind == "branch":
                        if j == 19:
                            pe.wait_ge(yT_hi_ready, layer * 2 + 1)
                            pe.wait_ge(yT_lo_ready, layer * 2 + 1)
                            pe.wait_ge(gate_ready, layer * 12 + 12)
                        if j == 20:
                            pe.wait_ge(pT_ready, layer * 2 + 2)
                        if j == 21:
                            pe.wait_ge(yT_hi_ready, layer * 2 + 2)
                            pe.wait_ge(yT_lo_ready, layer * 2 + 2)
                        groups = {19: [(0, (0, 1), 0, 0), (1, (2, 3), 2, 0)], 20: [(0, (0, 1), 4, 0), (1, (2, 3), 0, 1)],
                                  21: [(2, (4, 5, 6, 7), 2, 2)], 22: [(2, (4, 5, 6, 7), 0, 3)]}[j]
                        for br, ks, first_bank, read in groups:
                            if read:
                                pe.wait_ge(branch_read, layer * 6 + read)
                            for t in range(TT):
                                for k in ks:
                                    ins = product(bank(first_bank + t), *chunk(k, t), *split_piece(j, k % 4, 0, BANK), k == ks[0], k == ks[-1])
                                    if j == 22 and t == 1 and k == 5:
                                        merged_T(0)
                        ins.then_inc(split_used, 1)
                    elif h == 0:
                        if n == 0:
                            pe.wait_ge(mT_hi_ready, layer * 2 + 1)
                            pe.wait_ge(mT_lo_ready, layer * 2 + 1)
                        if n == 0:
                            pe.wait_ge(branch_read, layer * 6 + 4)
                        for t in range(TT):
                            ins = project_out(j, n, h, t)
                        ins.then_inc(split_used, 1)
                        if n == 0:
                            merged_T(1)
                    elif n == 0:
                        continue
                    else:
                        pe.wait_ge(mT_hi_ready, layer * 2 + 2)
                        pe.wait_ge(mT_lo_ready, layer * 2 + 2)
                        for t in range(TT):
                            for m in range(2):
                                ins = project_out(j - 1 + m, m, h, t)
                                if t == TT - 1:
                                    ins.then_inc(split_used, 1)
                            if t == 0:
                                ins.then_inc(out_sent, 1)
                    after(j)
                open_sublayer(layer * 2 + 1, 0, 4)

                def swiglu(stretch, panels, piece_base, panel0, blocks, e=None, turn_places=None):
                    def turn(p):
                        pe.wait_ge(gated_ready, panel0 + p + 1)
                        for b in range(blocks):
                            for c in range(panels[p] // P):
                                ins = TR(ps[:, HW1 + 2 * b, c * P:(c + 1) * P], gated[:, b, c * P:(c + 1) * P], ident)
                        ins.then_inc(gT_sent, 1)

                    def up(j, kind, h, width, b):
                        ks = range(4 * h, 4 * h + 4) if width == BANK else range(KD)
                        for k in ks:
                            ins = product(bank({"A": HW1, "B": HW3}[kind] + 2 * b, width), *chunk(k, b), *split_piece(j, k - ks[0], 0, width),
                                          k == 0, k == KD - 1)
                        return ins

                    if e is None:
                        for b in range(blocks):
                            open_tile(1, b)
                            for i in range(SPLIT):
                                kind, p, h = stretch.pieces[i]
                                pe.wait_ge(piece_used, piece_base + i + 1 + RING)
                                ins = up(i, kind, h, panels[p], b)
                                if b == blocks - 1:
                                    ins.then_inc(split_used, 1)
                                if b == 0 and i == 1:
                                    second_tile(1, 4)

                    for i, (kind, p, *rest) in enumerate(stretch.pieces):
                        if kind == "mod" or (e is None and i < SPLIT):
                            continue
                        j, h = stretch.split_no[i], rest[0]
                        width = panels[p]
                        pe.wait_ge(piece_used, piece_base + i + 1 + RING)
                        if kind in "AB":
                            if kind == "A" and p == 1 and h == 0:
                                pe.wait_ge(silu_ready, panel0 + 1)
                            if kind == "B" and p and h == 0:
                                pe.wait_ge(gated_ready, panel0 + p)
                            for b in range(blocks):
                                ins = up(j, kind, h, width, b)
                            ins.then_inc(split_used, 1)
                            if turn_places and kind == "B" and h == 1 and p == 0:
                                turn_places()
                            if kind == "B" and h == 0 and p:
                                pe.wait_ge(silu_ready, panel0 + p + 1)
                                turn(p - 1)
                        else:
                            if turn_places and p == 0 and h == 0:
                                pe.wait_ge(place_ready, e + 1)
                            if h == 0:
                                pe.wait_ge(gT_hi_ready, panel0 + p + 1)
                                pe.wait_ge(gT_lo_ready, panel0 + p + 1)
                            chunks = width // P
                            for b in range(blocks):
                                for c in range(2):
                                    k = 2 * h + c
                                    for n in range(2):
                                        ins = product(bank(2 * b + n), gT_hi[:, b, k, :], gT_lo[:, b, k, :],
                                                      *split_piece(j, c, n * BANK, D), p == 0 and k == 0,
                                                      p == len(panels) - 1 and k == chunks - 1)
                            ins.then_inc(split_used, 1)
                            if p == len(panels) - 2 and h == chunks // 2 - 1:
                                turn(p + 1)

                with pe.If(layer < 1):
                    swiglu(DENSE, DENSE_PANELS, MOD0.n + MIX.n, 0, 2)
                    pe.wait_ge(piece_used, LAYER_PIECES + MOD0.n + RING)
                    open_sublayer(2, 4, 0)
                with pe.Else():
                    second_tile(3, 4)
                    open_tile(3, 0)
                    open_tile(3, 1)
                    pe.wait_ge(rt_lo, 1)
                    for t in range(TT):
                        for k in range(KD):
                            ins = product(ps[:, ROUTE, t * EXPERTS:(t + 1) * EXPERTS], *chunk(k, t), w_rt_hi[:, k, :], w_rt_lo[:, k, :], k == 0, k == KD - 1)
                    ins.then_inc(logits_sent, 1)
                    pe.wait_ge(sel_ready, 1)
                    sel = rt[:, 5]
                    to = ps[:, ROUTE + 1, :]
                    MM(to[:, 0:8], past, sel[:, 0, :], start=True, stop=True)
                    MM(to[:, 8:16], past, sel[:, 1, :], start=True, stop=False)
                    MM(to[:, 8:16], ones, sel[:, 0, :], start=False, stop=True)
                    MM(to[:, 16:24], ones, sel[:, 0, :], start=True, stop=False)
                    MM(to[:, 16:24], ones, sel[:, 1, :], start=False, stop=True).then_inc(pos_sent, 1)
                    pe.wait_ge(hh_ready, 1)
                    pe.wait_ge(hl_ready, 1)
                    pe.wait_ge(counts_ready, 1)
                    def gather(b, n):
                        for part, first_bank in ((h_hi, 4), (h_lo, 6)):
                            for k in range(KD):
                                to = ps[:, first_bank + k // 4, (k % 4) * P:(k % 4 + 1) * P]
                                for t in range(TT):
                                    ins = MM(to, part[:, t, k * P:(k + 1) * P], pick[:, t, b * P:(b + 1) * P], start=t == 0, stop=t == 1)
                        ins.then_inc(gathered[b], 1)

                    def second_block(e, n):
                        with pe.If(pe.value_load(counts_i[0:1, bass.ds(e, 1)], min_val=0, max_val=SEQ) > P):
                            pe.wait_ge(xg_hi_ready[0], n)
                            pe.wait_ge(xg_lo_ready[0], n)
                            gather(1, n)
                        with pe.Else():
                            pe.sem_inc(gathered[1], 1)

                    pe.wait_ge(pick_ready, 1)
                    gather(0, 1)
                    second_block(0, 1)
                    with pe.Fori(0, EXPERTS) as e:
                        count = pe.value_load(counts_i[0:1, bass.ds(e, 1)], min_val=0, max_val=SEQ)

                        def expert(blocks):
                            for b in range(blocks):
                                pe.wait_ge(xg_hi_ready[b], e + 1)
                                pe.wait_ge(xg_lo_ready[b], e + 1)

                            def turn_places():
                                pe.wait_ge(added, e * 4 + 4)
                                for b in range(blocks):
                                    for t in range(TT):
                                        ins = TR(ps[:, 0, b * SEQ + t * P:b * SEQ + (t + 1) * P], pick_w[:, t, b * P:(b + 1) * P], ident)
                                ins.then_inc(place_sent, 1)

                            swiglu(EXPERT, EXPERT_PANELS, e * EXPERT.n + (MOD0.n + LAYER_PIECES + MIX.n),
                                   e * len(EXPERT_PANELS) + len(DENSE_PANELS), blocks, e, turn_places)

                            def scatter():
                                pe.wait_ge(y_act, e + 1)
                                pe.wait_ge(y_dve, e + 1)
                                for t in range(TT):
                                    for c in range(2):
                                        for b in range(blocks):
                                            ins = MM(bank(2 * t + c), place[:, b, t * P:(t + 1) * P], hbuf[:, b, c * BANK:(c + 1) * BANK],
                                                     start=b == 0, stop=b == blocks - 1)
                                        ins.then_inc(scattered, 1)

                            with pe.If(e < EXPERTS - 1):
                                pe.wait_ge(pick_ready, e + 2)
                                gather(0, e + 2)
                                scatter()
                                second_block(e + 1, e + 2)
                            with pe.Else():
                                scatter()

                        with pe.If(count > P):
                            expert(2)
                        with pe.Else():
                            expert(1)


_INS = ['x', 'c', 'w_mod_mix', 'b_mod_mix', 'w_in', 'w_pool', 'pool_scale', 'sinks', 'w_gate', 'w_branch_a',
        'w_branch_b', 'w_branch_c', 'w_out', 'ln_mix_g', 'ln_mix_b', 'w_mod_ffn', 'b_mod_ffn', 'ffn_w1', 'ffn_w3',
        'ffn_w2', 'w_router', 'b_router', 'exp_w1', 'exp_w3', 'exp_w2', 'ln_ffn_g', 'ln_ffn_b']


def kernel(**inputs):
    import numpy as _np
    import concourse.bacc as _bacc
    from concourse import mybir as _mybir
    from concourse.bass_utils import run_bass_kernel_spmd as _run

    nc = _bacc.Bacc("TRN2", target_bir_lowering=False, num_devices=1)
    arrays, args = {}, {}
    for name in _INS:
        a = _np.ascontiguousarray(inputs[name])
        arrays[f"in_{name}_dram"] = a
        args[name] = nc.dram_tensor(f"in_{name}_dram", a.shape, _mybir.dt.from_np(a.dtype), kind="ExternalInput").ap()
    table = constants()
    arrays["constants_dram"] = table
    consts = nc.dram_tensor("constants_dram", table.shape, _mybir.dt.float32, kind="ExternalInput").ap()
    out = nc.dram_tensor("out_dram", (1, SEQ, D), _mybir.dt.float32, kind="ExternalOutput").ap()
    trunk(nc, args, consts, out)
    r = _run(nc, [arrays], core_ids=[0])
    return r.results[0]["out_dram"]
```

```python
from contextlib import ExitStack

import numpy as np

import concourse.bass as bass
from concourse import mybir

F32 = mybir.dt.float32
F32R = mybir.dt.float32r
I32 = mybir.dt.int32
ALU = mybir.AluOpType
ACT = mybir.ActivationFunctionType
AX_X = mybir.AxisListType.X

P = 128
D = 1024
KD = D // P
SEQ = 256
TT = SEQ // P
DEPTH = 2
HD = 64
HALF = HD // 2
SB_HEADS = 4
WINDOWS = (2, 4, 8, 16)
Q_HEADS, KV_HEADS = 8, 2
CHUNK = 64
D_FF, D_FFE, EXPERTS = 2816, 3584, 8
EPS = 1e-5
ALPHA = (2 * DEPTH) ** 0.25
SCALE = HD ** -0.5
FAR = -1e30
BANK = 512

QA, KA, VA, UB, QC, KC, VC = 0, 256, 512, 768, 1024, 1536, 1792
PROJ = 1920

SPILL = WINDOWS[-1]
BAND_W = 2 * P + SPILL
C_IDENT, C_ONES, C_PAST, C_TRI = 0, P, 2 * P, 3 * P
C_BAND = 4 * P
C_COS = C_BAND + len(WINDOWS) * BAND_W
C_SIN = C_COS + TT * HD
C_SWM = C_SIN + TT * HD
C_IOTA = C_SWM + P
CONSTS = C_IOTA + SEQ


def constants():
    c = np.zeros((P, CONSTS), np.float32)
    i = np.arange(P)
    c[:, C_IDENT:C_IDENT + P] = np.eye(P)
    c[:, C_ONES:C_ONES + P] = 1.0
    c[:, C_PAST:C_PAST + P] = i[:, None] < i[None, :]
    c[:, C_TRI:C_TRI + P] = i[:, None] >= i[None, :]
    j, s = np.arange(P)[:, None], np.arange(SEQ)[None, :]
    for g, w in enumerate(WINDOWS):
        own = ((s - j >= 0) & (s - j < w)) / np.minimum(s + 1.0, w)
        full = ((s - j >= 0) & (s - j < w)) / float(w)
        base = C_BAND + g * BAND_W
        c[:, base:base + P] = own[:, :P] - np.eye(P)
        c[:, base + P:base + 2 * P] = full[:, :P] - np.eye(P)
        c[:, base + 2 * P:base + BAND_W] = full[:, P:P + SPILL]
    inv = np.power(np.float32(10000.0), -np.arange(HALF, dtype=np.float32) / np.float32(HALF)).astype(np.float32)
    for t in range(TT):
        ang = (np.arange(P) + t * P).astype(np.float32)[:, None] * inv[None, :]
        cos, sin = np.cos(ang), np.sin(ang)
        c[:, C_COS + t * HD:C_COS + (t + 1) * HD] = np.concatenate([cos, cos], 1)
        c[:, C_SIN + t * HD:C_SIN + (t + 1) * HD] = np.concatenate([-sin, sin], 1)
    c[:HD, C_SWM + HD:C_SWM + P] = FAR
    c[:, C_IOTA:C_IOTA + SEQ] = np.arange(SEQ)
    return c


RING, SPLIT = 6, 3
PIECE = 2048
IN_PANELS = 4
GATE_PANELS = 3 * D // BANK
MODS = 12
MOD_SHIFT_SCALE = 8
MOD_BEFORE = (4, 5, 6, 7, 8, 13, 14, 15, 17, 18, 20, 22)


def mod_stream():
    return [("mod", q) for q in range(MODS)]


def mix_stream():
    s = [("in", n, h) for n in range(3) for h in range(2)] + [("in", 3, 0)]
    s += [("gate", q // 2, q % 2) for q in range(2 * GATE_PANELS)]
    s += [("branch", n, h) for h in range(2) for n in range(2)]
    s += [("out", n, h) for h in range(2) for n in range(2)]
    for q in reversed(range(MODS)):
        s.insert(MOD_BEFORE[q], ("mod", q))
    return s


def ffn_stream(width, mods):
    panels = [min(BANK, width - n) for n in range(0, width, BANK)]
    s = []
    for p, w in enumerate(panels):
        halves = w // (BANK // 2)
        s += [("A", p, h) for h in range(halves)] + [("B", p, h) for h in range(halves)]
        if p:
            s += [("C", p - 1, h) for h in range(2)]
    s += [("C", len(panels) - 1, h) for h in range(panels[-1] // (BANK // 2))]
    if mods:
        for q in reversed(range(MODS)):
            s.insert(2 * q + 5, ("mod", q))
    return panels, s


def last_turn_after(panels):
    return 0 if panels[-1] <= BANK // 2 else 1


class Stretch:

    def __init__(self, pieces):
        self.pieces = pieces
        self.loads, self.split_no = [], []
        landed, n = [0] * RING, 0
        for i, piece in enumerate(pieces):
            landed[i % RING] += 32 if piece[0] == "branch" and piece[2] == 0 else 16
            self.loads.append(landed[i % RING])
            self.split_no.append(None if piece[0] == "mod" else n)
            n += piece[0] != "mod"
        self.landed, self.n_split, self.n = landed, n, len(pieces)
        assert n % SPLIT == 0


MOD0 = Stretch(mod_stream())
MIX = Stretch(mix_stream())
DENSE_PANELS, _dense = ffn_stream(D_FF, True)
DENSE = Stretch(_dense)
EXPERT_PANELS, _expert = ffn_stream(D_FFE, False)
EXPERT = Stretch(_expert)
assert EXPERT.n % RING == 0
LAYER_PIECES = MIX.n + DENSE.n
LAYER_SPLITS = MIX.n_split + DENSE.n_split

BRANCH_ORDER = [(0, 0), (1, 0), (1, 1), (0, 1), (2, 0), (2, 1)]
HW1, HW3 = 4, 5
ROUTE = 0
LOGITS = 64
HALF_P = P // 2
FOLDS = 2 * len(EXPERT_PANELS)

DVE_MIX_STEPS, DVE_DENSE_STEPS, DVE_ROUTE_STEPS = 39, 22, 32
ACT_MIX_STEPS = 2


class Chain:

    def __init__(self, eng, sem, base=0):
        self.eng, self.sem, self.base, self.n = eng, sem, base, 0

    def step(self, ins):
        ins.then_inc(self.sem, 1)
        self.n += 1
        self.eng.wait_ge(self.sem, self.base + self.n)


def trunk(nc, I, consts, out):
    with ExitStack() as ctx:
        def sb(name, shape, dt=F32, scope=ctx):
            return scope.enter_context(nc.sbuf_tensor(name, shape, dt))

        def sem(name):
            return ctx.enter_context(nc.semaphore(name))

        w_raw = sb("w_raw", [P, RING, PIECE])
        w_hi = sb("w_hi", [P, SPLIT, PIECE], F32R)
        w_lo = sb("w_lo", [P, SPLIT, PIECE], F32R)
        x = sb("x_sb", [P, TT, D])
        hbuf = sb("hbuf", [P, TT, D])
        actT_hi = sb("actT_hi", [P, KD, SEQ], F32R)
        actT_lo = sb("actT_lo", [P, KD, SEQ], F32R)
        cst = sb("cst", [P, CONSTS])
        mod_acc = sb("mod_acc", [P, 3 * D])
        gate1 = sb("gate1", [P, D])
        c_act = sb("c_act", [P, KD])
        stats = sb("stats", [P, TT, 2, 6])
        mv = sb("mv", [P, TT, 2])
        veps = sb("veps", [P, TT])
        std = sb("std", [P, TT])
        rstd = sb("rstd", [P, TT])
        small = sb("small", [P, 64])
        sinks = sb("sinks_sb", [P, Q_HEADS])
        pool_scale = sb("pool_scale_sb", [P, 2])
        counts_i = sb("counts_i", [P, EXPERTS + 1], I32)

        w_rt = sb("w_rt", [P, KD, EXPERTS])
        b_rt = sb("b_rt", [P, EXPERTS])

        mix = ExitStack()
        lnrow = sb("lnrow", [P, 2, D], scope=mix)
        mix.close()
        cT = sb("cT", [P, 6, SEQ], scope=mix)
        scores = sb("scores", [P, Q_HEADS, P], scope=mix)
        probT = sb("probT", [P, Q_HEADS, P], scope=mix)
        proj = sb("proj", [P, TT, PROJ], scope=mix)
        gates = sb("gates", [P, TT, 3 * D], scope=mix)
        w_pool = sb("w_pool_sb", [P, 2, HD], scope=mix)
        v_even = sb("v_even", [P, P], scope=mix)
        mix.close()
        aT = sb("aT", [P, 4, SEQ], scope=mix)
        z = sb("z_sb", [P, 1536], scope=mix)
        mix.close()
        soft = hbuf[:, :, :].rearrange("p t d -> p (t d)")[:, 0:1536]
        yT = hbuf[:, :, :].rearrange("p t d -> p (t d)").rearrange("p (k q) -> p k q", k=KD)
        ffn = ExitStack()
        h_hi = sb("h_hi", [P, TT, D], F32R, scope=ffn)
        h_lo = sb("h_lo", [P, TT, D], F32R, scope=ffn)
        yacc = sb("yacc", [P, TT, D], scope=ffn)
        silu = sb("silu", [P, 2, BANK], scope=ffn)
        gated = sb("gated", [P, 2, BANK], scope=ffn)
        fold = sb("fold", [HALF_P, 2, BANK], scope=ffn)
        gT_hi = sb("gT_hi", [P, 2, 4, P], F32R, scope=ffn)
        gT_lo = sb("gT_lo", [P, 2, 4, P], F32R, scope=ffn)
        pick = sb("pick", [P, TT, SEQ], F32R, scope=ffn)
        pick_w = sb("pick_w", [P, TT, SEQ], scope=ffn)
        place = sb("place", [P, 2, SEQ], scope=ffn)
        w_rt_hi = sb("w_rt_hi", [P, KD, EXPERTS], F32R, scope=ffn)
        w_rt_lo = sb("w_rt_lo", [P, KD, EXPERTS], F32R, scope=ffn)
        rt = sb("rt", [P, 8, TT, EXPERTS], scope=ffn)
        rs = sb("rs", [P, 8, TT, 1], scope=ffn)
        posm = sb("posm", [P, TT, EXPERTS + 1], scope=ffn)
        wsel = sb("wsel", [P, TT, EXPERTS + 1], scope=ffn)
        ffn.close()

        ps = ctx.enter_context(nc.psum_tensor("ps", [P, 8, BANK], F32))

        ident = cst[:, C_IDENT:C_IDENT + P]
        ones = cst[:, C_ONES:C_ONES + P]
        past = cst[:, C_PAST:C_PAST + P]
        tri = cst[:, C_TRI:C_TRI + P]
        iota = cst[:, C_IOTA:C_IOTA + SEQ]
        sw_mask = cst[:, C_SWM:C_SWM + P]

        raw_loaded = [sem(f"raw_loaded{i}") for i in range(RING)]
        piece_used = sem("piece_used")
        split_hi = sem("split_hi")
        split_used = sem("split_used")
        mod_step = sem("mod_step")
        acc_ready = sem("acc_ready")
        x_loaded, c_loaded, cst_loaded = sem("x_loaded"), sem("c_loaded"), sem("cst_loaded")
        tables_loaded, first_bias_loaded = sem("tables_loaded"), sem("first_bias_loaded")
        small_loaded, ln_loaded, rt_loaded = sem("small_loaded"), sem("ln_loaded"), sem("rt_loaded")
        acc_free, acc_zero, yacc_zero = sem("acc_free"), sem("acc_zero"), sem("yacc_zero")
        c_ready = sem("c_ready")
        out_stored = sem("out_stored")
        var_ready, std_ready = sem("var_ready"), sem("std_ready")
        mod_sent = sem("mod_sent")
        gate_sent, scale_ready, gate1_ready = sem("gate_sent"), sem("scale_ready"), sem("gate1_ready")
        h_ready, hT_sent, hT_hi_ready, hT_lo_ready = sem("h_ready"), sem("hT_sent"), sem("hT_hi_ready"), sem("hT_lo_ready")
        x_ready = sem("x_ready")
        dve_start, dve_mix, dve_ffn, act_mix = sem("dve_start"), sem("dve_mix"), sem("dve_ffn"), sem("act_mix")
        proj_ready, aT_sent, aT_ready = sem("proj_ready"), sem("aT_sent"), sem("aT_ready")
        z_sent, z_ready, softplus_ready, soft_ready = sem("z_sent"), sem("z_ready"), sem("softplus_ready"), sem("soft_ready")
        suffix_sent, logw_ready, expw_ready, w_ready = sem("suffix_sent"), sem("logw_ready"), sem("expw_ready"), sem("w_ready")
        ya_sent, ya_ready = sem("ya_sent"), sem("ya_ready")
        rope_ready, cT_sent, cT_ready = sem("rope_ready"), sem("cT_sent"), sem("cT_ready")
        pool_sent, pooled_ready, yb_sent, yb_ready = sem("pool_sent"), sem("pooled_ready"), sem("yb_sent"), sem("yb_ready")
        sc_sent, sc_ready, exp_ready, prob_ready = sem("sc_sent"), sem("sc_ready"), sem("exp_ready"), sem("prob_ready")
        pT_sent, pT_ready, yc_sent, yc_ready = sem("pT_sent"), sem("pT_ready"), sem("yc_sent"), sem("yc_ready")
        v_ready, gate_ready = sem("v_ready"), sem("gate_ready")
        branch_read, out_sent, y_sent = sem("branch_read"), sem("out_sent"), sem("y_sent")
        yT_hi_ready, yT_lo_ready = sem("yT_hi_ready"), sem("yT_lo_ready")
        merged_ready, mT_sent, mT_hi_ready, mT_lo_ready = sem("merged_ready"), sem("mT_sent"), sem("mT_hi_ready"), sem("mT_lo_ready")
        silu_ready, gated_ready = sem("silu_ready"), sem("gated_ready")
        packed_ready = sem("packed_ready")
        fold_copied, fold_added = sem("fold_copied"), sem("fold_added")
        gT_sent, gT_hi_ready, gT_lo_ready = sem("gT_sent"), sem("gT_hi_ready"), sem("gT_lo_ready")
        hh_ready, hl_ready, rt_hi, rt_lo = sem("hh_ready"), sem("hl_ready"), sem("rt_hi"), sem("rt_lo")
        logitsT_sent, logitsT_ready = sem("logitsT_sent"), sem("logitsT_ready")
        logits_sent, gap_ready, e2_ready, sel_ready = sem("logits_sent"), sem("gap_ready"), sem("e2_ready"), sem("sel_ready")
        pos_sent, counts_ready = sem("pos_sent"), sem("counts_ready")
        place_copied = sem("place_copied")
        pick_ready, place_sent, place_ready = sem("pick_ready"), sem("place_sent"), sem("place_ready")
        gathered_hi = [sem(f"gathered_hi{b}") for b in range(2)]
        gathered_lo = [sem(f"gathered_lo{b}") for b in range(2)]
        xg_hi_ready = [sem(f"xg_hi_ready{b}") for b in range(2)]
        xg_lo_ready = [sem(f"xg_lo_ready{b}") for b in range(2)]
        y_act, y_dve, scattered, added = sem("y_act"), sem("y_dve"), sem("scattered"), sem("added")

        block = ctx.enter_context(nc.Block())

        def weight_rows(w):
            return w.rearrange("(k p) n -> p k n", p=P)

        def bank(b, n=BANK):
            return ps[:, b, 0:n]

        @block.sync
        def _(sp):
            sp.sem_inc(piece_used, RING)
            sp.sem_inc(split_used, SPLIT)

            def load(slot, piece, layer, expert=None):
                kind, a, h = piece[0], piece[1], piece[-1]
                dst = w_raw[:, slot, :]
                d4, d8 = dst.rearrange("p (k n) -> p k n", k=4), dst.rearrange("p (k n) -> p k n", k=8)
                d2 = dst.rearrange("p (k n) -> p k n", k=2)
                if kind == "mod":
                    w = I["w_mod_ffn"] if layer[0] == "ffn" else I["w_mod_mix"]
                    src = weight_rows(w[layer[1]])
                    pairs = [(d2, src[:, 2 * (a % 4):2 * (a % 4) + 2, D * (a // 4):D * (a // 4 + 1)])]
                elif kind == "branch":
                    cols = slice(a * BANK, (a + 1) * BANK)
                    if h == 0:
                        pairs = [(d4[:, 0:2, :], weight_rows(I["w_branch_a"][layer])[:, :, cols]),
                                 (d4[:, 2:4, :], weight_rows(I["w_branch_b"][layer])[:, :, cols])]
                    else:
                        pairs = [(d4, weight_rows(I["w_branch_c"][layer])[:, :, cols])]
                elif kind == "C":
                    w = I["ffn_w2"][0] if expert is None else I["exp_w2"][0, expert]
                    pairs = [(d2, weight_rows(w)[:, 4 * a + 2 * h:4 * a + 2 * h + 2, :])]
                else:
                    w = {"in": lambda: I["w_in"][layer], "gate": lambda: I["w_gate"][layer],
                         "out": lambda: I["w_out"][layer],
                         "A": lambda: I["ffn_w1"][0] if expert is None else I["exp_w1"][0, expert],
                         "B": lambda: I["ffn_w3"][0] if expert is None else I["exp_w3"][0, expert]}[kind]()
                    width = w.shape[-1]
                    c0, c1 = a * BANK, min((a + 1) * BANK, width)
                    if c1 - c0 == BANK:
                        pairs = [(d4, weight_rows(w)[:, 4 * h:4 * h + 4, c0:c1])]
                    else:
                        pairs = [(d8, weight_rows(w)[:, :, c0:c1])]
                for d, s in pairs:
                    sp.dma_start(d, s).then_inc(raw_loaded[slot], 16)

            def stream(stretch, base, layer, expert=None, mod_layer=None, gap=0):
                for i, piece in enumerate(stretch.pieces):
                    before = base - RING + i + 1 + (gap if i < RING // 2 else 0)
                    sp.wait_ge(piece_used, before + RING)
                    load(i % RING, piece, mod_layer if piece[0] == "mod" else layer, expert)

            sp.dma_start(cst[:, 0:C_PAST], consts[:, 0:C_PAST]).then_inc(cst_loaded, 16)
            sp.dma_start(c_act[:, :], I["c"].rearrange("b (k p) -> p (b k)", p=P),
                         allow_slow_non_contiguous=True).then_inc(c_loaded, 16)
            xv = I["x"].rearrange("b (t p) d -> p (b t) d", p=P)
            sp.dma_start(x[:, :, :], xv).then_inc(x_loaded, 16)
            sp.wait_ge(acc_zero, 1)
            sp.dma_start(mod_acc[0:1, :], I["b_mod_mix"][0:1, :]).then_inc(first_bias_loaded, 16)
            stream(MOD0, 0, None, mod_layer=("mix", 0))
            with sp.Fori(0, DEPTH) as layer:
                stream(MIX, layer * LAYER_PIECES + MOD0.n, layer, mod_layer=("ffn", layer), gap=layer * (RING // 2))
                with sp.If(layer < 1):
                    stream(DENSE, MOD0.n + MIX.n, 0, mod_layer=("mix", 1), gap=RING // 2)
                with sp.Else():
                    moe0 = MOD0.n + LAYER_PIECES + MIX.n
                    sp.wait_ge(piece_used, moe0 + RING)
                    with sp.Fori(0, EXPERTS) as e:
                        stream(EXPERT, e * EXPERT.n + moe0, 1, expert=e)
            for t in range(TT):
                sp.wait_ge(x_ready, 2 * DEPTH + 1 + t)
                sp.dma_start(out.rearrange("b (t p) d -> p (b t) d", p=P)[:, t, :], x[:, t, :]).then_inc(out_stored, 16)
            sp.wait_ge(out_stored, TT * 16)

        @block.gpsimd
        def _(gp):
            def fresh_acc(bias_row, n):
                nc.gpsimd.memset(mod_acc[:, :], 0.0).then_inc(acc_zero, 1)
                gp.wait_ge(acc_zero, n + 1)
                gp.dma_start(mod_acc[0:1, :], bias_row).then_inc(acc_ready, 16)

            def ln_rows(g, b):
                gp.dma_start(lnrow[:, 0, :], g.partition_broadcast(P)).then_inc(ln_loaded, 16)
                gp.dma_start(lnrow[:, 1, :], b.partition_broadcast(P)).then_inc(ln_loaded, 16)

            nc.gpsimd.memset(mod_acc[:, :], 0.0).then_inc(acc_zero, 1)
            gp.dma_start(w_rt[:, :, :], I["w_router"][0].rearrange("(k p) e -> p k e", p=P)).then_inc(rt_loaded, 16)
            gp.dma_start(b_rt[:, :], I["b_router"][0].partition_broadcast(P)).then_inc(rt_loaded, 16)
            gp.wait_ge(piece_used, RING + MODS)
            gp.dma_start(cst[:, C_PAST:], consts[:, C_PAST:]).then_inc(tables_loaded, 16)
            with gp.Fori(0, DEPTH) as layer:
                gp.wait_ge(gate1_ready, layer * 2 + 1)
                gp.dma_start(sinks[:, :], I["sinks"][bass.ds(layer, 1), :].rearrange("a h -> (a h)").partition_broadcast(P)).then_inc(small_loaded, 16)
                gp.dma_start(pool_scale[:, :], I["pool_scale"][bass.ds(layer, 1), :].rearrange("a (k p) -> p (a k)", p=P),
                             allow_slow_non_contiguous=True).then_inc(small_loaded, 16)
                for par in range(2):
                    gp.dma_start(w_pool[par * HD:(par + 1) * HD, :, :],
                                 I["w_pool"][bass.ds(layer, 1)].rearrange("a (k r) c e -> c r (a k) e", r=2)[:, par],
                                 ).then_inc(small_loaded, 16)
                gp.wait_ge(gate_sent, layer * 2 + 1)
                gp.sem_inc(acc_free, 1)
                fresh_acc(I["b_mod_ffn"][bass.ds(layer, 1), :], layer * 2 + 1)
                gp.wait_ge(merged_ready, layer * 4 + 4)
                ln_rows(I["ln_mix_g"][bass.ds(layer, 1), :].rearrange("a d -> (a d)"),
                        I["ln_mix_b"][bass.ds(layer, 1), :].rearrange("a d -> (a d)"))
                with gp.If(layer < 1):
                    gp.wait_ge(gate_sent, 2)
                    fresh_acc(I["b_mod_mix"][1:2, :], 2)
                    gp.wait_ge(x_ready, 2)
                    ln_rows(I["ln_ffn_g"][0], I["ln_ffn_b"][0])
                with gp.Else():
                    gp.wait_ge(x_ready, 4)
                    nc.gpsimd.memset(yacc[:, :, :], 0.0).then_inc(yacc_zero, 1)
                    for b in range(2):
                        gp.wait_ge(gathered_lo[b], EXPERTS)
                    ln_rows(I["ln_ffn_g"][1], I["ln_ffn_b"][1])

        @block.scalar
        def _(act):
            A = nc.scalar.activation

            def round_piece(stretch, i, load_base, split_base):
                j = stretch.split_no[i]
                act.wait_ge(raw_loaded[i % RING], load_base[i % RING] + stretch.loads[i])
                act.wait_ge(split_used, split_base + j + 1)
                nc.scalar.copy(w_hi[:, j % SPLIT, :], w_raw[:, i % RING, :]).then_inc(split_hi, 1)

            def stream(stretch, load_base, split_base, after):
                for i, piece in enumerate(stretch.pieces):
                    if piece[0] == "mod" or i < SPLIT:
                        continue
                    j = stretch.split_no[i]
                    after(j - SPLIT)
                    round_piece(stretch, i, load_base, split_base)
                for j in range(stretch.n_split - SPLIT, stretch.n_split):
                    after(j)

            def root(n, t):
                act.wait_ge(var_ready, n)
                A(std[:, t:t + 1], veps[:, t:t + 1], ACT.Sqrt).then_inc(std_ready, 1)

            def one_plus_scale(sub, free):
                act.wait_ge(mod_sent, sub + 1)
                for c in range(2):
                    ins = A(bank(free + 2 + c), bank(free + 2 + c), ACT.Identity, bias=1.0)
                ins.then_inc(scale_ready, 1)

            def one_plus_gate(sub, held):
                act.wait_ge(gate_sent, sub + 1)
                for c in range(2):
                    ins = A(gate1[:, c * BANK:(c + 1) * BANK], bank(held + 2 + c), ACT.Identity, bias=1.0)
                ins.then_inc(gate1_ready, 1)

            def round_h(sub, t, held):
                for c in range(2):
                    act.wait_ge(hT_sent, sub * 4 + 2 * t + c + 1)
                    A(actT_hi[:, 4 * c:4 * c + 4, t * P:(t + 1) * P],
                      bank(held + 2 * t + c).rearrange("p (k q) -> p k q", k=4), ACT.Copy).then_inc(hT_hi_ready, 1)

            def norms(sub, n, free, held, ahead):
                ahead(0)
                root(n + 1, 0)
                ahead(1)
                root(n + 2, 0)
                one_plus_scale(sub, free)
                root(n + 3, 1)
                ahead(2)
                round_h(sub, 0, held)
                root(n + 4, 1)
                one_plus_gate(sub, held)
                round_h(sub, 1, held)

            act.wait_ge(c_loaded, 16)
            A(c_act[:, :], c_act[:, :], ACT.Silu).then_inc(c_ready, 1)
            for t in range(TT):
                root(t + 1, t)
            one_plus_scale(0, 4)
            round_h(0, 0, 0)
            round_piece(MIX, 0, MOD0.landed, 0)
            round_piece(MIX, 1, MOD0.landed, 0)
            round_piece(MIX, 2, MOD0.landed, 0)
            one_plus_gate(0, 0)
            round_h(0, 1, 0)

            with act.Fori(0, DEPTH) as layer:
                sbase = layer * LAYER_SPLITS
                chain = Chain(act, act_mix, layer * ACT_MIX_STEPS)

                def used(j):
                    act.wait_ge(split_used, sbase + j + 1 + SPLIT)

                def exp_scores(t):
                    act.wait_ge(sc_ready, layer * 2 + t + 1)
                    A(scores[:, :, :], scores[:, :, :], ACT.Exp)
                    A(small[:, 16:24], small[:, 16:24], ACT.Exp).then_inc(exp_ready, 1)

                def probs_T(t):
                    act.wait_ge(pT_sent, layer * 2 + t + 1)
                    A(probT[:, :, :], ps[:, 4:6, :].rearrange("p b (i q) -> p (b i) q", q=P), ACT.Copy).then_inc(pT_ready, 1)

                def yc_out(t):
                    act.wait_ge(yc_sent, layer * 2 + t + 1)
                    A(yT[:, 4:8, t * P:(t + 1) * P], bank(6).rearrange("p (i q) -> p i q", q=P), ACT.Copy).then_inc(yc_ready, 1)

                def after(j):
                    if j in (1, 3, 5):
                        used(j)
                        n = j // 2
                        for t in range(TT):
                            A(proj[:, t, n * BANK:(n + 1) * BANK], bank(2 * t + n % 2), ACT.Copy).then_inc(proj_ready, 1)
                    if j == 4:
                        act.wait_ge(aT_sent, layer + 1)
                        for b in range(2):
                            A(aT[:, 2 * b:2 * b + 2, :], bank(4 + b).rearrange("p (c q) -> p c q", c=2), ACT.Copy,
                              scale=1.0 if b else SCALE).then_inc(aT_ready, 1)
                    if j == 5:
                        act.wait_ge(z_sent, layer + 1)
                        A(z[:, 0:1024], ps[:, 4:6, :].rearrange("p b q -> p (b q)"), ACT.Copy)
                        A(z[:, 1024:1536].rearrange("p (b q) -> p b q", b=2), ps[:, 6:8, 0:256], ACT.Copy).then_inc(z_ready, 1)
                        act.wait_ge(z_ready, layer + 1)
                        chain.step(A(soft, z[:, :], ACT.Abs))
                    if j == 6:
                        used(j)
                        for t in range(TT):
                            twice = proj[:, t, KC:VC].rearrange("p (g r d) -> p r g d", g=2, r=2)
                            for r in range(2):
                                A(twice[:, r], bank(2 * t + 1)[:, 0:P].rearrange("p (g d) -> p g d", g=2), ACT.Copy)
                            A(proj[:, t, VC:PROJ], bank(2 * t + 1)[:, P:2 * P], ACT.Copy).then_inc(proj_ready, 1)
                        chain.step(A(soft, soft, ACT.Exp, scale=-1.0))
                    if j == 7:
                        A(soft, soft, ACT.Ln, bias=1.0).then_inc(softplus_ready, 1)
                    if j == 10:
                        act.wait_ge(logw_ready, layer + 1)
                        A(z[:, :], z[:, :], ACT.Exp).then_inc(expw_ready, 1)
                    if j == 11:
                        act.wait_ge(cT_sent, layer + 1)
                        act.wait_ge(ya_sent, layer + 1)
                        for b in range(3):
                            A(cT[:, 2 * b:2 * b + 2, :], bank(4 + b).rearrange("p (c q) -> p c q", c=2), ACT.Copy,
                              scale=SCALE if b < 2 else 1.0).then_inc(cT_ready, 1)
                        A(yT[:, 0:2, :], bank(7).rearrange("p (k q) -> p k q", k=2), ACT.Copy).then_inc(ya_ready, 1)
                    if j == 12:
                        act.wait_ge(pool_sent, layer + 1)
                        A(proj[:, :, QA:KA], bank(7).rearrange("p (k q) -> p k q", k=2), ACT.Copy).then_inc(pooled_ready, 1)
                        A(v_even[0:HD, :], proj[0:HD, 1, VC:PROJ], ACT.Copy)
                        A(v_even[HD:P, :], proj[HD:P, 0, VC:PROJ], ACT.Copy).then_inc(v_ready, 1)
                    if j == 13:
                        exp_scores(0)
                    if j == 14:
                        probs_T(0)
                        act.wait_ge(yb_sent, layer + 1)
                        for k in range(2):
                            ins = A(yT[:, 2 + k, :], bank(7)[:, k * 256:(k + 1) * 256], ACT.Copy, scale=pool_scale[:, k:k + 1])
                        ins.then_inc(yb_ready, 1)
                    if j == 15:
                        yc_out(0)
                    if j == 18:
                        yc_out(1)
                    if j == 16:
                        exp_scores(1)
                    if j == 17:
                        probs_T(1)
                    if j >= 8 and j % 2 == 0 and j <= 18:
                        used(j)
                        g = (j - 8) // 2
                        for t in range(TT):
                            A(gates[:, t, g * BANK:(g + 1) * BANK], bank(2 * t + g % 2), ACT.Sigmoid).then_inc(gate_ready, 1)
                    if j == 17:
                        used(17)
                        act.wait_ge(ya_ready, layer + 1)
                        act.wait_ge(yb_ready, layer + 1)
                        A(actT_hi[:, 0:4, :], yT[:, 0:4, :], ACT.Copy).then_inc(yT_hi_ready, 1)
                    if j == 19:
                        act.wait_ge(yc_ready, layer * 2 + 2)
                        A(actT_hi[:, 4:8, :], yT[:, 4:8, :], ACT.Copy).then_inc(yT_hi_ready, 1)
                    if j == 22:
                        merged_T(0)
                    if j == 23:
                        merged_T(1)

                def merged_T(n):
                    act.wait_ge(mT_sent, layer * 2 + n + 1)
                    A(actT_hi[:, 4 * n:4 * n + 4, :].rearrange("p k (t q) -> p t k q", t=TT),
                      ps[:, 2 - 2 * n:4 - 2 * n, :].rearrange("p t (k q) -> p t k q", k=4), ACT.Copy).then_inc(mT_hi_ready, 1)

                layer_loads = [MIX.landed[s] + DENSE.landed[s] for s in range(RING)]
                stream(MIX, [layer * layer_loads[s] + MOD0.landed[s] for s in range(RING)], sbase, after)
                assert chain.n == ACT_MIX_STEPS, chain.n
                norms(layer * 2 + 1, layer * 8 + 2, 0, 4,
                      lambda i: round_piece(DENSE, i, [layer * layer_loads[s] + MOD0.landed[s] + MIX.landed[s] for s in range(RING)],
                                            sbase + MIX.n_split))

                def panel_events(stretch, panels, split_base, panel0, blocks, folds=None):
                    first_b = {stretch.split_no[i]: p[1] for i, p in enumerate(stretch.pieces) if p[0] == "B" and p[2] == 0}
                    last = {(p[0], p[1]): stretch.split_no[i] for i, p in enumerate(stretch.pieces) if p[0] != "mod"}
                    last = {v: k for k, v in last.items()}
                    last_turn = stretch.split_no[stretch.pieces.index(("C", len(panels) - 2, last_turn_after(panels)))]

                    def gT_part(p):
                        act.wait_ge(gT_sent, panel0 + p + 1)
                        w = panels[p]
                        for b in range(blocks):
                            n = HALF_P if b and folds is not None else P
                            ins = A(gT_hi[:, b, 0:w // P, 0:n], ps[:, HW1 + 2 * b, 0:w].rearrange("p (c q) -> p c q", q=P)[:, :, 0:n], ACT.Copy)
                        ins.then_inc(gT_hi_ready, 1)

                    def after(j):
                        kind, p = last.get(j, ("", 0))
                        if kind == "A":
                            act.wait_ge(split_used, split_base + j + 1 + SPLIT)
                            if p:
                                act.wait_ge(gated_ready, panel0 + p)
                            w = panels[p]
                            if folds is not None:
                                A(fold[:, 0, 0:w], ps[HALF_P:P, HW1 + 2, 0:w], ACT.Copy).then_inc(fold_copied, 1)
                            for b in range(1 if folds is not None else blocks):
                                ins = A(silu[:, b, 0:w], ps[:, HW1 + 2 * b, 0:w], ACT.Silu)
                            if folds is not None:
                                act.wait_ge(fold_added, folds + 2 * p + 1)
                                ins = A(silu[0:HALF_P, 1, 0:w], fold[:, 0, 0:w], ACT.Silu)
                            ins.then_inc(silu_ready, 1)
                        if kind == "B" and folds is not None:
                            act.wait_ge(split_used, split_base + j + 1 + SPLIT)
                            A(fold[:, 1, 0:panels[p]], ps[HALF_P:P, HW3 + 2, 0:panels[p]], ACT.Copy).then_inc(fold_copied, 1)
                        if j in first_b and first_b[j]:
                            gT_part(first_b[j] - 1)
                        if j == last_turn:
                            gT_part(len(panels) - 1)

                    return after

                with act.If(layer < 1):
                    stream(DENSE, [MOD0.landed[s] + MIX.landed[s] for s in range(RING)], MIX.n_split,
                           panel_events(DENSE, DENSE_PANELS, MIX.n_split, 0, 2))
                    norms(2, 6, 4, 0, lambda i: round_piece(MIX, i, [layer_loads[s] + MOD0.landed[s] for s in range(RING)], LAYER_SPLITS))
                with act.Else():
                    act.wait_ge(rt_loaded, 32)
                    A(w_rt_hi[:, :, :], w_rt[:, :, :], ACT.Copy).then_inc(rt_hi, 1)
                    for t in range(TT):
                        ins = A(h_hi[:, t, :], hbuf[:, t, :], ACT.Copy)
                    ins.then_inc(hh_ready, 1)
                    act.wait_ge(logitsT_sent, 1)
                    A(place[0:EXPERTS, 0, :], ps[0:EXPERTS, ROUTE, 0:SEQ], ACT.Copy).then_inc(logitsT_ready, 1)
                    act.wait_ge(gap_ready, 1)
                    A(rs[:, 4], rs[:, 3], ACT.Exp).then_inc(e2_ready, 1)
                    act.wait_ge(counts_ready, 1)
                    moe_loads = [MOD0.landed[s] + 2 * MIX.landed[s] + DENSE.landed[s] for s in range(RING)]
                    moe_splits = LAYER_SPLITS + MIX.n_split

                    def round_expert_piece(i, e):
                        ahead, i = divmod(i, EXPERT.n)
                        round_piece(EXPERT, i, [e * EXPERT.landed[s] + moe_loads[s] + ahead * EXPERT.landed[s] for s in range(RING)],
                                    e * EXPERT.n_split + (moe_splits + ahead * EXPERT.n_split))

                    def gathered_rows(b, n):
                        act.wait_ge(gathered_hi[b], n)
                        A(actT_hi[:, :, b * P:(b + 1) * P],
                          ps[:, 4:6, :].rearrange("p c (k q) -> p (c k) q", q=P), ACT.Copy).then_inc(xg_hi_ready[b], 1)

                    def second_block(e, n):
                        with act.If(act.value_load(counts_i[0:1, bass.ds(e, 1)], min_val=0, max_val=SEQ) > P):
                            gathered_rows(1, n)
                        with act.Else():
                            act.sem_inc(xg_hi_ready[1], 1)

                    gathered_rows(0, 1)
                    second_block(0, 1)
                    with act.Fori(0, EXPERTS) as e:
                        count = act.value_load(counts_i[0:1, bass.ds(e, 1)], min_val=0, max_val=SEQ)

                        def expert(blocks, packed=False):
                            after = panel_events(EXPERT, EXPERT_PANELS, e * EXPERT.n_split + moe_splits,
                                                 e * len(EXPERT_PANELS) + len(DENSE_PANELS), blocks, e * FOLDS if packed else None)
                            if not packed:
                                act.sem_inc(fold_copied, FOLDS)
                            for i in range(SPLIT, EXPERT.n):
                                after(i - SPLIT)
                                if i - SPLIT == 3:
                                    act.wait_ge(place_sent, e + 1)
                                    ins = A(place[:, 0:blocks, :], ps[:, 0, 0:blocks * SEQ].rearrange("p (b q) -> p b q", q=SEQ), ACT.Copy)
                                    if packed:
                                        ins.then_inc(place_copied, 1)
                                        act.wait_ge(place_copied, e + 1)
                                        ins = A(place[HALF_P:P, 1, :], ps[0:HALF_P, 0, SEQ:2 * SEQ], ACT.Copy)
                                    else:
                                        act.sem_inc(place_copied, 1)
                                    ins.then_inc(place_ready, 1)
                                round_expert_piece(i, e)

                            def tail(last):
                                for n in range(SPLIT):
                                    after(EXPERT.n - SPLIT + n)
                                    if n == SPLIT - 1:
                                        act.wait_ge(split_used, e * EXPERT.n_split + (moe_splits + EXPERT.n_split + SPLIT))
                                        for b in range(blocks):
                                            ins = A(hbuf[:, b, 0:BANK], bank(2 * b), ACT.Copy)
                                        ins.then_inc(y_act, 1)
                                    if not last:
                                        round_expert_piece(EXPERT.n + n, e)
                                if not last:
                                    gathered_rows(0, e + 2)
                                    second_block(e + 1, e + 2)

                            with act.If(e < EXPERTS - 1):
                                tail(False)
                            with act.Else():
                                tail(True)

                        with act.If(count > P):
                            with act.If(count > P + HALF_P):
                                expert(2)
                            with act.Else():
                                expert(2, packed=True)
                        with act.Else():
                            expert(1)
                    for t in range(TT):
                        root(15 + t, t)

        @block.vector
        def _(dve):
            TS, TTn, STT, RED = nc.vector.tensor_scalar, nc.vector.tensor_tensor, nc.vector.scalar_tensor_tensor, nc.vector.tensor_reduce

            def rest_of_piece(stretch, i, split_base):
                j = stretch.split_no[i]
                dve.wait_ge(split_hi, split_base + j + 1)
                TTn(w_lo[:, j % SPLIT, :], w_raw[:, i % RING, :], w_hi[:, j % SPLIT, :].bitcast(F32),
                    ALU.subtract).then_inc(piece_used, 1)

            def mod_piece(stretch, i, load_base, piece_base, step_base, acc_no):
                q = stretch.pieces[i][1]
                if q == 0:
                    if stretch is MOD0:
                        dve.wait_ge(first_bias_loaded, 16)
                    else:
                        dve.wait_ge(acc_ready, acc_no * 16)
                    dve.wait_ge(c_ready, 1)
                dve.wait_ge(raw_loaded[i % RING], load_base[i % RING] + stretch.loads[i])
                w = w_raw[:, i % RING, :].rearrange("p (k n) -> p k n", k=2)
                previous = max((m for m in range(i) if stretch.pieces[m][0] == "mod"), default=None)
                for m in range(4):
                    k, n = m // 2, m % 2
                    acc = mod_acc[:, (q // 4) * D + n * BANK:(q // 4) * D + (n + 1) * BANK]
                    if m == 0 and q:
                        dve.wait_ge(mod_step, step_base + 3 * q)
                    if m == 1 and q:
                        dve.wait_ge(piece_used, piece_base + previous + 1 + RING)
                    if m >= 2:
                        dve.wait_ge(mod_step, step_base + 3 * q + m - 1)
                    ins = STT(acc, w[:, k, n * BANK:(n + 1) * BANK], c_act[:, 2 * (q % 4) + k:2 * (q % 4) + k + 1], acc,
                              ALU.mult, ALU.add)
                    ins.then_inc(piece_used if m == 3 else mod_step, 1)

            def stream(stretch, load_base, split_base, piece_base, step_base, acc_no, after):
                for i, piece in enumerate(stretch.pieces):
                    if piece[0] == "mod":
                        mod_piece(stretch, i, load_base, piece_base, step_base, acc_no)
                        continue
                    if i < SPLIT:
                        continue
                    j = stretch.split_no[i]
                    after(j - SPLIT)
                    rest_of_piece(stretch, i, split_base)
                for j in range(stretch.n_split - SPLIT, stretch.n_split):
                    after(j)

            def statistics(chain, src, t):
                for c in range(2):
                    ins = nc.vector.bn_stats(stats[:, t, c, :], src[:, t, c * BANK:(c + 1) * BANK])
                chain.step(ins)
                nc.vector.memset(veps[:, t:t + 1], 0.0)
                chain.step(nc.vector.bn_aggr(mv[:, t, :], stats[:, t, :, :].rearrange("p c s -> p (c s)")))
                TS(veps[:, t:t + 1], mv[:, t, 1:2], EPS, None, ALU.add).then_inc(var_ready, 1)

            def inverse_std(chain, n, t):
                dve.wait_ge(std_ready, n)
                chain.step(nc.vector.reciprocal(rstd[:, t:t + 1], std[:, t:t + 1]))

            def halves(t):
                return [hbuf[:, t, c * BANK:(c + 1) * BANK] for c in range(2)]

            def residual(chain, f, t):
                for c, part in enumerate(halves(t)):
                    ins = TTn(part, f(t, c), gate1[:, c * BANK:(c + 1) * BANK], ALU.mult)
                chain.step(ins)
                for c, part in enumerate(halves(t)):
                    ins = STT(part, x[:, t, c * BANK:(c + 1) * BANK], ALPHA, part, ALU.mult, ALU.add)
                chain.step(ins)

            def layer_norm(chain, t):
                chain.step(STT(hbuf[:, t, :], hbuf[:, t, :], mv[:, t, 0:1], lnrow[:, 0, :], ALU.subtract, ALU.mult))
                return STT(x[:, t, :], hbuf[:, t, :], rstd[:, t:t + 1], lnrow[:, 1, :], ALU.mult, ALU.add)

            def modulate(chain, t, free):
                for c, part in enumerate(halves(t)):
                    ins = STT(part, x[:, t, c * BANK:(c + 1) * BANK], mv[:, t, 0:1], bank(free + 2 + c), ALU.subtract, ALU.mult)
                chain.step(ins)
                for c, part in enumerate(halves(t)):
                    STT(part, part, rstd[:, t:t + 1], bank(free + c), ALU.mult, ALU.add).then_inc(h_ready, 1)

            def rest_of_h(sub, t, held):
                for c in range(2):
                    dve.wait_ge(hT_hi_ready, sub * 4 + 2 * t + c + 1)
                    at = (slice(None), slice(4 * c, 4 * c + 4), slice(t * P, (t + 1) * P))
                    TTn(actT_lo[at], bank(held + 2 * t + c).rearrange("p (k q) -> p k q", k=4), actT_hi[at].bitcast(F32),
                        ALU.subtract).then_inc(hT_lo_ready, 1)

            def norms(chain, sub, n, free, held, f, f_done, n_ln, ahead):
                ahead(0)
                dve.wait_ge(gate1_ready, sub)
                f_done(0)
                residual(chain, f, 0)
                statistics(chain, hbuf, 0)
                dve.wait_ge(ln_loaded, n_ln)
                inverse_std(chain, n + 1, 0)
                chain.step(layer_norm(chain, 0))
                statistics(chain, x, 0)
                ahead(1)
                f_done(1)
                residual(chain, f, 1)
                statistics(chain, hbuf, 1)
                inverse_std(chain, n + 2, 0)
                dve.wait_ge(scale_ready, sub + 1)
                modulate(chain, 0, free)
                inverse_std(chain, n + 3, 1)
                chain.step(layer_norm(chain, 1))
                rest_of_h(sub, 0, held)
                statistics(chain, x, 1)
                inverse_std(chain, n + 4, 1)
                modulate(chain, 1, free)
                ahead(2)
                rest_of_h(sub, 1, held)
                dve.sem_inc(x_ready, 1)

            dve.wait_ge(x_loaded, 16)
            dve.sem_inc(x_ready, 1)
            chain = Chain(dve, dve_start)
            for t in range(TT):
                statistics(chain, x, t)
            dve.sem_inc(added, 4)
            for t in range(TT):
                inverse_std(chain, t + 1, t)
            for i in range(MOD0.n):
                mod_piece(MOD0, i, [0] * RING, 0, 0, 0)
                if i == MOD_SHIFT_SCALE + 1:
                    dve.wait_ge(scale_ready, 1)
                    for t in range(TT):
                        modulate(chain, t, 4)
                if i == MOD_SHIFT_SCALE + 2:
                    rest_of_h(0, 0, 0)
            for i in range(SPLIT):
                rest_of_piece(MIX, i, 0)
            rest_of_h(0, 1, 0)

            with dve.Fori(0, DEPTH) as layer:
                sbase = layer * LAYER_SPLITS
                chain = Chain(dve, dve_mix, layer * DVE_MIX_STEPS)
                step = chain.step
                z0 = z[:, 0:1024].rearrange("p (h q) -> p h q", h=4)
                z1 = z[:, 1024:1536].rearrange("p (h q) -> p h q", h=4)
                s0 = soft[:, 0:1024].rearrange("p (h q) -> p h q", h=4)
                s1 = soft[:, 1024:1536].rearrange("p (h q) -> p h q", h=4)
                past4 = past.unsqueeze(1).broadcast_to([P, 4, P])
                sink_v = sinks[:, :].rearrange("p (i r) -> p r i", r=2)
                mx = small[:, 0:8]
                mx_v = mx.rearrange("p (r i) -> p r i", r=2)
                es = small[:, 16:24]
                den, rden = small[:, 24:32], small[:, 32:40]

                def rotate(t):
                    v = proj[:, t, QC:VC].rearrange("p (h d) -> p h d", d=HD)
                    n = v.shape[1]
                    ta = gates[:, 0, 3 * D - n * HD:3 * D].rearrange("p (h d) -> p h d", d=HD)
                    tb = gates[:, 1, 3 * D - n * HD:3 * D].rearrange("p (h d) -> p h d", d=HD)
                    cos = cst[:, C_COS + t * HD:C_COS + (t + 1) * HD].unsqueeze(1).broadcast_to([P, n, HD])
                    sin = cst[:, C_SIN + t * HD:C_SIN + (t + 1) * HD].unsqueeze(1)
                    TTn(ta, v, cos, ALU.mult)
                    TTn(tb[:, :, 0:HALF], v[:, :, HALF:HD], sin[:, :, 0:HALF].broadcast_to([P, n, HALF]), ALU.mult)
                    step(TTn(tb[:, :, HALF:HD], v[:, :, 0:HALF], sin[:, :, HALF:HD].broadcast_to([P, n, HALF]), ALU.mult))
                    TTn(v, ta, tb, ALU.add).then_inc(rope_ready, 1)
                    dve.wait_ge(rope_ready, layer * 2 + t + 1)

                def shift_scores(t):
                    dve.wait_ge(sc_sent, layer * 2 + t + 1)
                    raw = ps[:, 4:6, :].rearrange("p b (i q) -> p (b i) q", q=P)
                    if t == 0:
                        step(TTn(scores[:, :, :], raw, sw_mask.unsqueeze(1).broadcast_to([P, 8, P]), ALU.add))
                        dve.wait_ge(small_loaded, layer * 64 + 64)
                        raw = scores[:, :, :]
                    step(RED(mx, raw, AX_X, ALU.max))
                    step(TTn(mx_v, mx_v, sink_v, ALU.max))
                    TTn(es.rearrange("p (r i) -> p r i", r=2), sink_v, mx_v, ALU.subtract)
                    TTn(scores[:, :, :], raw, mx.unsqueeze(2).broadcast_to([P, 8, P]), ALU.subtract).then_inc(sc_ready, 1)

                def divide_scores(t):
                    dve.wait_ge(exp_ready, layer * 2 + t + 1)
                    step(RED(den, scores[:, :, :], AX_X, ALU.add))
                    step(TTn(den, den, es, ALU.add))
                    step(nc.vector.reciprocal(rden, den))
                    TTn(scores[:, :, :], scores[:, :, :], rden.unsqueeze(2).broadcast_to([P, 8, P]), ALU.mult).then_inc(prob_ready, 1)

                def gated_branch(n, br, first_bank):
                    for t in range(TT):
                        gate = gates[:, t, br * D + n * BANK:br * D + (n + 1) * BANK]
                        ins = TTn(gate, gate, bank(first_bank + t), ALU.mult)
                    ins.then_inc(branch_read, 1)
                    dve.wait_ge(branch_read, layer * 6 + BRANCH_ORDER.index((br, n)) + 1)

                def gate_columns(n, br, t):
                    return gates[:, t, br * D + n * BANK:br * D + (n + 1) * BANK]

                def after(j):
                    if j == 8:
                        dve.wait_ge(softplus_ready, layer + 1)
                        step(STT(soft, z[:, :], 0.0, soft, ALU.max, ALU.add))
                        TTn(s0[:, :, 0:P], s0[:, :, 0:P], past4, ALU.mult)
                        TTn(s1, s1, past4, ALU.mult).then_inc(soft_ready, 1)
                    if j == 6:
                        dve.wait_ge(proj_ready, layer * 8 + 8)
                        dve.wait_ge(tables_loaded, 16)
                        for t in range(TT):
                            rotate(t)
                    if j == 9:
                        dve.wait_ge(suffix_sent, layer + 1)
                        TTn(z[:, 0:1024], z[:, 0:1024], ps[:, 4:6, :].rearrange("p b q -> p (b q)"), ALU.subtract)
                        step(TTn(z[:, 1024:1536], z[:, 1024:1536], bank(6), ALU.subtract))
                        TS(z[:, :], z[:, :], 0.0, None, ALU.min).then_inc(logw_ready, 1)
                    if j == 10:
                        dve.wait_ge(expw_ready, layer + 1)
                        TTn(z0[:, :, 0:P], z0[:, :, 0:P], past4, ALU.mult)
                        TTn(z1, z1, past4, ALU.mult).then_inc(w_ready, 1)
                    if j == 12:
                        shift_scores(0)
                    if j == 13:
                        divide_scores(0)
                    if j == 15:
                        shift_scores(1)
                    if j == 16:
                        divide_scores(1)
                    if j == 17:
                        yT_rest(0)
                    if j == 19:
                        dve.wait_ge(gate_ready, layer * 12 + 12)
                        yT_rest(1)
                        dve.wait_ge(split_used, sbase + 20 + SPLIT)
                        gated_branch(0, 0, 0)
                        gated_branch(0, 1, 2)
                        for t in range(TT):
                            ins = TTn(gate_columns(0, 0, t), gate_columns(0, 0, t), gate_columns(0, 1, t), ALU.add)
                        step(ins)
                    if j == 20:
                        dve.wait_ge(split_used, sbase + 21 + SPLIT)
                        gated_branch(1, 1, 0)
                        gated_branch(1, 0, 4)
                        for t in range(TT):
                            ins = TTn(gate_columns(1, 0, t), gate_columns(1, 0, t), gate_columns(1, 1, t), ALU.add)
                        step(ins)
                    if j in (22, 23):
                        n = j - 22
                        dve.wait_ge(mT_hi_ready, layer * 2 + n + 1)
                        part = (slice(None), slice(4 * n, 4 * n + 4), slice(None))
                        TTn(actT_lo[part].rearrange("p k (t q) -> p t k q", t=TT),
                            ps[:, 2 - 2 * n:4 - 2 * n, :].rearrange("p t (k q) -> p t k q", k=4),
                            actT_hi[part].bitcast(F32).rearrange("p k (t q) -> p t k q", t=TT), ALU.subtract).then_inc(mT_lo_ready, 1)
                    if j in (21, 22):
                        n = j - 21
                        dve.wait_ge(split_used, sbase + j + 1 + SPLIT)
                        gated_branch(n, 2, 2 - 2 * n)
                        for t in range(TT):
                            TTn(hbuf[:, t, n * BANK:(n + 1) * BANK], gate_columns(n, 0, t), gate_columns(n, 2, t), ALU.add).then_inc(merged_ready, 1)

                def yT_rest(c):
                    dve.wait_ge(yT_hi_ready, layer * 2 + c + 1)
                    part = (slice(None), slice(4 * c, 4 * c + 4), slice(None))
                    TTn(actT_lo[part], yT[part], actT_hi[part].bitcast(F32), ALU.subtract).then_inc(yT_lo_ready, 1)

                layer_loads = [MIX.landed[s] + DENSE.landed[s] for s in range(RING)]
                stream(MIX, [layer * layer_loads[s] + MOD0.landed[s] for s in range(RING)], sbase,
                       layer * LAYER_PIECES + MOD0.n, layer * (6 * MODS) + 3 * MODS, layer * 2 + 1, after)
                norms(chain, layer * 2 + 1, layer * 8 + 2, 0, 4, lambda t, c: bank(4 + 2 * t + c),
                      lambda t: dve.wait_ge(split_used, sbase + (MIX.n_split + SPLIT)) if t else dve.wait_ge(out_sent, layer + 1),
                      layer * 64 + 32,
                      lambda i: rest_of_piece(DENSE, i, sbase + MIX.n_split))
                assert chain.n == DVE_MIX_STEPS, chain.n

                def panel_events(stretch, panels, split_base, panel0, blocks, folds=None):
                    first_b = {stretch.split_no[i]: p[1] for i, p in enumerate(stretch.pieces) if p[0] == "B" and p[2] == 0}
                    last = {(p[0], p[1]): stretch.split_no[i] for i, p in enumerate(stretch.pieces) if p[0] != "mod"}
                    last = {v: k for k, v in last.items()}
                    last_turn = stretch.split_no[stretch.pieces.index(("C", len(panels) - 2, last_turn_after(panels)))]

                    def gT_part(p):
                        dve.wait_ge(gT_hi_ready, panel0 + p + 1)
                        w = panels[p]
                        for b in range(1 if folds is not None else blocks):
                            ins = TTn(gT_lo[:, b, 0:w // P, :], ps[:, HW1 + 2 * b, 0:w].rearrange("p (c q) -> p c q", q=P),
                                      gT_hi[:, b, 0:w // P, :].bitcast(F32), ALU.subtract)
                        if folds is not None:
                            ins = TTn(gT_hi[:, 1, 0:w // P, HALF_P:P], ps[:, HW1 + 2, 0:w].rearrange("p (c q) -> p c q", q=P)[:, :, 0:HALF_P],
                                      gT_hi[:, 1, 0:w // P, 0:HALF_P].bitcast(F32), ALU.subtract)
                        ins.then_inc(gT_lo_ready, 1)

                    def after(j):
                        kind, p = last.get(j, ("", 0))
                        if j in first_b and first_b[j]:
                            gT_part(first_b[j] - 1)
                        w = panels[p]
                        if kind in ("A", "B") and folds is not None:
                            m = "AB".index(kind)
                            dve.wait_ge(fold_copied, folds + 2 * p + m + 1)
                            TTn(fold[:, m, 0:w], fold[:, m, 0:w], ps[0:HALF_P, (HW1, HW3)[m] + 2, 0:w], ALU.add).then_inc(fold_added, 1)
                        if kind == "B":
                            dve.wait_ge(split_used, split_base + j + 1 + SPLIT)
                            dve.wait_ge(silu_ready, panel0 + p + 1)
                            for b in range(1 if folds is not None else blocks):
                                ins = TTn(gated[:, b, 0:w], silu[:, b, 0:w], ps[:, HW3 + 2 * b, 0:w], ALU.mult)
                            if folds is not None:
                                dve.wait_ge(fold_added, folds + 2 * p + 2)
                                ins = TTn(gated[0:HALF_P, 1, 0:w], silu[0:HALF_P, 1, 0:w], fold[:, 1, 0:w], ALU.mult)
                            ins.then_inc(gated_ready, 1)
                        if j == last_turn:
                            gT_part(len(panels) - 1)

                    return after

                with dve.If(layer < 1):
                    chain = Chain(dve, dve_ffn, 0)
                    stream(DENSE, [MOD0.landed[s] + MIX.landed[s] for s in range(RING)], MIX.n_split,
                           MOD0.n + MIX.n, 6 * MODS, 2, panel_events(DENSE, DENSE_PANELS, MIX.n_split, 0, 2))
                    norms(chain, 2, 6, 4, 0, lambda t, c: bank(2 * t + c),
                          lambda t: dve.wait_ge(split_used, LAYER_SPLITS + SPLIT) if t else dve.wait_ge(y_sent, 1), 64,
                          lambda i: rest_of_piece(MIX, i, LAYER_SPLITS))
                    assert chain.n == DVE_DENSE_STEPS, chain.n
                with dve.Else():
                    chain = Chain(dve, dve_ffn, DVE_DENSE_STEPS)
                    step = chain.step
                    dve.wait_ge(rt_hi, 1)
                    TTn(w_rt_lo[:, :, :], w_rt[:, :, :], w_rt_hi[:, :, :].bitcast(F32), ALU.subtract).then_inc(rt_lo, 1)
                    dve.wait_ge(hh_ready, 1)
                    for t in range(TT):
                        ins = TTn(h_lo[:, t, :], hbuf[:, t, :], h_hi[:, t, :].bitcast(F32), ALU.subtract)
                    ins.then_inc(hl_ready, 1)
                    wide = [P, TT, EXPERTS]
                    number = iota[:, 0:EXPERTS].unsqueeze(1).broadcast_to(wide)
                    logit, tmp, is1, rest, is2, sel, pos = (rt[:, n] for n in range(7))
                    m1, i1, m2, gap, e2, w1, w2 = (rs[:, n] for n in range(7))
                    dve.wait_ge(logits_sent, 1)
                    step(TTn(logit, ps[:, ROUTE + 1, LOGITS:LOGITS + 16].rearrange("p (t e) -> p t e", t=TT), b_rt[:, :].unsqueeze(1).broadcast_to(wide), ALU.add))

                    def largest(values, m, is_it):
                        step(RED(m, values, AX_X, ALU.max))
                        step(TTn(tmp, values, m.broadcast_to(wide), ALU.not_equal))
                        step(STT(tmp, tmp, 64.0, number, ALU.mult, ALU.add))
                        step(RED(i1, tmp, AX_X, ALU.min))
                        step(TTn(is_it, number, i1.broadcast_to(wide), ALU.is_equal))

                    largest(logit, m1, is1)
                    step(STT(rest, is1, -1e38, logit, ALU.mult, ALU.add))
                    largest(rest, m2, is2)
                    TTn(sel, is1, is2, ALU.add).then_inc(sel_ready, 1)
                    TTn(gap, m2, m1, ALU.subtract).then_inc(gap_ready, 1)
                    dve.wait_ge(e2_ready, 1)
                    step(TS(w2, e2, 1.0, None, ALU.add))
                    step(nc.vector.reciprocal(w1, w2))
                    step(TTn(w2, e2, w1, ALU.mult))
                    step(TTn(tmp, is1, w1.broadcast_to(wide), ALU.mult))
                    step(TTn(is2, is2, w2.broadcast_to(wide), ALU.mult))
                    nc.vector.memset(wsel[:, :, EXPERTS:], 0.0)
                    nc.vector.memset(posm[:, :, EXPERTS:], -1.0)
                    step(TTn(wsel[:, :, 0:EXPERTS], tmp, is2, ALU.add))
                    dve.wait_ge(pos_sent, 1)
                    step(STT(pos, ps[:, ROUTE + 1, 0:16].rearrange("p (t e) -> p t e", t=TT), 1.0, sel, ALU.add, ALU.mult))
                    step(TS(posm[:, :, 0:EXPERTS], pos, -1.0, None, ALU.add))
                    nc.vector.tensor_copy(counts_i[:, 0:EXPERTS], ps[:, ROUTE + 1, 16:24]).then_inc(counts_ready, 1)
                    dve.wait_ge(counts_ready, 1)
                    moe_splits = LAYER_SPLITS + MIX.n_split

                    def pick_tokens(e):
                        for t in range(TT):
                            at = posm[:, t, bass.ds(e, 1)]
                            TS(pick[:, t, :], iota, at, None, ALU.is_equal)
                            ins = TS(pick_w[:, t, :], iota, at, wsel[:, t, bass.ds(e, 1)], ALU.is_equal, ALU.mult)
                        ins.then_inc(pick_ready, 1)

                    def rest_of_expert_piece(i, e):
                        ahead, i = divmod(i, EXPERT.n)
                        rest_of_piece(EXPERT, i, e * EXPERT.n_split + (moe_splits + ahead * EXPERT.n_split))

                    def gathered_rows(b, n):
                        dve.wait_ge(gathered_lo[b], n)
                        nc.vector.tensor_copy(actT_lo[:, :, b * P:(b + 1) * P],
                                              ps[:, 6:8, :].rearrange("p c (k q) -> p (c k) q", q=P)).then_inc(xg_lo_ready[b], 1)

                    def second_block(e, n):
                        with dve.If(dve.value_load(counts_i[0:1, bass.ds(e, 1)], min_val=0, max_val=SEQ) > P):
                            gathered_rows(1, n)
                        with dve.Else():
                            dve.sem_inc(xg_lo_ready[1], 1)

                    pick_tokens(0)
                    gathered_rows(0, 1)
                    second_block(0, 1)
                    dve.wait_ge(yacc_zero, 1)
                    with dve.Fori(0, EXPERTS) as e:
                        count = dve.value_load(counts_i[0:1, bass.ds(e, 1)], min_val=0, max_val=SEQ)

                        def expert(blocks, packed=False):
                            after = panel_events(EXPERT, EXPERT_PANELS, e * EXPERT.n_split + moe_splits,
                                                 e * len(EXPERT_PANELS) + len(DENSE_PANELS), blocks, e * FOLDS if packed else None)
                            if not packed:
                                dve.sem_inc(fold_added, FOLDS)
                                dve.sem_inc(packed_ready, 1)
                            else:
                                dve.wait_ge(xg_hi_ready[1], e + 1)
                                dve.wait_ge(xg_lo_ready[1], e + 1)
                                nc.vector.tensor_copy(actT_hi[:, :, P + HALF_P:2 * P], actT_lo[:, :, P:P + HALF_P].bitcast(F32)).then_inc(packed_ready, 1)
                            for i in range(SPLIT, EXPERT.n):
                                after(i - SPLIT)
                                rest_of_expert_piece(i, e)
                                if i == EXPERT.n // 2:
                                    pick_tokens(e + 1)

                            def tail(last):
                                for n in range(SPLIT):
                                    after(EXPERT.n - SPLIT + n)
                                    if n == SPLIT - 1:
                                        dve.wait_ge(split_used, e * EXPERT.n_split + (moe_splits + EXPERT.n_split + SPLIT))
                                        for b in range(blocks):
                                            ins = nc.vector.tensor_copy(hbuf[:, b, BANK:D], bank(2 * b + 1))
                                        ins.then_inc(y_dve, 1)
                                    if not last:
                                        rest_of_expert_piece(EXPERT.n + n, e)
                                if not last:
                                    gathered_rows(0, e + 2)
                                for t in range(TT):
                                    for c in range(2):
                                        dve.wait_ge(scattered, e * 4 + 2 * t + c + 1)
                                        part = yacc[:, t, c * BANK:(c + 1) * BANK]
                                        TTn(part, part, bank(2 * t + c), ALU.add).then_inc(added, 1)
                                if not last:
                                    second_block(e + 1, e + 2)

                            with dve.If(e < EXPERTS - 1):
                                tail(False)
                            with dve.Else():
                                tail(True)

                        with dve.If(count > P):
                            with dve.If(count > P + HALF_P):
                                expert(2)
                            with dve.Else():
                                expert(2, packed=True)
                        with dve.Else():
                            expert(1)
                    dve.wait_ge(added, 4 * EXPERTS + 4)
                    dve.wait_ge(ln_loaded, 128)
                    dve.wait_ge(gate1_ready, 4)
                    for t in range(TT):
                        residual(chain, lambda t, c: yacc[:, t, c * BANK:(c + 1) * BANK], t)
                        statistics(chain, hbuf, t)
                    for t in range(TT):
                        inverse_std(chain, 15 + t, t)
                        layer_norm(chain, t).then_inc(x_ready, 1)
                    assert chain.n == DVE_ROUTE_STEPS, chain.n

        @block.tensor
        def _(pe):
            MM, TR = nc.tensor.matmul, nc.tensor.transpose

            def product(to, hi, lo, w_h, w_l, first, last):
                MM(to, hi, w_h, start=first, stop=False)
                MM(to, hi, w_l, start=False, stop=False)
                return MM(to, lo, w_h, start=False, stop=last)

            def packed_product(to, packed, _, w_h, w_l, first, last):
                MM(to, packed, w_h, start=first, stop=False)
                return MM(to, packed, w_l, start=False, stop=last)

            def split_piece(j, k, n, width):
                at = slice(k * width + n, k * width + n + min(width, BANK))
                return w_hi[:, j % SPLIT, at], w_lo[:, j % SPLIT, at]

            def h_transposed(sub, t, first_bank):
                for c in range(2):
                    pe.wait_ge(h_ready, sub * 4 + 2 * t + c + 1)
                    for k in range(4):
                        ins = TR(ps[:, first_bank + c, k * P:(k + 1) * P], hbuf[:, t, (4 * c + k) * P:(4 * c + k + 1) * P], ident)
                    ins.then_inc(hT_sent, 1)

            def send_modulation(free):
                for q in range(4):
                    ins = MM(bank(free + q), ones, mod_acc[:, q * BANK:(q + 1) * BANK], start=True, stop=True)
                ins.then_inc(mod_sent, 1)

            def open_sublayer(sub, free, held, gate_pieces=None):
                send_modulation(free)
                h_transposed(sub, 0, held)
                if gate_pieces is not None:
                    pe.wait_ge(piece_used, gate_pieces + RING)
                for q in range(2):
                    ins = MM(bank(held + 2 + q), ones, mod_acc[:, (4 + q) * BANK:(5 + q) * BANK], start=True, stop=True)
                ins.then_inc(gate_sent, 1)

            def second_tile(sub, held):
                pe.wait_ge(gate1_ready, sub + 1)
                h_transposed(sub, 1, held + 2)

            def open_tile(sub, t, c):
                pe.wait_ge(hT_hi_ready, sub * 4 + 2 * t + c + 1)
                pe.wait_ge(hT_lo_ready, sub * 4 + 2 * t + c + 1)

            def chunk(k, t):
                return actT_hi[:, k, t * P:(t + 1) * P], actT_lo[:, k, t * P:(t + 1) * P]

            pe.wait_ge(cst_loaded, 16)
            pe.wait_ge(piece_used, MOD_SHIFT_SCALE + RING)
            open_sublayer(0, 4, 0, MOD0.n)
            with pe.Fori(0, DEPTH) as layer:
                pbase = layer * LAYER_PIECES + MOD0.n

                def project(j, n, h, width=BANK, tiles=range(TT)):
                    ks = range(4 * h, 4 * h + 4) if width == BANK else range(KD)
                    for t in tiles:
                        for k in ks:
                            w = split_piece(j, k - ks[0], 0, width)
                            ins = product(bank(2 * t + n % 2, width), *chunk(k, t), *w, k == 0, k == KD - 1)
                    if TT - 1 in tiles:
                        ins.then_inc(split_used, 1)

                def stick_scores():
                    pe.wait_ge(aT_ready, layer * 2 + 2)
                    for h in range(SB_HEADS):
                        par, pair = h % 2, h // 2
                        rows = slice(par * HD, (par + 1) * HD)
                        MM(ps[:, 4 + par, pair * SEQ:(pair + 1) * SEQ], aT[rows, 2 + pair, 0:P], aT[rows, pair, :], start=True, stop=True)
                        ins = MM(ps[:, 6 + par, pair * P:(pair + 1) * P], aT[rows, 2 + pair, P:SEQ], aT[rows, pair, P:SEQ], start=True, stop=True)
                    ins.then_inc(z_sent, 1)

                def suffix_sums():
                    pe.wait_ge(soft_ready, layer + 1)
                    for par in range(2):
                        MM(bank(4 + par), tri, soft[:, par * BANK:(par + 1) * BANK], start=True, stop=False)
                        MM(bank(4 + par).rearrange("p (a q) -> p a q", q=SEQ)[:, :, P:SEQ], ones,
                           soft[:, 1024 + par * SEQ:1024 + (par + 1) * SEQ].rearrange("p (a q) -> p a q", q=P), start=False, stop=True)
                    MM(bank(6), tri, soft[:, 1024:1536], start=True, stop=True).then_inc(suffix_sent, 1)

                def stick_values():
                    pe.wait_ge(w_ready, layer + 1)
                    for h in range(SB_HEADS):
                        par, pair = h % 2, h // 2
                        rows = slice(par * HD, (par + 1) * HD)
                        v = slice(VA + h * HD, VA + (h + 1) * HD)
                        w0 = z[:, (2 * par + pair) * SEQ:(2 * par + pair + 1) * SEQ]
                        w1 = z[:, 1024 + (2 * par + pair) * P:1024 + (2 * par + pair + 1) * P]
                        MM(ps[rows, 7, pair * SEQ:(pair + 1) * SEQ], proj[:, 0, v], w0, start=True, stop=False)
                        ins = MM(ps[rows, 7, pair * SEQ + P:(pair + 1) * SEQ], proj[:, 1, v], w1, start=False, stop=True)
                    ins.then_inc(ya_sent, 1)

                def pool_windows():
                    pe.wait_ge(ya_ready, layer + 1)
                    for g in range(len(WINDOWS)):
                        rows = slice((g % 2) * HD, (g % 2 + 1) * HD)
                        u = slice(UB + g * HD, UB + (g + 1) * HD)
                        at, band = (g // 2) * SEQ, C_BAND + g * BAND_W
                        MM(ps[rows, 7, at:at + P], proj[:, 0, u], cst[:, band:band + P], start=True, stop=True)
                        MM(ps[rows, 7, at + P:at + 2 * P], proj[:, 1, u], cst[:, band + P:band + 2 * P], start=True, stop=False)
                        ins = MM(ps[rows, 7, at + P:at + P + SPILL], proj[:, 0, u], cst[:, band + 2 * P:band + BAND_W], start=False, stop=True)
                    ins.then_inc(pool_sent, 1)

                def pool_mix():
                    for g in range(len(WINDOWS)):
                        rows = slice((g % 2) * HD, (g % 2 + 1) * HD)
                        at = (g // 2) * SEQ
                        ins = MM(ps[rows, 7, at:at + SEQ], w_pool[rows, g // 2, :], proj[rows, g // 2, QA:KA], start=True, stop=True)
                    ins.then_inc(yb_sent, 1)

                def band_scores(t):
                    for h in range(Q_HEADS):
                        par, i, g = h % 2, h // 2, h // (Q_HEADS // KV_HEADS)
                        rows = slice(par * HD, (par + 1) * HD)
                        q0 = t * P
                        key = lambda c: cT[rows, 4 + g, c * CHUNK:(c + 1) * CHUNK]
                        before = 2 * t - 1 if t else 1
                        MM(ps[:, 4 + par, i * P:i * P + CHUNK], cT[rows, i, q0:q0 + P], key(2 * t), start=True, stop=True)
                        MM(ps[0:CHUNK, 4 + par, i * P + CHUNK:(i + 1) * P], cT[rows, i, q0:q0 + CHUNK], key(before), start=True, stop=True)
                        ins = MM(ps[CHUNK:P, 4 + par, i * P + CHUNK:(i + 1) * P], cT[rows, i, q0 + CHUNK:q0 + P], key(2 * t + 1), start=True, stop=True)
                    ins.then_inc(sc_sent, 1)

                def turn_probs(t):
                    pe.wait_ge(prob_ready, layer * 2 + t + 1)
                    for n in range(Q_HEADS):
                        ins = TR(ps[:, 4 + n // 4, (n % 4) * P:(n % 4 + 1) * P], scores[:, n, :], ident)
                    ins.then_inc(pT_sent, 1)

                def band_values(t):
                    pe.wait_ge(pT_ready, layer * 2 + t + 1)
                    pe.wait_ge(v_ready, layer + 1)
                    if t:
                        pe.wait_ge(yc_ready, layer * 2 + 1)
                    for par in range(2):
                        for g in range(KV_HEADS):
                            for odd in range(2):
                                v = v_even[:, :] if t and not odd else proj[:, t, VC:PROJ]
                                qs = slice(odd * CHUNK, (odd + 1) * CHUNK)
                                to = ps[par * HD:(par + 1) * HD, 6, 2 * g * P:(2 * g + 2) * P].rearrange("p (i q) -> p i q", q=P)
                                ins = MM(to[:, :, qs], v[:, g * HD:(g + 1) * HD], probT[:, 4 * par + 2 * g:4 * par + 2 * g + 2, qs],
                                         start=True, stop=True)
                    ins.then_inc(yc_sent, 1)

                def project_out(j, n, h, t):
                    for k in range(4 * h, 4 * h + 4):
                        ins = product(bank(4 + 2 * t + n), *chunk(k, t), *split_piece(j, k % 4, 0, BANK), k == 0, k == KD - 1)
                    return ins

                def merged_T(n):
                    pe.wait_ge(merged_ready, layer * 4 + 2 * n + 2)
                    for t in range(TT):
                        for k in range(4):
                            ins = TR(ps[:, 2 - 2 * n + t, k * P:(k + 1) * P], hbuf[:, t, (4 * n + k) * P:(4 * n + k + 1) * P], ident)
                    ins.then_inc(mT_sent, 1)

                def after(j):
                    if j == 3:
                        pe.wait_ge(proj_ready, layer * 8 + 2)
                        for c in range(4):
                            for t in range(TT):
                                ins = TR(ps[:, 4 + c // 2, (c % 2) * SEQ + t * P:(c % 2) * SEQ + (t + 1) * P], proj[:, t, c * P:(c + 1) * P], ident)
                        ins.then_inc(aT_sent, 1)
                    if j == 5:
                        stick_scores()
                    if j == 9:
                        suffix_sums()
                    if j == 10:
                        pe.wait_ge(rope_ready, layer * 2 + 2)
                        pe.wait_ge(logw_ready, layer + 1)
                        for c in range(6):
                            for t in range(TT):
                                ins = TR(ps[:, 4 + c // 2, (c % 2) * SEQ + t * P:(c % 2) * SEQ + (t + 1) * P], proj[:, t, QC + c * P:QC + (c + 1) * P], ident)
                        ins.then_inc(cT_sent, 1)
                    if j == 11:
                        stick_values()
                    if j == 12:
                        pe.wait_ge(cT_ready, layer * 3 + 3)
                        band_scores(0)
                        pool_windows()
                    if j == 13:
                        pool_mix()
                    if j == 14:
                        turn_probs(0)
                    if j == 15:
                        band_values(0)
                        band_scores(1)
                    if j == 17:
                        turn_probs(1)
                    if j == 18:
                        band_values(1)

                for i in range(SPLIT):
                    if i < 2:
                        open_tile(layer * 2, 0, i)
                    pe.wait_ge(piece_used, pbase + i + 1 + RING)
                    project(i, *MIX.pieces[i][1:], tiles=[0])
                    if i == 1:
                        second_tile(layer * 2, 0)
                for i in range(SPLIT):
                    if i < 2:
                        open_tile(layer * 2, 1, i)
                    project(i, *MIX.pieces[i][1:], tiles=[1])

                for i, piece in enumerate(MIX.pieces):
                    if piece[0] == "mod" or i < SPLIT:
                        continue
                    j = MIX.split_no[i]
                    kind, n, h = piece
                    pe.wait_ge(piece_used, pbase + i + 1 + RING)
                    if kind == "in":
                        if n >= 2 and h == 0:
                            pe.wait_ge(proj_ready, layer * 8 + 2 * (n - 1))
                        project(j, n, h, BANK if n < 3 else BANK // 2)
                    elif kind == "gate":
                        if j == 13:
                            pe.wait_ge(small_loaded, layer * 64 + 64)
                            pe.wait_ge(pooled_ready, layer + 1)
                        if h == 0:
                            if n < 2:
                                pe.wait_ge(proj_ready, layer * 8 + 6 + 2 * n)
                            else:
                                pe.wait_ge(gate_ready, layer * 12 + 2 * (n - 1))
                        project(j, n, h)
                    elif kind == "branch":
                        if j == 19:
                            pe.wait_ge(yT_hi_ready, layer * 2 + 1)
                            pe.wait_ge(yT_lo_ready, layer * 2 + 1)
                            pe.wait_ge(gate_ready, layer * 12 + 12)
                        if j == 20:
                            pe.wait_ge(pT_ready, layer * 2 + 2)
                        if j == 21:
                            pe.wait_ge(yT_hi_ready, layer * 2 + 2)
                            pe.wait_ge(yT_lo_ready, layer * 2 + 2)
                        groups = {19: [(0, (0, 1), 0, 0), (1, (2, 3), 2, 0)], 20: [(0, (0, 1), 4, 0), (1, (2, 3), 0, 1)],
                                  21: [(2, (4, 5, 6, 7), 2, 2)], 22: [(2, (4, 5, 6, 7), 0, 3)]}[j]
                        for br, ks, first_bank, read in groups:
                            if read:
                                pe.wait_ge(branch_read, layer * 6 + read)
                            for t in range(TT):
                                for k in ks:
                                    ins = product(bank(first_bank + t), *chunk(k, t), *split_piece(j, k % 4, 0, BANK), k == ks[0], k == ks[-1])
                                    if j == 22 and t == 1 and k == 5:
                                        merged_T(0)
                        ins.then_inc(split_used, 1)
                    elif h == 0:
                        if n == 0:
                            pe.wait_ge(mT_hi_ready, layer * 2 + 1)
                            pe.wait_ge(mT_lo_ready, layer * 2 + 1)
                            pe.wait_ge(branch_read, layer * 6 + 4)
                        for t in range(TT):
                            ins = project_out(j, n, h, t)
                        ins.then_inc(split_used, 1)
                        if n == 0:
                            merged_T(1)
                    elif n == 0:
                        continue
                    else:
                        pe.wait_ge(mT_hi_ready, layer * 2 + 2)
                        pe.wait_ge(mT_lo_ready, layer * 2 + 2)
                        for t in range(TT):
                            for m in range(2):
                                ins = project_out(j - 1 + m, m, h, t)
                                if t == TT - 1:
                                    ins.then_inc(split_used, 1)
                            if t == 0:
                                ins.then_inc(out_sent, 1)
                    after(j)
                open_sublayer(layer * 2 + 1, 0, 4)

                def swiglu(stretch, panels, piece_base, panel0, blocks, e=None, turn_places=None, packed=False):
                    def turn(p):
                        pe.wait_ge(gated_ready, panel0 + p + 1)
                        for b in range(blocks):
                            n = HALF_P if b and packed else P
                            for c in range(panels[p] // P):
                                ins = TR(ps[:, HW1 + 2 * b, c * P:c * P + n], gated[0:n, b, c * P:(c + 1) * P], ident[0:n, 0:n])
                        ins.then_inc(gT_sent, 1)

                    def up(j, kind, h, width, b):
                        ks = range(4 * h, 4 * h + 4) if width == BANK else range(KD)
                        for k in ks:
                            ins = (packed_product if b and packed else product)(
                                bank({"A": HW1, "B": HW3}[kind] + 2 * b, width), *chunk(k, b), *split_piece(j, k - ks[0], 0, width),
                                k == 0, k == KD - 1)
                        return ins

                    def down(j, p, h, b):
                        for c in range(2):
                            k = 2 * h + c
                            for n in range(2):
                                ins = (packed_product if b and packed else product)(
                                    bank(2 * b + n), gT_hi[:, b, k, :], gT_lo[:, b, k, :], *split_piece(j, c, n * BANK, D),
                                    p == 0 and k == 0, p == len(panels) - 1 and k == panels[p] // P - 1)
                        return ins

                    if e is None:
                        for b in range(blocks):
                            for i in range(SPLIT):
                                if i < 2:
                                    open_tile(1, b, i)
                                kind, p, h = stretch.pieces[i]
                                pe.wait_ge(piece_used, piece_base + i + 1 + RING)
                                ins = up(i, kind, h, panels[p], b)
                                if b == blocks - 1:
                                    ins.then_inc(split_used, 1)
                                if b == 0 and i == 1:
                                    second_tile(1, 4)

                    for i, (kind, p, *rest) in enumerate(stretch.pieces):
                        if kind == "mod" or (e is None and i < SPLIT):
                            continue
                        j, h = stretch.split_no[i], rest[0]
                        width = panels[p]
                        pe.wait_ge(piece_used, piece_base + i + 1 + RING)
                        if kind in "AB":
                            if kind == "A" and p == 1 and h == 0:
                                pe.wait_ge(silu_ready, panel0 + 1)
                            if kind == "B" and p and h == 0:
                                pe.wait_ge(gated_ready, panel0 + p)
                            for b in range(blocks):
                                ins = up(j, kind, h, width, b)
                                if b == blocks - 1:
                                    ins.then_inc(split_used, 1)
                                if kind == "B" and h == 0 and p and b == 0:
                                    pe.wait_ge(silu_ready, panel0 + p + 1)
                                    turn(p - 1)
                            if turn_places and kind == "B" and h == 1 and p == 0:
                                turn_places()
                        else:
                            if turn_places and p == 0 and h == 0:
                                pe.wait_ge(place_ready, e + 1)
                            if h == 0:
                                pe.wait_ge(gT_hi_ready, panel0 + p + 1)
                                pe.wait_ge(gT_lo_ready, panel0 + p + 1)
                            if e is None and j == stretch.n_split - 2:
                                continue
                            if e is None and j == stretch.n_split - 1:
                                for b in range(blocks):
                                    ins = down(j - 1, p - 1, 1, b)
                                    if b == blocks - 1:
                                        ins.then_inc(split_used, 1)
                                    ins = down(j, p, h, b)
                                    ins.then_inc(split_used if b == blocks - 1 else y_sent, 1)
                                continue
                            for b in range(blocks):
                                ins = down(j, p, h, b)
                            ins.then_inc(split_used, 1)
                            if p == len(panels) - 2 and h == last_turn_after(panels):
                                turn(p + 1)

                with pe.If(layer < 1):
                    swiglu(DENSE, DENSE_PANELS, MOD0.n + MIX.n, 0, 2)
                    pe.wait_ge(piece_used, LAYER_PIECES + MOD0.n + RING)
                    open_sublayer(2, 4, 0)
                with pe.Else():
                    second_tile(3, 4)
                    open_tile(3, 0, 1)
                    open_tile(3, 1, 1)
                    pe.wait_ge(rt_lo, 1)
                    for k in range(KD):
                        ins = product(ps[0:EXPERTS, ROUTE, 0:SEQ], w_rt_hi[:, k, :], w_rt_lo[:, k, :], actT_hi[:, k, :], actT_lo[:, k, :],
                                      k == 0, k == KD - 1)
                    ins.then_inc(logitsT_sent, 1)
                    pe.wait_ge(logitsT_ready, 1)
                    for t in range(TT):
                        ins = TR(ps[:, ROUTE + 1, LOGITS + t * EXPERTS:LOGITS + (t + 1) * EXPERTS], place[0:EXPERTS, 0, t * P:(t + 1) * P],
                                 ident[0:EXPERTS, 0:EXPERTS])
                    ins.then_inc(logits_sent, 1)
                    pe.wait_ge(sel_ready, 1)
                    sel = rt[:, 5]
                    to = ps[:, ROUTE + 1, :]
                    MM(to[:, 0:8], past, sel[:, 0, :], start=True, stop=True)
                    MM(to[:, 8:16], past, sel[:, 1, :], start=True, stop=False)
                    MM(to[:, 8:16], ones, sel[:, 0, :], start=False, stop=True)
                    MM(to[:, 16:24], ones, sel[:, 0, :], start=True, stop=False)
                    MM(to[:, 16:24], ones, sel[:, 1, :], start=False, stop=True).then_inc(pos_sent, 1)
                    pe.wait_ge(hh_ready, 1)
                    pe.wait_ge(hl_ready, 1)
                    pe.wait_ge(counts_ready, 1)
                    def gather(b, n):
                        for part, first_bank, signal in ((h_hi, 4, gathered_hi), (h_lo, 6, gathered_lo)):
                            for k in range(KD):
                                to = ps[:, first_bank + k // 4, (k % 4) * P:(k % 4 + 1) * P]
                                for t in range(TT):
                                    ins = MM(to, part[:, t, k * P:(k + 1) * P], pick[:, t, b * P:(b + 1) * P], start=t == 0, stop=t == 1)
                            ins.then_inc(signal[b], 1)

                    def second_block(e, n):
                        with pe.If(pe.value_load(counts_i[0:1, bass.ds(e, 1)], min_val=0, max_val=SEQ) > P):
                            pe.wait_ge(xg_hi_ready[0], n)
                            pe.wait_ge(xg_lo_ready[0], n)
                            gather(1, n)
                        with pe.Else():
                            pe.sem_inc(gathered_hi[1], 1)
                            pe.sem_inc(gathered_lo[1], 1)

                    pe.wait_ge(pick_ready, 1)
                    gather(0, 1)
                    second_block(0, 1)
                    with pe.Fori(0, EXPERTS) as e:
                        count = pe.value_load(counts_i[0:1, bass.ds(e, 1)], min_val=0, max_val=SEQ)

                        def expert(blocks, packed=False):
                            if packed:
                                pe.wait_ge(packed_ready, e + 1)
                            for b in range(blocks):
                                pe.wait_ge(xg_hi_ready[b], e + 1)
                                pe.wait_ge(xg_lo_ready[b], e + 1)

                            def turn_places():
                                pe.wait_ge(added, e * 4 + 4)
                                for b in range(blocks):
                                    for t in range(TT):
                                        ins = TR(ps[:, 0, b * SEQ + t * P:b * SEQ + (t + 1) * P], pick_w[:, t, b * P:(b + 1) * P], ident)
                                ins.then_inc(place_sent, 1)

                            swiglu(EXPERT, EXPERT_PANELS, e * EXPERT.n + (MOD0.n + LAYER_PIECES + MIX.n),
                                   e * len(EXPERT_PANELS) + len(DENSE_PANELS), blocks, e, turn_places, packed)

                            def scatter():
                                pe.wait_ge(y_act, e + 1)
                                pe.wait_ge(y_dve, e + 1)
                                for t in range(TT):
                                    for c in range(2):
                                        for b in range(blocks):
                                            ins = MM(bank(2 * t + c), place[:, b, t * P:(t + 1) * P], hbuf[:, b, c * BANK:(c + 1) * BANK],
                                                     start=b == 0, stop=b == blocks - 1)
                                        ins.then_inc(scattered, 1)

                            with pe.If(e < EXPERTS - 1):
                                pe.wait_ge(pick_ready, e + 2)
                                gather(0, e + 2)
                                scatter()
                                second_block(e + 1, e + 2)
                            with pe.Else():
                                scatter()

                        with pe.If(count > P):
                            with pe.If(count > P + HALF_P):
                                expert(2)
                            with pe.Else():
                                expert(2, packed=True)
                        with pe.Else():
                            expert(1)


_INS = ['x', 'c', 'w_mod_mix', 'b_mod_mix', 'w_in', 'w_pool', 'pool_scale', 'sinks', 'w_gate', 'w_branch_a',
        'w_branch_b', 'w_branch_c', 'w_out', 'ln_mix_g', 'ln_mix_b', 'w_mod_ffn', 'b_mod_ffn', 'ffn_w1', 'ffn_w3',
        'ffn_w2', 'w_router', 'b_router', 'exp_w1', 'exp_w3', 'exp_w2', 'ln_ffn_g', 'ln_ffn_b']


def kernel(**inputs):
    import numpy as _np
    import concourse.bacc as _bacc
    from concourse import mybir as _mybir
    from concourse.bass_utils import run_bass_kernel_spmd as _run

    nc = _bacc.Bacc("TRN2", target_bir_lowering=False, num_devices=1)
    arrays, args = {}, {}
    for name in _INS:
        a = _np.ascontiguousarray(inputs[name])
        arrays[f"in_{name}_dram"] = a
        args[name] = nc.dram_tensor(f"in_{name}_dram", a.shape, _mybir.dt.from_np(a.dtype), kind="ExternalInput").ap()
    table = constants()
    arrays["constants_dram"] = table
    consts = nc.dram_tensor("constants_dram", table.shape, _mybir.dt.float32, kind="ExternalInput").ap()
    out = nc.dram_tensor("out_dram", (1, SEQ, D), _mybir.dt.float32, kind="ExternalOutput").ap()
    trunk(nc, args, consts, out)
    r = _run(nc, [arrays], core_ids=[0])
    return r.results[0]["out_dram"]
```
